# Optimizing a Trainium2 kernel written in Bass

```python
import jax, jax.numpy as jnp
from jax import lax
import numpy as np

D_MODEL = 1024
BATCH = 1
SEQ = 256
DEPTH = 1

HEAD_DIM = 64
A_HEADS = 8
B_HEADS = 8
IDX_HEADS = 8
IDX_DIM = 64
DILATED_PATTERNS = ((128, 1), (512, 4), (2048, 16))
TOPK_MAX = 256
D_A = A_HEADS * HEAD_DIM
D_B = B_HEADS * HEAD_DIM
D_FF = ((8 * D_MODEL + 767) // 768) * 256
ROPE_THETA = 10000.0
RMS_EPS = 1e-6
BLOCK = 128
ATTN_SCALE = HEAD_DIM ** -0.5
IDX_SCALE = (IDX_DIM ** -0.5) * (IDX_HEADS ** -0.5)
IN_SPLITS = (D_A, D_A, D_A, D_B, HEAD_DIM, HEAD_DIM, IDX_HEADS * IDX_DIM, IDX_DIM, IDX_HEADS, D_MODEL, D_MODEL)
IN_OFFSETS = tuple(int(o) for o in np.cumsum(IN_SPLITS)[:-1])
D_IN = int(sum(IN_SPLITS))


def rmsnorm(x, g):
    x32 = x.astype(jnp.float32)
    y = x32 * lax.rsqrt(jnp.mean(x32 * x32, axis=-1, keepdims=True) + RMS_EPS)
    return (y * g.astype(jnp.float32)).astype(x.dtype)

def rope(z, pos):
    half = z.shape[-1] // 2
    inv_freq = ROPE_THETA ** (-jnp.arange(half, dtype=jnp.float32) / half)
    ang = pos.astype(jnp.float32)[:, None] * inv_freq[None, :]
    cos = jnp.cos(ang)[None, :, None, :]
    sin = jnp.sin(ang)[None, :, None, :]
    z32 = z.astype(jnp.float32)
    z1, z2 = z32[..., :half], z32[..., half:]
    return jnp.concatenate([z1 * cos - z2 * sin, z2 * cos + z1 * sin], axis=-1).astype(z.dtype)

def dilated_window_attention(q, k, v, window, dilation):
    B, T, H, hd = q.shape
    steps = window // dilation
    seg = dilation * BLOCK
    t_pad = -(-T // seg) * seg
    m_len = t_pad // dilation
    nb = m_len // BLOCK

    def to_blocks(z):
        z = jnp.pad(z, ((0, 0), (0, t_pad - T), (0, 0), (0, 0)))
        z = z.reshape(B, m_len, dilation, H, hd).transpose(0, 2, 3, 1, 4)
        return z.reshape(B, dilation, H, nb, BLOCK, hd)

    qb, kb, vb = to_blocks(q), to_blocks(k), to_blocks(v)

    def with_prev(z):
        prev = jnp.pad(z[:, :, :, :-1], ((0, 0), (0, 0), (0, 0), (1, 0), (0, 0), (0, 0)))
        return jnp.concatenate([prev, z], axis=4)

    k2, v2 = with_prev(kb), with_prev(vb)
    s = jnp.einsum('brhnqd,brhnkd->brhnqk', qb, k2).astype(jnp.float32) * ATTN_SCALE
    qi = jnp.arange(BLOCK)[:, None]
    kj = jnp.arange(2 * BLOCK)[None, :]
    dist = qi + BLOCK - kj
    band = (dist >= 0) & (dist <= steps)
    has_prev = (jnp.arange(nb)[:, None, None] > 0) | (kj >= BLOCK)[None]
    mask = band[None] & has_prev
    s = jnp.where(mask, s, -jnp.inf)
    m = jnp.max(s, axis=-1, keepdims=True)
    p = jnp.exp(s - m)
    den = jnp.sum(p, axis=-1, keepdims=True)
    o = jnp.einsum('brhnqk,brhnkd->brhnqd', p.astype(v.dtype), v2).astype(jnp.float32) / den
    lse = (m + jnp.log(den))[..., 0]
    o = o.reshape(B, dilation, H, m_len, hd).transpose(0, 3, 1, 2, 4).reshape(B, t_pad, H, hd)[:, :T]
    lse = lse.reshape(B, dilation, H, m_len).transpose(0, 3, 1, 2).reshape(B, t_pad, H)[:, :T]
    return o, lse

def dilated_mixture(q, k, v):
    outs, lses = [], []
    for window, dilation in DILATED_PATTERNS:
        o, l = dilated_window_attention(q, k, v, window, dilation)
        outs.append(o)
        lses.append(l)
    w = jax.nn.softmax(jnp.stack(lses, axis=0), axis=0)
    return jnp.sum(w[..., None] * jnp.stack(outs, axis=0), axis=0)

def indexed_sparse_attention(q, k, v, qi, ki, wi):
    B, T, H, hd = q.shape
    topk = min(TOPK_MAX, T // 4)
    nb = T // BLOCK
    key_pos = jnp.arange(T)

    def blocks(z):
        return jnp.moveaxis(z.reshape((B, nb, BLOCK) + z.shape[2:]), 1, 0)

    def one_block(args):
        q_blk, qi_blk, wi_blk, start = args
        q_pos = start + jnp.arange(BLOCK)
        causal = key_pos[None, :] <= q_pos[:, None]
        dots = jnp.einsum('bqhd,bsd->bqhs', qi_blk, ki).astype(jnp.float32)
        score = jnp.einsum('bqh,bqhs->bqs', wi_blk.astype(jnp.float32), jax.nn.relu(dots)) * IDX_SCALE
        score = jnp.where(causal[None], score, -jnp.inf)
        _, sel = lax.top_k(score, topk)
        valid = sel <= q_pos[None, :, None]
        k_sel = jax.vmap(lambda kk, ii: kk[ii])(k, sel)
        v_sel = jax.vmap(lambda vv, ii: vv[ii])(v, sel)
        s = jnp.einsum('bqhd,bqkd->bhqk', q_blk, k_sel).astype(jnp.float32) * ATTN_SCALE
        s = jnp.where(valid[:, None], s, -jnp.inf)
        p = jax.nn.softmax(s, axis=-1)
        return jnp.einsum('bhqk,bqkd->bqhd', p.astype(v.dtype), v_sel)

    starts = jnp.arange(nb, dtype=jnp.int32) * BLOCK
    out = lax.map(one_block, (blocks(q), blocks(qi), blocks(wi), starts))
    return jnp.moveaxis(out, 0, 1).reshape(B, T, H, hd)

def first_inputs(seed: int = 0) -> dict:
    key = jax.random.key(seed)
    ks = jax.random.split(key, 12)
    f32 = jnp.float32

    def dense(k, shape, fan_in):
        return jax.random.normal(k, shape, f32) * fan_in ** -0.5

    def gain(k, shape):
        return 1.0 + 0.02 * jax.random.normal(k, shape, f32)

    return {
        'x': jax.random.normal(ks[0], (BATCH, SEQ, D_MODEL), f32),
        'norm_mix': gain(ks[1], (DEPTH, D_MODEL)),
        'w_in': dense(ks[2], (DEPTH, D_MODEL, D_IN), D_MODEL),
        'w_up_a': dense(ks[3], (DEPTH, D_A, D_MODEL), D_A),
        'w_up_b': dense(ks[4], (DEPTH, D_B, D_MODEL), D_B),
        'w_out': dense(ks[5], (DEPTH, D_MODEL, D_MODEL), D_MODEL),
        'norm_ffn': gain(ks[6], (DEPTH, D_MODEL)),
        'w_gate': dense(ks[7], (DEPTH, D_MODEL, D_FF), D_MODEL),
        'w_up': dense(ks[8], (DEPTH, D_MODEL, D_FF), D_MODEL),
        'w_down': dense(ks[9], (DEPTH, D_FF, D_MODEL), D_FF),
        'norm_final': gain(ks[10], (D_MODEL,)),
    }

def first_block(x, norm_mix, w_in, w_up_a, w_up_b, w_out, norm_ffn, w_gate, w_up, w_down, norm_final):
    B, T, _ = x.shape
    pos = jnp.arange(T, dtype=jnp.int32)
    for layer in range(DEPTH):
        h = rmsnorm(x, norm_mix[layer])
        proj = h @ w_in[layer]
        qa, ka, va, qb, kb, vb, qi, ki, wi, ga, gb = jnp.split(proj, IN_OFFSETS, axis=-1)
        qa = rope(qa.reshape(B, T, A_HEADS, HEAD_DIM), pos)
        ka = rope(ka.reshape(B, T, A_HEADS, HEAD_DIM), pos)
        va = va.reshape(B, T, A_HEADS, HEAD_DIM)
        y_a = dilated_mixture(qa, ka, va).astype(x.dtype).reshape(B, T, D_A)
        qb = rope(qb.reshape(B, T, B_HEADS, HEAD_DIM), pos)
        kb = rope(kb[:, :, None], pos)[:, :, 0]
        qi = rope(qi.reshape(B, T, IDX_HEADS, IDX_DIM), pos)
        ki = rope(ki[:, :, None], pos)[:, :, 0]
        y_b = indexed_sparse_attention(qb, kb, vb, qi, ki, wi).reshape(B, T, D_B)
        merged = jax.nn.sigmoid(ga) * (y_a @ w_up_a[layer]) + jax.nn.sigmoid(gb) * (y_b @ w_up_b[layer])
        x = x + merged @ w_out[layer]
        h = rmsnorm(x, norm_ffn[layer])
        x = x + (jax.nn.silu(h @ w_gate[layer]) * (h @ w_up[layer])) @ w_down[layer]
    return rmsnorm(x, norm_final)


MIX_WIDTH = D_MODEL
N_HEADS = (MIX_WIDTH // 2) // HEAD_DIM
N_KV_HEADS = 2
ATTN_WIDTH = N_HEADS * HEAD_DIM
KV_WIDTH = N_KV_HEADS * HEAD_DIM
CONV_CH = MIX_WIDTH - ATTN_WIDTH
CONV_GROUPS = CONV_CH // HEAD_DIM
CONV_W = 31
IN_WIDTH = ATTN_WIDTH + 2 * KV_WIDTH + 2 * CONV_CH
Q_BLOCK = 128
GRID_W = 64
ROPE_AXIS_DIM = HEAD_DIM // 2
N_KEYS = 128
N_EXPERTS = N_KEYS * N_KEYS
PEER_HEADS = 8
PEER_DQ = 256
PEER_TOPK = 16
TOKEN_CHUNK = 128
EPS = 1e-6


def _rmsnorm(x, g):
    xf = x.astype(jnp.float32)
    y = xf * lax.rsqrt(jnp.mean(xf * xf, axis=-1, keepdims=True) + EPS)
    return (y * g.astype(jnp.float32)).astype(x.dtype)

def _layernorm(x, g, b):
    xf = x.astype(jnp.float32)
    mu = jnp.mean(xf, axis=-1, keepdims=True)
    var = jnp.mean(jnp.square(xf - mu), axis=-1, keepdims=True)
    y = (xf - mu) * lax.rsqrt(var + EPS)
    return (y * g.astype(jnp.float32) + b.astype(jnp.float32)).astype(x.dtype)

def _rope_rotate(x, ang):
    p = ang.shape[-1]
    cos = jnp.cos(ang)[:, None, :]
    sin = jnp.sin(ang)[:, None, :]
    xf = x.astype(jnp.float32)
    x1, x2 = xf[..., :p], xf[..., p:]
    return jnp.concatenate([x1 * cos - x2 * sin, x2 * cos + x1 * sin], axis=-1)

def _axial_rope(x, ang_row, ang_col):
    r = _rope_rotate(x[..., :ROPE_AXIS_DIM], ang_row)
    c = _rope_rotate(x[..., ROPE_AXIS_DIM:], ang_col)
    return jnp.concatenate([r, c], axis=-1).astype(x.dtype)

def _gqa_blocked(q, k, v):
    b, s, hkv, g, hd = q.shape
    nb = s // Q_BLOCK
    qb = q.reshape(b, nb, Q_BLOCK, hkv, g, hd).transpose(1, 0, 2, 3, 4, 5)

    def one_block(qblk):
        sc = jnp.einsum('bqkgd,bskd->bkgqs', qblk, k).astype(jnp.float32)
        p = jax.nn.softmax(sc, axis=-1).astype(v.dtype)
        return jnp.einsum('bkgqs,bskd->bqkgd', p, v)

    ob = lax.map(one_block, qb)
    return ob.transpose(1, 0, 2, 3, 4, 5).reshape(b, s, hkv * g * hd)

def _conformer_conv(a, gate, conv_dw, conv_b, conv_ln_g, conv_ln_b):
    h = a * jax.nn.sigmoid(gate)
    pad = (CONV_W - 1) // 2
    h = lax.conv_general_dilated(
        h, conv_dw.astype(h.dtype), window_strides=(1,), padding=((pad, pad),),
        dimension_numbers=('NWC', 'WIO', 'NWC'), feature_group_count=CONV_CH)
    h = h + conv_b.astype(h.dtype)
    h = _layernorm(h, conv_ln_g, conv_ln_b)
    return jax.nn.silu(h)

def _peer(xn, peer_wq, peer_keys, peer_u, peer_v):
    t, d = xn.shape
    xc_all = xn.reshape(t // TOKEN_CHUNK, TOKEN_CHUNK, d)
    half = PEER_DQ // 2

    def chunk(xc):
        q = (xc @ peer_wq).reshape(TOKEN_CHUNK, PEER_HEADS, PEER_DQ)
        s1 = jnp.einsum('chd,nd->chn', q[..., :half], peer_keys[0]).astype(jnp.float32)
        s2 = jnp.einsum('chd,nd->chn', q[..., half:], peer_keys[1]).astype(jnp.float32)
        v1, i1 = lax.top_k(s1, PEER_TOPK)
        v2, i2 = lax.top_k(s2, PEER_TOPK)
        cand_s = (v1[..., :, None] + v2[..., None, :]).reshape(TOKEN_CHUNK, PEER_HEADS, -1)
        cand_i = (i1[..., :, None] * N_KEYS + i2[..., None, :]).reshape(TOKEN_CHUNK, PEER_HEADS, -1)
        top_s, pos = lax.top_k(cand_s, PEER_TOPK)
        e = jnp.take_along_axis(cand_i, pos, axis=-1)
        g = jax.nn.softmax(top_s, axis=-1).astype(xc.dtype)
        u = peer_u[e]
        h = jax.nn.gelu(jnp.einsum('cd,chkd->chk', xc, u))
        return jnp.einsum('chk,chkd->cd', g * h, peer_v[e])

    return lax.map(chunk, xc_all).reshape(t, d)

def second_inputs(seed: int = 0) -> dict:
    key = jax.random.key(seed)
    ks = jax.random.split(key, 16)
    f32 = jnp.float32
    nrm = lambda k, shp, sc: jax.random.normal(k, shp, f32) * sc
    return {
        "x": nrm(ks[0], (BATCH, SEQ, D_MODEL), 1.0),
        "norm1_g": 1.0 + nrm(ks[1], (D_MODEL,), 0.02),
        "w_in": nrm(ks[2], (D_MODEL, IN_WIDTH), D_MODEL ** -0.5),
        "q_norm_g": 1.0 + nrm(ks[3], (HEAD_DIM,), 0.02),
        "k_norm_g": 1.0 + nrm(ks[4], (HEAD_DIM,), 0.02),
        "conv_dw": nrm(ks[5], (CONV_W, 1, CONV_CH), CONV_W ** -0.5),
        "conv_b": nrm(ks[6], (CONV_CH,), 0.01),
        "conv_ln_g": 1.0 + nrm(ks[7], (CONV_CH,), 0.02),
        "conv_ln_b": nrm(ks[8], (CONV_CH,), 0.01),
        "w_out": nrm(ks[9], (MIX_WIDTH, D_MODEL), MIX_WIDTH ** -0.5),
        "norm2_g": 1.0 + nrm(ks[10], (D_MODEL,), 0.02),
        "peer_wq": nrm(ks[11], (D_MODEL, PEER_HEADS * PEER_DQ), D_MODEL ** -0.5),
        "peer_keys": nrm(ks[12], (2, N_KEYS, PEER_DQ // 2), (PEER_DQ // 2) ** -0.5),
        "peer_u": nrm(ks[13], (N_EXPERTS, D_MODEL), D_MODEL ** -0.5),
        "peer_v": nrm(ks[14], (N_EXPERTS, D_MODEL), 0.3),
        "final_g": 1.0 + nrm(ks[15], (D_MODEL,), 0.02),
    }

def second_block(x, norm1_g, w_in, q_norm_g, k_norm_g, conv_dw, conv_b, conv_ln_g,
              conv_ln_b, w_out, norm2_g, peer_wq, peer_keys, peer_u, peer_v, final_g):
    b, s, d = x.shape
    rows = s // GRID_W
    row = jnp.repeat(jnp.arange(rows), GRID_W).astype(jnp.float32)
    col = jnp.tile(jnp.arange(GRID_W), rows).astype(jnp.float32)
    n_pairs = ROPE_AXIS_DIM // 2
    inv_freq = ROPE_THETA ** (-jnp.arange(n_pairs, dtype=jnp.float32) / n_pairs)
    ang_row = row[:, None] * inv_freq[None, :]
    ang_col = col[:, None] * inv_freq[None, :]
    group = N_HEADS // N_KV_HEADS

    for _ in range(DEPTH):
        h = _rmsnorm(x, norm1_g)
        p = h @ w_in
        o0 = ATTN_WIDTH
        o1 = o0 + KV_WIDTH
        o2 = o1 + KV_WIDTH
        o3 = o2 + CONV_CH
        q = p[..., :o0].reshape(b, s, N_HEADS, HEAD_DIM)
        k = p[..., o0:o1].reshape(b, s, N_KV_HEADS, HEAD_DIM)
        v = p[..., o1:o2].reshape(b, s, N_KV_HEADS, HEAD_DIM)
        q = _axial_rope(_rmsnorm(q, q_norm_g), ang_row, ang_col)
        k = _axial_rope(_rmsnorm(k, k_norm_g), ang_row, ang_col)
        q = (q * (HEAD_DIM ** -0.5)).reshape(b, s, N_KV_HEADS, group, HEAD_DIM)
        attn_out = _gqa_blocked(q, k, v)
        conv_out = _conformer_conv(p[..., o2:o3], p[..., o3:], conv_dw, conv_b,
                                   conv_ln_g, conv_ln_b)
        mixed = jnp.concatenate([attn_out, conv_out], axis=-1)
        x = x + mixed @ w_out
        hn = _rmsnorm(x, norm2_g).reshape(b * s, d)
        x = x + _peer(hn, peer_wq, peer_keys, peer_u, peer_v).reshape(b, s, d)

    return _rmsnorm(x, final_g)


def setup_inputs(seed=0):
    out = dict(first_inputs(seed))
    for name, value in second_inputs(seed + 1).items():
        if name != "x":
            out[name + "_2"] = value
    return out


def reference(
    x, norm_mix, w_in, w_up_a, w_up_b, w_out, norm_ffn, w_gate, w_up, w_down, norm_final,
    norm1_g_2, w_in_2, q_norm_g_2, k_norm_g_2, conv_dw_2, conv_b_2, conv_ln_g_2, conv_ln_b_2,
    w_out_2, norm2_g_2, peer_wq_2, peer_keys_2, peer_u_2, peer_v_2, final_g_2,
):
    x = first_block(
        x, norm_mix, w_in, w_up_a, w_up_b, w_out, norm_ffn, w_gate, w_up, w_down, norm_final,
    )
    return second_block(
        x, norm1_g_2, w_in_2, q_norm_g_2, k_norm_g_2, conv_dw_2, conv_b_2, conv_ln_g_2,
        conv_ln_b_2, w_out_2, norm2_g_2, peer_wq_2, peer_keys_2, peer_u_2, peer_v_2, final_g_2,
    )


_drawn_inputs = setup_inputs


def setup_inputs(seed=0):
    import zlib

    import numpy as np

    out = dict(_drawn_inputs(seed))
    spreads = {}
    factors = {'norm1_g_2': 3.384,
     'q_norm_g_2': 8.0,
     'k_norm_g_2': 8.0,
     'conv_b_2': 15.24,
     'conv_ln_g_2': 13.416,
     'conv_ln_b_2': 24.819,
     'norm2_g_2': 10.3,
     'final_g_2': 8.218}
    for name, (base, spread) in spreads.items():
        noise = np.random.default_rng([zlib.crc32(name.encode()), seed]).standard_normal(out[name].shape)
        drawn = base * np.exp(spread * noise) if base else spread * noise
        out[name] = __import__('jax').numpy.asarray(drawn.astype(out[name].dtype))
    for name, factor in factors.items():
        out[name] = (out[name] * factor).astype(out[name].dtype)
    return out
```

```python
from contextlib import ExitStack

import numpy as np
import concourse.bass as bass
from concourse import mybir

F32 = mybir.dt.float32
U32 = mybir.dt.uint32
ALU = mybir.AluOpType
ACT = mybir.ActivationFunctionType
AX_X = mybir.AxisListType.X

P = 128
T = 256
TT = T // P
D = 1024
KD = D // P
HD = 64
NH = 8
FF = 2816
KF = FF // P
TOPK = 64
TAPS = 31
PAD = (TAPS - 1) // 2
NKEY = 128
NEXP = NKEY * NKEY
ETOP = 16
NGATE = 2 * KD
CC = 4
EPS = 1e-6
NNORM = 6
TURNED = (0, 1, 3, 4)
SCALE = HD ** -0.5
IDX_SCALE = (HD ** -0.5) * (NH ** -0.5)
MASKED = -1e30
TAKEN = -3e38

SLOT = 4096
RING = 5
WEIGHTS = (["qi", "qb", "qa", "ka", "va", "ga0", "ga1", "gb0", "gb1", "upa", "upb", "wo0", "wo1"]
           + [f"ff{j}" for j in range(KF // 2)] + [f"dn{j}" for j in range(6)]
           + ["q2", "ca", "cg", "wp0", "wp1"] + [f"wq{j}" for j in range(4)])
NSLOT = len(WEIGHTS)
SMALL = 3 * HD + NH

C_ID, C_COS, C_SIN, C_ACOS, C_ASIN = 0, 128, 256, 384, 512
C_MEAN, C_IOTA, C_LOGC, C_CAUSAL = 640, 768, 784, 784 + 512
NCONST = 784 + 1024
G_NORM, G_QK, G_TAP, G_CONV, G_KEYS = 0, 32, 160, 160 + CC * TAPS, 160 + CC * TAPS + 3 * CC
NPARAM = G_KEYS + 2 * NKEY


def constants():
    c = np.zeros((P, NCONST), np.float32)
    c[:, C_ID:C_ID + P] = np.eye(P)
    half = HD // 2
    freq = (np.float32(10000.0) ** (-np.arange(half, dtype=np.float32) / np.float32(half))).astype(np.float32)
    quarter = HD // 4
    afreq = (np.float32(10000.0) ** (-np.arange(quarter, dtype=np.float32) / np.float32(quarter))).astype(np.float32)
    for t in range(TT):
        pos = np.arange(t * P, (t + 1) * P)
        ang = pos.astype(np.float32)[:, None] * freq
        c[:, C_COS + t * HD:C_COS + (t + 1) * HD] = np.concatenate([np.cos(ang)] * 2, 1)
        c[:, C_SIN + t * HD:C_SIN + (t + 1) * HD] = np.concatenate([-np.sin(ang), np.sin(ang)], 1)
        row, col = (pos // 64).astype(np.float32)[:, None] * afreq, (pos % 64).astype(np.float32)[:, None] * afreq
        c[:, C_ACOS + t * HD:C_ACOS + (t + 1) * HD] = np.concatenate(
            [np.cos(row)] * 2 + [np.cos(col)] * 2, 1)
        c[:, C_ASIN + t * HD:C_ASIN + (t + 1) * HD] = np.concatenate(
            [-np.sin(row), np.sin(row), -np.sin(col), np.sin(col)], 1)
        q, k = pos[:, None], np.arange(T)[None, :]
        dist = q - k
        count = ((dist >= 0) & (dist <= P)).astype(np.int64)
        for dilation in (4, 16):
            count += (dist >= 0) & (dist % dilation == 0)
        c[:, C_LOGC + t * T:C_LOGC + (t + 1) * T] = np.where(count > 0, np.log(np.maximum(count, 1)), MASKED)
        c[:, C_CAUSAL + t * T:C_CAUSAL + (t + 1) * T] = np.where(dist >= 0, 0.0, MASKED)
    c[:, C_MEAN:C_MEAN + P] = 1.0 / (CC * P)
    c[:, C_IOTA:C_IOTA + 16] = np.arange(16)
    return c


class Psum:

    POOLS = {"D": (0, 1, 2), "S": (3, 4), "T": (5, 6)}

    def __init__(self, banks, filled, emptied):
        self.banks, self.filled, self.emptied = banks, filled, emptied
        self.at, self.order, self.uses, self.turn = {}, [], [0] * 8, dict.fromkeys(self.POOLS, 0)
        self.started = 0

    def plan(self, pool, name, bank=None):
        if bank is None:
            bank = self.POOLS[pool][self.turn[pool] % len(self.POOLS[pool])]
            self.turn[pool] += 1
        self.at[name] = (bank, self.uses[bank])
        self.order.append(name)
        self.uses[bank] += 1

    def bank(self, name):
        return self.banks[self.at[name][0]]

    def start(self, pe, name, freed=None):
        assert self.order[self.started] == name, (self.order[self.started], name)
        self.started += 1
        b, n = self.at[name]
        if freed:
            pe.wait_ge(*freed)
        elif n:
            pe.wait_ge(self.emptied[b], n)
        return self.banks[b]

    def fill(self, ins, name):
        ins.then_inc(self.filled[self.at[name][0]], 1)

    def full(self, eng, name):
        b, n = self.at[name]
        eng.wait_ge(self.filled[b], n + 1)
        return self.banks[b]

    def empty(self, ins, name):
        ins.then_inc(self.emptied[self.at[name][0]], 1)

    def copied(self, eng, name):
        b, n = self.at[name]
        eng.wait_ge(self.emptied[b], n + 1)


def units(kind):
    return [(kind, t, j) for t in range(TT) for j in range(NH // 2)]


def pair_of(j):
    h = 4 * (j // 2) + j % 2
    return (h, h + 2)


IDX_UNITS = [(0, (0, 2, 4, 6)), (0, (1, 3, 5, 7))] + [(1, pair_of(j)) for j in range(NH // 2)]


def nkeys(kind, t):
    return TT if kind == "G" else t + 1


def plan_psum(ps):
    def norm(i):
        for t in range(TT):
            for half in range(2):
                ps.plan("ST"[half], ("norm", i, t, half))

    def attention(kind, extra):
        for s in range(len(units(kind)) + 2):
            if s < 8:
                ps.plan("S", ("scores",) + units(kind)[s])
            for name in extra.get(s, []):
                ps.plan("D", name)
            if 1 <= s < 9:
                ps.plan("T", ("probs",) + units(kind)[s - 1])
            if s == 7:
                ps.plan("T", ("y", kind, 0))
        ps.plan("T", ("y", kind, 1))

    norm(0)
    for block in ("qi", "small", "qb"):
        for t in range(TT):
            ps.plan("D", (block, t))
    for t in range(TT):
        ps.plan("T", ("turn", "qi", t))
    ps.plan("T", ("turn", "k"))
    for t in range(TT):
        ps.plan("D", ("qa", t))
    for t in range(TT):
        ps.plan("T", ("turn", "qb", t))
    for n in range(3):
        ps.plan("S", ("index", n))
    for t in range(TT):
        ps.plan("D", ("ka", t))
    for n in range(3, 6):
        ps.plan("S", ("index", n))
    for t in range(TT):
        ps.plan("T", ("turn", "qa", t))
    for t in range(TT):
        ps.plan("D", ("va", t))
    for t in range(TT):
        ps.plan("T", ("turn", "ka", t))
    attention("A", {s: [("gate", s // 2)] for s in (0, 2, 4, 6)})
    attention("B", {s: [("gate", 4 + s // 2)] for s in (0, 2, 4, 6)})
    for c in range(KD):
        ps.plan("D", ("up", c))
    for t in range(TT):
        for half in range(2):
            ps.plan("D", ("out", t, half))
    norm(1)
    for j in range(KF // 2):
        ps.plan("D", ("ffg", j))
        ps.plan("D", ("ffu", j))
    for t in range(TT):
        for half in range(2):
            n = t * 2 + half
            ps.plan(None, ("down", t, half), bank=(0, 1, 2, 3)[n])
    norm(2)
    for t in range(TT):
        ps.plan("D", ("kv2", t))
    for t in range(TT):
        ps.plan("D", ("q2", t))
    for c in range(CC):
        ps.plan("D", ("conv", c))
    ps.plan("T", ("turn", "k2"))
    for t in range(TT):
        ps.plan("T", ("turn", "q2", t))
    attention("G", {})
    ps.plan("D", ("mean",))
    ps.plan("D", ("var",))
    for t in range(TT):
        for half in range(2):
            ps.plan("D", ("out2", t, half))
    norm(3)
    for h in range(NH):
        ps.plan("D", ("query", h))
        if h:
            ps.plan("S", ("match", h - 1))
    ps.plan("S", ("match", NH - 1))
    for t in range(TT):
        for half in range(2):
            ps.plan(None, ("mix", t, half), bank=(0, 1, 2, 5)[t * 2 + half])


def bass_two_blocks_kernel(nc, x_in, stream, w_small, consts_in, params_in, norm_final, norm2_g, final_g,
                           peer_u, peer_v, out):
    with ExitStack() as ctx:
        def sb(name, shape, dt=F32):
            return ctx.enter_context(nc.sbuf_tensor(name, shape, dt))

        def sem(name):
            return ctx.enter_context(nc.semaphore(name))

        arena = sb("arena", [P, 32 * D])
        weight = [arena[:, r * SLOT:(r + 1) * SLOT] for r in range(RING)]
        gates = arena[:, RING * SLOT:RING * SLOT + NGATE * T].rearrange("p (c t) -> p c t", t=T)
        ff_at = RING * SLOT + NGATE * T
        ff = arena[:, ff_at:ff_at + KF * T].rearrange("p (c t) -> p c t", t=T)
        qT = {n: arena[:, ff_at + i * D:ff_at + (i + 1) * D].rearrange("p (c t) -> p c t", t=T)
              for i, n in enumerate(("qi", "qb", "qa", "ka"))}
        kT = arena[:, ff_at + 4 * D:ff_at + 4 * D + 512].rearrange("p (w t) -> p w t", t=T)
        va = arena[:, ff_at + 4 * D + 512:ff_at + 5 * D + 512].rearrange("p (t n) -> p t n", t=TT)
        tail = ff_at + KF * T
        rotated = arena[:, tail:tail + 2048].rearrange("p (b t n) -> p b t n", b=2, t=TT)
        vb = arena[:, tail + 2048:tail + 2048 + 128].rearrange("p (t n) -> p t n", t=TT)
        v2 = arena[:, tail + 2176:tail + 2176 + 256].rearrange("p (t n) -> p t n", t=TT)
        assert tail + 2176 + 256 <= 32 * D
        qT["q2"] = qT["qi"]
        g0 = RING * SLOT
        conv_in = arena[:, g0:g0 + CC * (T + 2 * PAD)].rearrange("p (c t) -> p c t", c=CC)
        g1 = g0 + CC * (T + 2 * PAD)
        conv_a = arena[:, g1:g1 + D].rearrange("p (c t) -> p c t", c=CC)
        conv_b = arena[:, g1 + D:g1 + 2 * D].rearrange("p (c t) -> p c t", c=CC)
        rstd_c = arena[:, g1 + 2 * D:g1 + 2 * D + 2 * T].rearrange("p (c t) -> p c t", c=2)
        assert g1 + 2 * D + 2 * T <= ff_at
        v_rows = [arena[:, i * D:(i + 1) * D] for i in range(ETOP)]
        u_rows = [arena[:, (ETOP + i) * D:(ETOP + i + 1) * D] for i in range(ETOP)]

        X = sb("residual", [P, TT, D])
        xs = sb("normed", [P, TT, D])
        merged = xs[:, :, :].rearrange("p t n -> p (t n)").rearrange("p (c t) -> p c t", t=T)
        hT = sb("hT", [P, KD, T])
        yT = sb("yT", [P, KD, T])
        hn = yT[:, :, :].rearrange("p c t -> p (c t)").rearrange("p (t n) -> p t n", t=TT)
        consts = sb("consts", [P, NCONST])
        params = sb("params", [P, NPARAM])
        gain2 = sb("gain2", [P, D])
        tmp = gain2[:, :].rearrange("p (b n) -> p b n", b=2)

        work = sb("work", [P, 7168])
        S_sb = work[:, 0:1024].rearrange("p (b n) -> p b n", b=2)
        E_sb = work[:, 1024:2048].rearrange("p (b n) -> p b n", b=2)
        PT = work[:, 2048:3072].rearrange("p (b n) -> p b n", b=2)
        relu = work[:, 3072:4096].rearrange("p (b n) -> p b n", b=2)
        score = work[:, 4096:4608].rearrange("p (t n) -> p t n", t=TT)
        selected = work[:, 4608:5120].rearrange("p (t n) -> p t n", t=TT)
        small_w = work[:, 5120:5120 + KD * SMALL].rearrange("p (k n) -> p k n", k=KD)
        assert KD * SMALL <= 2048
        match = work[:, 0:4096].rearrange("p (g n) -> p g n", g=TT * NH)
        diag = work[:, 4096:6144].rearrange("p (i n) -> p i n", i=ETOP)
        query = work[:, 6144:7168].rearrange("p (b w t) -> p b w t", b=2, w=2)
        y_tok = work[:, 5120:5120 + NH * HD]

        sumsq = sb("sumsq", [P, 2 * NNORM])
        var = sb("var", [P, 2 * NNORM])
        root = sb("root", [P, 2 * NNORM])
        rstd = sb("rstd", [P, 2 * NNORM])
        flag = sb("flag", [P, 1])
        wi = sb("wi", [P, TT, NH])
        top8 = sb("top8", [P, 8])
        negmax = sb("negmax", [P, 3, TT, NH])
        den = sb("den", [P, 3, TT, NH])
        rden = sb("rden", [P, 3, TT, NH])
        head_ss = sb("head_ss", [P, 2, NH])
        head_var = sb("head_var", [P, 2, NH])
        head_root = sb("head_root", [P, 2, NH])
        head_rstd = sb("head_rstd", [P, 2, NH])
        turn_tab = sb("turn_tab", [P, TT, 4, HD])
        s_work = gain2[:, 0:4 * NKEY].rearrange("p (s w n) -> p s w n", s=2, w=2)
        s_top = sb("s_top", [P, 2, ETOP])
        s_idx = sb("s_idx", [P, 2, ETOP], U32)
        cand = gain2[:, 4 * NKEY:4 * NKEY + 512].rearrange("p (s n) -> p s n", s=2)
        c_top = sb("c_top", [P, 2, ETOP])
        c_pos = sb("c_pos", [P, ETOP], U32)
        c_digit = sb("c_digit", [P, 2, ETOP], U32)
        c_part = sb("c_part", [P, 2, ETOP])
        expert = sb("expert", [P, 2, ETOP], U32)
        c_neg = sb("c_neg", [P, 2, 1])
        c_exp = sb("c_exp", [P, 2, ETOP])
        c_sum = sb("c_sum", [P, 2, 1])
        c_rs = sb("c_rs", [P, 2, 1])
        dots = sb("dots", [P, ETOP])
        gelu = sb("gelu", [P, ETOP])
        mixw = sb("mixw", [P, ETOP])

        ident = consts[:, C_ID:C_ID + P]
        mean_w = consts[:, C_MEAN:C_MEAN + P]
        iota = consts[:, C_IOTA:C_IOTA + 16]
        final_gain = consts[:, C_LOGC:C_LOGC + D]
        keysT = params[:, G_KEYS:G_KEYS + 2 * NKEY].rearrange("p (w n) -> p w n", w=2)

        def table(at, t, n=HD):
            return consts[:, at + t * n:at + (t + 1) * n]

        filled = [sem(f"filled_bank{b}") for b in range(7)]
        emptied = [sem(f"emptied_bank{b}") for b in range(7)]
        banks = [ctx.enter_context(nc.psum_tensor(f"bank{b}", [P, 512], F32)) for b in range(8)]
        y_bank = banks[7]
        ps = Psum(banks, filled, emptied)
        plan_psum(ps)
        weight_in = [sem(f"weight_in{r}") for r in range(RING)]
        x_in_done = [sem(f"x_in{t}") for t in range(TT)]
        consts_done = sem("consts_in")
        small_done = sem("small_in")
        gain2_done = sem("gain2_in")
        norm_final_done = sem("norm_final_in")
        final_done = sem("final_gain_in")
        sumsq_done = sem("sumsq_done")
        var_done = sem("var_done")
        residual_done = sem("residual_done")
        merged_done = sem("merged_done")
        root_done = sem("root_done")
        normed = sem("normed")
        rotated_done = sem("rotated_done")
        relu_used = sem("relu_used")
        max_done = sem("max_done")
        exp_done = sem("exp_done")
        pv_done = sem("pv_done")
        y_emptied = sem("y_emptied")
        gate_done = sem("gate_done")
        down_read = sem("down_read")
        act_step = sem("act_step")
        dve_step = sem("dve_step")
        head_sq_done = sem("head_sq_done")
        head_var_done = sem("head_var_done")
        head_root_done = sem("head_root_done")
        conv_sig = sem("conv_sig")
        conv_done = sem("conv_done")
        center_done = sem("center_done")
        square_done = sem("square_done")
        lvar_done = sem("lvar_done")
        lroot_done = sem("lroot_done")
        lnorm_done = sem("lnorm_done")
        conv_out = sem("conv_out")
        match_done = sem("match_done")
        u_free = sem("u_batches_free")
        v_free = sem("v_batches_free")
        u_in = [sem(f"u_in{b}") for b in range(4)]
        v_in = [sem(f"v_in{b}") for b in range(4)]
        experts_ready = sem("experts_ready")
        cexp_done = sem("cexp_done")
        gelu_done = sem("gelu_done")
        mixw_done = sem("mixw_done")
        diag_done = sem("diag_done")
        fout_done = sem("fout_done")
        out_done = sem("out_done")

        def weight_ready(eng, name):
            n = WEIGHTS.index(name)
            eng.wait_ge(weight_in[n % RING], 16 * (n // RING + 1))
            return weight[n % RING]

        block = ctx.enter_context(nc.Block())

        @block.sync
        def _(sp):
            for t in range(TT):
                sp.dma_start(X[:, t, :], x_in[t * P:(t + 1) * P, :]).then_inc(x_in_done[t], 16)
            sp.dma_start(consts[:, :], consts_in).then_inc(consts_done, 16)
            sp.dma_start(params[:, :], params_in).then_inc(consts_done, 16)
            last = {"qi": ("qi", 1), "qb": ("qb", 1), "qa": ("qa", 1), "ka": ("ka", 1), "va": ("va", 1),
                    "ga0": ("gate", 1), "ga1": ("gate", 3), "gb0": ("gate", 5), "gb1": ("gate", 7),
                    "upa": ("up", KD - 1), "upb": ("up", KD - 1), "wo0": ("out", 1, 0), "wo1": ("out", 1, 1),
                    "dn5": ("kv2", 1), "q2": ("q2", 1), "ca": ("conv", CC - 1), "cg": ("conv", CC - 1),
                    "wp0": ("out2", 1, 0), "wp1": ("out2", 1, 1)}
            for n, name in enumerate(WEIGHTS):
                if n >= RING:
                    before = WEIGHTS[n - RING]
                    if before in last:
                        ps.full(sp, last[before])
                    elif before.startswith("ff"):
                        ps.full(sp, ("ffu", int(before[2:])))
                    else:
                        sp.wait_ge(down_read, int(before[2:]) + 1)
                sp.dma_start(weight[n % RING], stream[n]).then_inc(weight_in[n % RING], 16)
                if name == "qi":
                    sp.dma_start(small_w, w_small).then_inc(small_done, 16)
                if name == "dn0":
                    sp.wait_ge(merged_done, KD)
                    sp.dma_start(gain2[:, :], norm_final).then_inc(norm_final_done, 16)
                if name == "wq0":
                    ps.full(sp, ("out2", 0, 0))
                    sp.dma_start(gain2[:, :], norm2_g).then_inc(gain2_done, 16)
                    sp.dma_start(final_gain, final_g).then_inc(final_done, 16)
            for t in range(TT):
                sp.wait_ge(fout_done, t + 1)
                sp.dma_start(out[t * P:(t + 1) * P, :], X[:, t, :]).then_inc(out_done, 16)
            sp.wait_ge(out_done, 16 * TT)

        @block.tensor
        def _(pe):
            mm = nc.tensor.matmul

            def normed_turn(i):
                for t in range(TT):
                    pe.wait_ge(normed, TT * i + t + 1)
                    for half in range(2):
                        name = ("norm", i, t, half)
                        bank = ps.start(pe, name)
                        for c in range(4):
                            k = 4 * half + c
                            ins = nc.tensor.transpose(bank[:, c * P:(c + 1) * P], xs[:, t, k * P:(k + 1) * P], ident)
                        ps.fill(ins, name)
                for t in range(TT):
                    for half in range(2):
                        ps.copied(pe, ("norm", i, t, half))

            def tokens(block_name, t, w, n):
                bank = ps.start(pe, (block_name, t))
                for k in range(KD):
                    ins = mm(bank[:, 0:n], hT[:, k, t * P:(t + 1) * P], w[:, k, 0:n], start=k == 0, stop=k == KD - 1)
                ps.fill(ins, (block_name, t))

            def cols(name, n=512):
                return weight_ready(pe, name)[:, 0:KD * n].rearrange("p (k n) -> p k n", n=n)

            def turn(source, name, n):
                bank = ps.start(pe, name)
                for c in range(n):
                    ins = nc.tensor.transpose(bank[:, c * P:(c + 1) * P], source(c), ident)
                ps.fill(ins, name)

            def turn_queries(name, b, count):
                for t in range(TT):
                    pe.wait_ge(rotated_done, count + t)
                    turn(lambda c: rotated[:, b, t, c * P:(c + 1) * P], ("turn", name, t), 4)

            pe.wait_ge(consts_done, 32)
            normed_turn(0)
            w = cols("qi")
            for t in range(TT):
                tokens("qi", t, w, 512)
            pe.wait_ge(small_done, 16)
            for t in range(TT):
                tokens("small", t, small_w, SMALL)
            w = cols("qb")
            for t in range(TT):
                tokens("qb", t, w, 512)
            turn_queries("qi", 0, 1)
            pe.wait_ge(rotated_done, 4)
            turn(lambda c: rotated[:, 1, c % 2, (c // 2) * P:(c // 2 + 1) * P], ("turn", "k"), 4)
            w = cols("qa")
            for t in range(TT):
                tokens("qa", t, w, 512)
            turn_queries("qb", 0, 5)

            def index_unit(n):
                t, heads = IDX_UNITS[n]
                nk = (t + 1) * P
                bank = ps.start(pe, ("index", n))
                for i, h in enumerate(heads):
                    rows = slice(HD * (h % 2), HD * (h % 2) + HD)
                    ins = mm(bank[:, i * nk:(i + 1) * nk], qT["qi"][rows, h // 2, t * P:(t + 1) * P],
                             kT[rows, 0, 0:nk], start=True, stop=True)
                ps.fill(ins, ("index", n))

            for t in range(TT):
                ps.copied(pe, ("turn", "qi", t))
            ps.copied(pe, ("turn", "k"))
            for n in range(3):
                index_unit(n)
            w = cols("ka")
            for t in range(TT):
                tokens("ka", t, w, 512)
            for n in range(3, 6):
                index_unit(n)
            turn_queries("qa", 1, 7)
            w = cols("va")
            for t in range(TT):
                tokens("va", t, w, 512)
            turn_queries("ka", 0, 9)

            def gate_fill(f):
                w = weight_ready(pe, ("ga0", "ga1", "gb0", "gb1")[f // 2])
                w = w.rearrange("p (k n) -> p k n", k=KD)
                bank = ps.start(pe, ("gate", f))
                for c in range(2):
                    at = ((2 * f + c) % 4) * P
                    for k in range(KD):
                        ins = mm(bank[:, c * T:(c + 1) * T], w[:, k, at:at + P], hT[:, k, :], start=k == 0, stop=k == KD - 1)
                ps.fill(ins, ("gate", f))

            def attention(kind, index, queries, key_of, value_of, beside):
                todo = units(kind)
                for s in range(len(todo) + 2):
                    if s < len(todo):
                        _, t, j = todo[s]
                        nk = nkeys(kind, t) * P
                        bank = ps.start(pe, ("scores",) + todo[s])
                        for i, h in enumerate(pair_of(j)):
                            rows = slice(HD * (h % 2), HD * (h % 2) + HD)
                            ins = mm(bank[:, i * nk:(i + 1) * nk], queries[rows, h // 2, t * P:(t + 1) * P],
                                     key_of(h)[rows, 0:nk], start=True, stop=True)
                        ps.fill(ins, ("scores",) + todo[s])
                    if beside and s % 2 == 0 and s < 8:
                        gate_fill(beside - 1 + s // 2)
                    if 1 <= s < 9:
                        _, t, j = todo[s - 1]
                        nb = nkeys(kind, t)
                        pe.wait_ge(exp_done, 8 * index + s)
                        turn(lambda c: E_sb[:, (s - 1) % 2, c * P:(c + 1) * P], ("probs",) + todo[s - 1], 2 * nb)
                    if s == 7:
                        turn_y(kind, index, 0)
                    if s >= 2:
                        _, t, j = todo[s - 2]
                        nb = nkeys(kind, t)
                        ps.copied(pe, ("probs",) + todo[s - 2])
                        if j == 0 and 2 * index + t:
                            pe.wait_ge(y_emptied, 2 * index + t)
                        for i, h in enumerate(pair_of(j)):
                            for kb in range(nb):
                                ins = mm(y_bank[:, h * HD:(h + 1) * HD], PT[:, (s - 2) % 2, (i * nb + kb) * P:(i * nb + kb + 1) * P],
                                         value_of(kb, h), start=kb == 0, stop=kb == nb - 1)
                        ins.then_inc(pv_done, 1)
                turn_y(kind, index, 1)

            def turn_y(kind, index, t):
                pe.wait_ge(y_emptied, 2 * index + t + 1)
                turn(lambda c: y_tok[:, c * P:(c + 1) * P], ("y", kind, t), 4)

            for name in ("qa", "ka"):
                for t in range(TT):
                    ps.copied(pe, ("turn", name, t))
            for t in range(TT):
                ps.copied(pe, ("va", t))
            attention("A", 0, qT["qa"], lambda h: qT["ka"][:, h // 2, :], lambda kb, h: va[:, kb, h * HD:(h + 1) * HD], 1)
            for t in range(TT):
                ps.copied(pe, ("turn", "qb", t))
            attention("B", 1, qT["qb"], lambda h: kT[:, 1, :], lambda kb, h: vb[:, kb, :], 5)

            upa = weight_ready(pe, "upa").rearrange("p (k n) -> p k n", k=4)
            upb = weight_ready(pe, "upb").rearrange("p (k n) -> p k n", k=4)
            for kind in "AB":
                for t in range(TT):
                    ps.copied(pe, ("y", kind, t))
            for c in range(KD):
                bank = ps.start(pe, ("up", c))
                for i, w in enumerate((upa, upb)):
                    for k in range(4):
                        ins = mm(bank[:, i * T:(i + 1) * T], w[:, k, c * P:(c + 1) * P], yT[:, 4 * i + k, :],
                                 start=k == 0, stop=k == 3)
                ps.fill(ins, ("up", c))

            def project(name, w0, w1, source):
                w = [weight_ready(pe, n).rearrange("p (k n) -> p k n", k=KD) for n in (w0, w1)]
                for t in range(TT):
                    for half in range(2):
                        bank = ps.start(pe, (name, t, half))
                        for k in range(KD):
                            ins = mm(bank[:, :], source[:, k, t * P:(t + 1) * P], w[half][:, k, :],
                                     start=k == 0, stop=k == KD - 1)
                        ps.fill(ins, (name, t, half))

            pe.wait_ge(merged_done, KD)
            project("out", "wo0", "wo1", merged)

            normed_turn(1)
            for j in range(KF // 2):
                w = weight_ready(pe, f"ff{j}").rearrange("p (k n) -> p k n", k=KD)
                for part, name in enumerate(("ffg", "ffu")):
                    bank = ps.start(pe, (name, j))
                    for c in range(2):
                        at = (2 * part + c) * P
                        for k in range(KD):
                            ins = mm(bank[:, c * T:(c + 1) * T], w[:, k, at:at + P], hT[:, k, :], start=k == 0, stop=k == KD - 1)
                    ps.fill(ins, (name, j))
            accs = [[ps.start(pe, ("down", t, half)) for half in range(2)] for t in range(TT)]
            for j in range(6):
                w = weight_ready(pe, f"dn{j}").rearrange("p (k n) -> p k n", k=4)
                nk = min(4, KF - 4 * j)
                for k in range(4 * j, 4 * j + nk):
                    if k % 2 == 0:
                        ps.copied(pe, ("ffu", k // 2))
                for t in range(TT):
                    for k in range(4 * j, 4 * j + nk):
                        for half in range(2):
                            ins = mm(accs[t][half][:, :], ff[:, k, t * P:(t + 1) * P], w[:, k - 4 * j, half * 512:(half + 1) * 512],
                                     start=k == 0, stop=k == KF - 1)
                            if k == KF - 1:
                                ps.fill(ins, ("down", t, half))
                if j < 5:
                    ins.then_inc(down_read, 1)

            normed_turn(2)
            w = weight_ready(pe, "dn5")[:, 2 * D:4 * D].rearrange("p (k n) -> p k n", k=KD)
            for t in range(TT):
                tokens("kv2", t, w, T)
            w = cols("q2")
            for t in range(TT):
                tokens("q2", t, w, 512)
            wa = weight_ready(pe, "ca").rearrange("p (k n) -> p k n", k=KD)
            wg = weight_ready(pe, "cg").rearrange("p (k n) -> p k n", k=KD)
            for c in range(CC):
                bank = ps.start(pe, ("conv", c))
                for i, w in enumerate((wa, wg)):
                    for k in range(KD):
                        ins = mm(bank[:, i * T:(i + 1) * T], w[:, k, c * P:(c + 1) * P], hT[:, k, :], start=k == 0, stop=k == KD - 1)
                ps.fill(ins, ("conv", c))
            pe.wait_ge(rotated_done, 12)
            turn(lambda c: rotated[:, 0, c % 2, (c // 2) * P:(c // 2 + 1) * P], ("turn", "k2"), 4)
            turn_queries("q2", 1, 13)
            ps.copied(pe, ("turn", "k2"))
            for t in range(TT):
                ps.copied(pe, ("turn", "q2", t))
            attention("G", 2, qT["q2"], lambda h: kT[:, h // 4, :], lambda kb, h: v2[:, kb, (h // 4) * HD:(h // 4 + 1) * HD], 0)
            pe.wait_ge(conv_done, 1)
            bank = ps.start(pe, ("mean",))
            for c in range(CC):
                ins = mm(bank[:, 0:T], mean_w, conv_a[:, c, :], start=c == 0, stop=c == CC - 1)
            ps.fill(ins, ("mean",))
            pe.wait_ge(square_done, 1)
            bank = ps.start(pe, ("var",))
            for c in range(CC):
                ins = mm(bank[:, 0:T], mean_w, conv_b[:, c, :], start=c == 0, stop=c == CC - 1)
            ps.fill(ins, ("var",))
            for t in range(TT):
                ps.copied(pe, ("y", "G", t))
            pe.wait_ge(conv_out, 1)
            project("out2", "wp0", "wp1", yT)

            normed_turn(3)

            def key_scores(h):
                ps.copied(pe, ("query", h))
                bank = ps.start(pe, ("match", h), freed=(match_done, h - 1) if h >= 2 else None)
                for t in range(TT):
                    for i in range(2):
                        at = (2 * t + i) * NKEY
                        ins = mm(bank[:, at:at + NKEY], query[:, h % 2, i, t * P:(t + 1) * P], keysT[:, i, :],
                                 start=True, stop=True)
                        if h % 2 and t == 0 and i == 0:
                            ins.then_inc(v_free, 1)
                ps.fill(ins, ("match", h))

            for h in range(NH):
                w = weight_ready(pe, f"wq{h // 2}").rearrange("p (k n) -> p k n", k=KD)
                bank = ps.start(pe, ("query", h))
                for i in range(2):
                    at = (2 * (h % 2) + i) * P
                    for k in range(KD):
                        ins = mm(bank[:, i * T:(i + 1) * T], w[:, k, at:at + P], hT[:, k, :], start=k == 0, stop=k == KD - 1)
                ps.fill(ins, ("query", h))
                if h:
                    key_scores(h - 1)
            key_scores(NH - 1)

            for t in range(TT):
                accs = [ps.start(pe, ("mix", t, half)) for half in range(2)]
                for half in range(2):
                    mm(accs[half][:, :], ident, X[:, t, half * 512:(half + 1) * 512], start=True, stop=True)
                with pe.Fori(t * NH, (t + 1) * NH, 1) as g:
                    for b in range(4):
                        pe.wait_ge(v_in[b], (g + 1) * 64)
                        pe.wait_ge(diag_done, g * 4 + (b + 1))
                        for i in range(4 * b, 4 * b + 4):
                            for half in range(2):
                                ins = mm(accs[half][:, :], diag[:, i, :], v_rows[i][:, half * 512:(half + 1) * 512],
                                         start=False, stop=True, skip_group_check=True)
                        ins.then_inc(v_free, 1)

        @block.scalar
        def _(act):
            activation = nc.scalar.activation
            steps = [0]

            def settle(ins):
                steps[0] += 1
                ins.then_inc(act_step, 1)
                act.wait_ge(act_step, steps[0])

            def norm_sums(i):
                for t in range(TT):
                    if i == 0:
                        act.wait_ge(x_in_done[t], 16)
                    else:
                        act.wait_ge(residual_done, TT * (i - 1) + t + 1)
                    activation(hT[:, 4 * t:4 * t + 4, :].rearrange("p c t -> p (c t)"), X[:, t, :], ACT.Square,
                               accum_out=sumsq[:, TT * i + t:TT * i + t + 1]).then_inc(sumsq_done, 1)
                    act.wait_ge(var_done, TT * i + t + 1)
                    activation(root[:, TT * i + t:TT * i + t + 1], var[:, TT * i + t:TT * i + t + 1],
                               ACT.Sqrt).then_inc(root_done, 1)

            def copy_turned(name, out_ap):
                bank = ps.full(act, name)
                ps.empty(activation(out_ap, bank[:, :].rearrange("p (c t) -> p c t", c=4), ACT.Copy), name)

            def index_relu(n):
                bank = ps.full(act, ("index", n))
                if n >= 2:
                    act.wait_ge(relu_used, n - 1)
                ps.empty(activation(relu[:, n % 2, :], bank[:, :], ACT.Relu), ("index", n))

            def attention(kind, index, base, beside):
                todo = units(kind)
                for s in range(len(todo) + 1):
                    if s < len(todo):
                        _, t, j = todo[s]
                        nk = nkeys(kind, t) * P
                        act.wait_ge(max_done, 8 * index + s + 1)
                        if s >= 2:
                            ps.full(act, ("probs",) + todo[s - 2])
                        for i, h in enumerate(pair_of(j)):
                            source = ps.bank(("scores",) + todo[s]) if kind == "G" else S_sb[:, s % 2, :]
                            ins = activation(E_sb[:, s % 2, i * nk:(i + 1) * nk], source[:, i * nk:(i + 1) * nk], ACT.Exp,
                                             bias=negmax[:, index, t, h:h + 1], scale=SCALE if kind == "G" else 1.0,
                                             accum_out=den[:, index, t, h:h + 1])
                        ins.then_inc(exp_done, 1)
                    if beside and s % 2 == 0 and s < 8:
                        f = beside - 1 + s // 2
                        bank = ps.full(act, ("gate", f))
                        ps.empty(activation(gates[:, 2 * f:2 * f + 2, :], bank[:, :].rearrange("p (c t) -> p c t", c=2),
                                            ACT.Copy), ("gate", f))
                    if s == 8:
                        copy_turned(("y", kind, 0), yT[:, base:base + 4, 0:P])
                    if s >= 1:
                        name = ("probs",) + todo[s - 1]
                        n = 2 * nkeys(kind, todo[s - 1][1]) * P
                        bank = ps.full(act, name)
                        if s >= 3:
                            act.wait_ge(pv_done, 8 * index + s - 2)
                        ps.empty(activation(PT[:, (s - 1) % 2, 0:n], bank[:, 0:n], ACT.Copy), name)
                copy_turned(("y", kind, 1), yT[:, base:base + 4, P:T])

            act.wait_ge(consts_done, 32)
            norm_sums(0)
            for t in range(TT):
                copy_turned(("turn", "qi", t), qT["qi"][:, :, t * P:(t + 1) * P])
            name = ("turn", "k")
            ps.empty(activation(kT[:, :, :].rearrange("p w t -> p (w t)"), ps.full(act, name)[:, :], ACT.Copy), name)
            for t in range(TT):
                copy_turned(("turn", "qb", t), qT["qb"][:, :, t * P:(t + 1) * P])
            for n in range(6):
                index_relu(n)
            for t in range(TT):
                copy_turned(("turn", "qa", t), qT["qa"][:, :, t * P:(t + 1) * P])
            for t in range(TT):
                bank = ps.full(act, ("va", t))
                ps.empty(activation(va[:, t, :], bank[:, :], ACT.Copy), ("va", t))
            for t in range(TT):
                copy_turned(("turn", "ka", t), qT["ka"][:, :, t * P:(t + 1) * P])
            attention("A", 0, 0, 1)
            attention("B", 1, 4, 5)
            ps.copied(act, ("gate", 7))
            ps.copied(act, ("gate", 6))
            ps.copied(act, ("gate", 5))
            for half in range(2):
                part = gates.rearrange("p (g c) t -> p g (c t)", g=2)[:, :, half * 4 * T:(half + 1) * 4 * T]
                activation(part, part, ACT.Sigmoid).then_inc(gate_done, 1)

            norm_sums(1)
            for j in range(KF // 2):
                bank = ps.full(act, ("ffg", j))
                ps.empty(activation(ff[:, 2 * j:2 * j + 2, :], bank[:, :].rearrange("p (c t) -> p c t", c=2), ACT.Silu), ("ffg", j))
            norm_sums(2)
            norm_sums(3)

            for n in range(2 * TT):
                t = n % TT
                name, cols = (("kv2", t), 2 * HD) if n < TT else (("q2", t), NH * HD)
                bank = ps.full(act, name)
                if n >= 2:
                    act.wait_ge(head_var_done, n - 1)
                activation(relu[:, n % 2, 0:cols], bank[:, 0:cols], ACT.Square).then_inc(head_sq_done, 1)
                act.wait_ge(head_var_done, n + 1)
                nh = cols // HD
                activation(head_root[:, n % 2, 0:nh], head_var[:, n % 2, 0:nh], ACT.Sqrt).then_inc(head_root_done, 1)
            for c in range(CC):
                bank = ps.full(act, ("conv", c))
                activation(conv_b[:, c, :], bank[:, T:2 * T], ACT.Sigmoid).then_inc(conv_sig, 1)
            name = ("turn", "k2")
            ps.empty(activation(kT[:, :, :].rearrange("p w t -> p (w t)"), ps.full(act, name)[:, :], ACT.Copy), name)
            for t in range(TT):
                copy_turned(("turn", "q2", t), qT["q2"][:, :, t * P:(t + 1) * P])
            attention("G", 2, 0, 0)
            act.wait_ge(center_done, 1)
            activation(conv_b[:, :, :], conv_a[:, :, :], ACT.Square).then_inc(square_done, 1)
            act.wait_ge(lvar_done, 1)
            activation(rstd_c[:, 1, :], rstd_c[:, 0, :], ACT.Sqrt).then_inc(lroot_done, 1)
            act.wait_ge(lnorm_done, 1)
            for c in range(CC):
                ins = activation(yT[:, 4 + c, :], conv_a[:, c, :], ACT.Silu,
                                 bias=params[:, G_CONV + 2 * CC + c:G_CONV + 2 * CC + c + 1],
                                 scale=params[:, G_CONV + CC + c:G_CONV + CC + c + 1])
            ins.then_inc(conv_out, 1)
            norm_sums(4)

            def copy_query(h):
                bank = ps.full(act, ("query", h))
                if h >= 2:
                    ps.full(act, ("match", h - 2))
                ps.empty(activation(query[:, h % 2, :, :], bank[:, :].rearrange("p (w t) -> p w t", w=2), ACT.Copy), ("query", h))

            def copy_match(h):
                bank = ps.full(act, ("match", h))
                out_ap = match.rearrange("p (t h) n -> p t h n", t=TT)[:, :, h, :]
                activation(out_ap, bank[:, :].rearrange("p (t n) -> p t n", t=TT), ACT.Copy)\
                    .then_inc(match_done, 1 if h < NH - 1 else 1 + NH)

            for h in range(NH):
                copy_query(h)
                if h:
                    copy_match(h - 1)
            copy_match(NH - 1)

            with act.Fori(0, TT * NH, 2) as g0:
                for b in range(2):
                    g = g0 + b
                    act.wait_ge(experts_ready, g + 1)
                    activation(c_exp[:, b, :], c_top[:, b, :], ACT.Exp, bias=c_neg[:, b, :],
                               accum_out=c_sum[:, b, :]).then_inc(cexp_done, 1)
                    act.wait_ge(u_free, g * 4 + 8)
                    activation(gelu[:, :], dots[:, :], ACT.Gelu_apprx_tanh).then_inc(gelu_done, 1)
                    act.wait_ge(mixw_done, g + 1)
                    for batch in range(4):
                        act.wait_ge(v_free, g * 4 + batch + 1)
                        for i in range(4 * batch, 4 * batch + 4):
                            ins = activation(diag[:, i, :], ident, ACT.Copy, scale=mixw[:, i:i + 1])
                        ins.then_inc(diag_done, 1)
            norm_sums(5)

        @block.vector
        def _(dve):
            v = nc.vector
            steps = [0]
            loop_step = dve.alloc_register("dve_loop_step")
            in_loop = [False]

            def settle(ins):
                steps[0] += 1
                ins.then_inc(dve_step, 1)
                if in_loop[0]:
                    dve.wait_ge(dve_step, loop_step)
                    dve.reg_add(loop_step, loop_step, 1)
                else:
                    dve.wait_ge(dve_step, steps[0])

            def column(buf, n):
                return buf[:, n:n + 1]

            def row(ap, n, width):
                return ap.unsqueeze(1).broadcast_to([P, n, width])

            def each(ap, n, width):
                return ap.unsqueeze(2).broadcast_to([P, n, width])

            def norm_scale(i, t):
                n = TT * i + t
                dve.wait_ge(sumsq_done, n + 1)
                v.tensor_scalar(column(var, n), column(sumsq, n), 1.0 / D, EPS, ALU.mult, ALU.add).then_inc(var_done, 1)
                dve.wait_ge(root_done, n + 1)
                settle(v.reciprocal(column(rstd, n), column(root, n)))

            def norm(i):
                for t in range(TT):
                    norm_scale(TURNED[i], t)
                    v.tensor_scalar(xs[:, t, :], X[:, t, :], column(rstd, TT * TURNED[i] + t), None,
                                    ALU.mult).then_inc(normed, 1)
                dve.wait_ge(normed, TT * (i + 1))
                for t in range(TT):
                    for half in range(2):
                        name = ("norm", i, t, half)
                        bank = ps.full(dve, name)
                        at = G_NORM + 8 * i + 4 * half
                        ps.empty(v.tensor_tensor(hT[:, 4 * half:4 * half + 4, t * P:(t + 1) * P],
                                                 bank[:, :].rearrange("p (c t) -> p c t", c=4),
                                                 each(params[:, at:at + 4], 4, P), ALU.mult), name)

            def residual(i, name):
                for t in range(TT):
                    for half in range(2):
                        bank = ps.full(dve, (name, t, half))
                        part = X[:, t, half * 512:(half + 1) * 512]
                        ps.empty(v.tensor_tensor(part, part, bank[:, :], ALU.add), (name, t, half))
                    ps.copied(dve, (name, t, 0))
                    ps.copied(dve, (name, t, 1))
                    v.memset(flag[:, :], 0.0).then_inc(residual_done, 1)
                    dve.wait_ge(residual_done, TT * i + t + 1)

            def rope(source, heads, t, out_ap, last):
                n = heads * HD
                a, b = tmp[:, 0, 0:n], tmp[:, 1, 0:n]
                halves = lambda ap: ap.rearrange("p (h w) -> p h w", h=2)
                settle(v.tensor_tensor(a.rearrange("p (h w) -> p h w", w=HD), source.rearrange("p (h w) -> p h w", w=HD),
                                       row(table(C_COS, t), heads, HD), ALU.mult))
                swapped = source.rearrange("p (h s w) -> p h s w", s=2, w=HD // 2)[:, :, ::-1, :]
                sine = table(C_SIN, t).rearrange("p (s w) -> p s w", s=2).unsqueeze(1).broadcast_to([P, heads, 2, HD // 2])
                ins = v.tensor_tensor(b.rearrange("p (h s w) -> p h s w", s=2, w=HD // 2), swapped, sine, ALU.mult)
                if last is not None:
                    ps.empty(ins, last)
                    ps.copied(dve, last)
                else:
                    settle(ins)
                if out_ap.shape == (P, n):
                    return v.tensor_tensor(out_ap, a, b, ALU.add)
                return v.tensor_tensor(out_ap, row(a, 2, n), row(b, 2, n), ALU.add)

            def rope_queries(name, b, before):
                for t in range(TT):
                    bank = ps.full(dve, (name, t))
                    if before is not None:
                        ps.full(dve, before(t))
                    rope(bank[:, :], NH, t, rotated[:, b, t, :], (name, t)).then_inc(rotated_done, 1)
                    rotated_count[0] += 1
                    dve.wait_ge(rotated_done, rotated_count[0])

            rotated_count = [0]

            dve.wait_ge(consts_done, 32)
            for t in range(TT):
                for w in range(2):
                    gain = params[:, G_QK + w * HD:G_QK + (w + 1) * HD]
                    v.tensor_tensor(turn_tab[:, t, 2 * w, :], table(C_ACOS, t), gain, ALU.mult)
                    four = lambda ap: ap.rearrange("p (g s w) -> p g s w", g=2, s=2)
                    last = v.tensor_tensor(four(turn_tab[:, t, 2 * w + 1, :]), four(table(C_ASIN, t)),
                                           four(gain)[:, :, ::-1, :], ALU.mult)
            settle(last)
            norm(0)
            rope_queries("qi", 0, None)
            for t in range(TT):
                bank = ps.full(dve, ("small", t))
                v.tensor_copy(vb[:, t, :], bank[:, HD:2 * HD])
                v.tensor_copy(wi[:, t, :], bank[:, 3 * HD:SMALL])
                settle(rope(bank[:, 2 * HD:3 * HD], 1, t, rotated[:, 1, t, 0:P].rearrange("p (w n) -> p w n", w=2), None))
                rope(bank[:, 0:HD], 1, t, rotated[:, 1, t, P:2 * P].rearrange("p (w n) -> p w n", w=2),
                     ("small", t)).then_inc(rotated_done, 1)
                rotated_count[0] += 1
                dve.wait_ge(rotated_done, rotated_count[0])
            rope_queries("qb", 0, lambda t: ("turn", "qi", t))
            rope_queries("qa", 1, lambda t: ("turn", "k"))

            def index_sum(n):
                t, heads = IDX_UNITS[n]
                nk = (t + 1) * P
                ps.copied(dve, ("index", n))
                for i, h in enumerate(heads):
                    part = relu[:, n % 2, i * nk:(i + 1) * nk]
                    if h == 0:
                        ins = v.tensor_scalar(score[:, t, 0:nk], part, wi[:, t, 0:1], None, ALU.mult)
                    else:
                        ins = v.scalar_tensor_tensor(score[:, t, 0:nk], part, wi[:, t, h:h + 1], score[:, t, 0:nk],
                                                     ALU.mult, ALU.add)
                    if h != heads[-1]:
                        settle(ins)
                ins.then_inc(relu_used, 1)
                dve.wait_ge(relu_used, n + 1)

            for n in range(3):
                index_sum(n)
            rope_queries("ka", 0, lambda t: ("turn", "qb", t))
            for n in range(3, 6):
                index_sum(n)
            for t in range(TT):
                nk = (t + 1) * P
                settle(v.scalar_tensor_tensor(score[:, t, 0:nk], score[:, t, 0:nk], IDX_SCALE, table(C_CAUSAL, t, T)[:, 0:nk],
                                              ALU.mult, ALU.add))

            def select_round(t):
                nk = (t + 1) * P
                settle(v.max(top8[:, :], score[:, t, 0:nk]))
                settle(v.match_replace(score[:, t, 0:nk], top8[:, :], score[:, t, 0:nk], TAKEN))

            def select_mask(t):
                nk = (t + 1) * P
                settle(v.tensor_scalar(selected[:, t, 0:nk], score[:, t, 0:nk], TAKEN / 2, MASKED, ALU.is_gt, ALU.mult))
                settle(v.tensor_tensor(selected[:, t, 0:nk], selected[:, t, 0:nk], table(C_CAUSAL, t, T)[:, 0:nk], ALU.add))

            conv_turn = [0]

            def conv_taps(n):
                for _ in range(n):
                    tap, c = divmod(conv_turn[0], CC)
                    if tap == TAPS:
                        return
                    conv_turn[0] += 1
                    w = params[:, G_TAP + c * TAPS + tap:G_TAP + c * TAPS + tap + 1]
                    shifted = conv_in[:, c, tap:tap + T]
                    if tap == 0:
                        ins = v.tensor_scalar(conv_a[:, c, :], shifted, w, params[:, G_CONV + c:G_CONV + c + 1], ALU.mult, ALU.add)
                    else:
                        dve.wait_ge(dve_step, steps[0] - CC + 1)
                        ins = v.scalar_tensor_tensor(conv_a[:, c, :], shifted, w, conv_a[:, c, :], ALU.mult, ALU.add)
                    steps[0] += 1
                    ins.then_inc(dve_step, 1)

            def attention(kind, index, bias):
                todo = units(kind)
                for s in range(len(todo)):
                    _, t, j = todo[s]
                    nk = nkeys(kind, t) * P
                    name = ("scores",) + todo[s]
                    bank = ps.full(dve, name)
                    pair = negmax[:, index, t, pair_of(j)[0]:pair_of(j)[1] + 1:2]
                    if kind == "G":
                        settle(v.tensor_reduce(pair, bank[:, 0:2 * nk].rearrange("p (h n) -> p h n", h=2), AX_X, ALU.max))
                        v.tensor_scalar(pair, pair, -SCALE, None, ALU.mult).then_inc(max_done, 1)
                    else:
                        scaled = S_sb[:, s % 2, 0:2 * nk].rearrange("p (h n) -> p h n", h=2)
                        if s >= 2:
                            dve.wait_ge(exp_done, 8 * index + s - 1)
                        elif index:
                            dve.wait_ge(exp_done, 8 * index)
                        ps.empty(v.scalar_tensor_tensor(scaled, bank[:, 0:2 * nk].rearrange("p (h n) -> p h n", h=2), SCALE,
                                                        row(bias(t)[:, 0:nk], 2, nk), ALU.mult, ALU.add), name)
                        ps.copied(dve, name)
                        v.tensor_reduce(pair, scaled, AX_X, ALU.max, negate=True).then_inc(max_done, 1)
                    if kind == "A":
                        for _ in range(2):
                            select_round(s // 4)
                        if s % 4 == 3:
                            select_mask(s // 4)
                    if kind == "G":
                        dve.wait_ge(exp_done, 8 * index + s + 1)
                        ps.empty(v.memset(flag[:, :], 0.0), name)
                        ps.copied(dve, name)
                        conv_taps(18)
                    if s == 6:
                        normalise(kind, index, 0)
                normalise(kind, index, 1)

            def normalise(kind, index, t):
                dve.wait_ge(exp_done, 8 * index + 4 * t + 4)
                settle(v.reciprocal(rden[:, index, t, :], den[:, index, t, :]))
                dve.wait_ge(pv_done, 8 * index + 4 * t + 4)
                if index or t:
                    before = ("y", kind, 0) if t else ("y", "ABG"[index - 1], 1)
                    ps.full(dve, before)
                v.tensor_tensor(y_tok[:, :].rearrange("p (h n) -> p h n", h=NH), y_bank[:, :].rearrange("p (h n) -> p h n", h=NH),
                                each(rden[:, index, t, :], NH, HD), ALU.mult).then_inc(y_emptied, 1)

            attention("A", 0, lambda t: table(C_LOGC, t, T))
            attention("B", 1, lambda t: selected[:, t, :])

            for c in range(KD):
                bank = ps.full(dve, ("up", c))
                dve.wait_ge(gate_done, c // 4 + 1)
                t2 = tmp[:, c % 2, :].rearrange("p (g t) -> p g t", g=2)
                ps.empty(v.tensor_tensor(t2, bank[:, :].rearrange("p (g t) -> p g t", g=2),
                                         gates.rearrange("p (g c) t -> p g c t", g=2)[:, :, c, :], ALU.mult), ("up", c))
                ps.copied(dve, ("up", c))
                v.tensor_tensor(merged[:, c, :], t2[:, 0, :], t2[:, 1, :], ALU.add).then_inc(merged_done, 1)
                dve.wait_ge(merged_done, c + 1)
            residual(0, "out")
            norm(1)
            for j in range(KF // 2):
                bank = ps.full(dve, ("ffu", j))
                ps.copied(dve, ("ffg", j))
                part = ff[:, 2 * j:2 * j + 2, :]
                ps.empty(v.tensor_tensor(part, part, bank[:, :].rearrange("p (c t) -> p c t", c=2), ALU.mult), ("ffu", j))
            residual(1, "down")
            dve.wait_ge(norm_final_done, 16)
            for t in range(TT):
                norm_scale(2, t)
                v.scalar_tensor_tensor(X[:, t, :], X[:, t, :], column(rstd, TT * 2 + t), gain2[:, :], ALU.mult,
                                       ALU.mult).then_inc(residual_done, 1)
                dve.wait_ge(residual_done, TT * 2 + t + 1)
            norm(2)

            def head_norm(n, bank, heads):
                b = n % 2
                dve.wait_ge(head_sq_done, n + 1)
                settle(v.tensor_reduce(head_ss[:, b, 0:heads], relu[:, b, 0:heads * HD].rearrange("p (h w) -> p h w", w=HD), AX_X, ALU.add))
                v.tensor_scalar(head_var[:, b, 0:heads], head_ss[:, b, 0:heads], 1.0 / HD, EPS, ALU.mult, ALU.add).then_inc(head_var_done, 1)
                dve.wait_ge(head_root_done, n + 1)
                settle(v.reciprocal(head_rstd[:, b, 0:heads], head_root[:, b, 0:heads]))
                ins = v.tensor_tensor(tmp[:, 0, 0:heads * HD].rearrange("p (h w) -> p h w", w=HD),
                                      bank[:, 0:heads * HD].rearrange("p (h w) -> p h w", w=HD),
                                      each(head_rstd[:, b, 0:heads], heads, HD), ALU.mult)
                return ins

            def axial(t, heads, w, a, b):
                z = tmp[:, 0, 0:heads * HD]
                v.tensor_tensor(a.rearrange("p (h w) -> p h w", w=HD), z.rearrange("p (h w) -> p h w", w=HD),
                                row(turn_tab[:, t, 2 * w, :], heads, HD), ALU.mult)
                for g in range(2):
                    five = lambda ap: ap.rearrange("p (h g s w) -> p h g s w", g=2, s=2, w=HD // 4)[:, :, g]
                    sine = turn_tab[:, t, 2 * w + 1, :].rearrange("p (g s w) -> p g s w", g=2, s=2)[:, g]
                    ins = v.tensor_tensor(five(b), five(z)[:, :, ::-1, :], sine.unsqueeze(1).broadcast_to([P, heads, 2, HD // 4]), ALU.mult)
                settle(ins)

            settle(v.memset(conv_in[:, :, 0:PAD], 0.0))
            settle(v.memset(conv_in[:, :, PAD + T:], 0.0))
            for t in range(TT):
                bank = ps.full(dve, ("kv2", t))
                dve.wait_ge(head_sq_done, t + 1)
                v.tensor_copy(v2[:, t, :], bank[:, 2 * HD:4 * HD])
                ins = head_norm(t, bank, 2)
                ps.empty(ins, ("kv2", t))
                ps.copied(dve, ("kv2", t))
                a, b = tmp[:, 1, 0:P], tmp[:, 1, P:2 * P]
                axial(t, 2, 1, a, b)
                pair = lambda ap: ap.rearrange("p (h w) -> p h w", h=2).unsqueeze(2).broadcast_to([P, 2, 2, HD])
                v.tensor_tensor(rotated[:, 0, t, 0:2 * P].rearrange("p (h s w) -> p h s w", h=2, s=2), pair(a), pair(b),
                                ALU.add).then_inc(rotated_done, 1)
                rotated_count[0] += 1
                dve.wait_ge(rotated_done, rotated_count[0])
            for t in range(TT):
                bank = ps.full(dve, ("q2", t))
                ins = head_norm(TT + t, bank, NH)
                ps.empty(ins, ("q2", t))
                ps.copied(dve, ("q2", t))
                axial(t, NH, 0, rotated[:, 1, t, :], tmp[:, 1, :])
                v.tensor_tensor(rotated[:, 1, t, :], rotated[:, 1, t, :], tmp[:, 1, :], ALU.add).then_inc(rotated_done, 1)
                rotated_count[0] += 1
                dve.wait_ge(rotated_done, rotated_count[0])
            for c in range(CC):
                bank = ps.full(dve, ("conv", c))
                dve.wait_ge(conv_sig, c + 1)
                ps.empty(v.tensor_tensor(conv_in[:, c, PAD:PAD + T], bank[:, 0:T], conv_b[:, c, :], ALU.mult), ("conv", c))
            for c in range(CC):
                ps.copied(dve, ("conv", c))
            attention("G", 2, None)
            conv_taps(CC * TAPS)
            dve.wait_ge(dve_step, steps[0])
            settle(v.memset(flag[:, :], 0.0))
            v.memset(flag[:, :], 0.0).then_inc(conv_done, 1)
            bank = ps.full(dve, ("mean",))
            ps.empty(v.tensor_tensor(conv_a[:, :, :], conv_a[:, :, :], row(bank[:, 0:T], CC, T), ALU.subtract), ("mean",))
            ps.copied(dve, ("mean",))
            v.memset(flag[:, :], 0.0).then_inc(center_done, 1)
            bank = ps.full(dve, ("var",))
            ps.empty(v.tensor_scalar(rstd_c[:, 0, :], bank[:, 0:T], EPS, None, ALU.add), ("var",))
            ps.copied(dve, ("var",))
            v.memset(flag[:, :], 0.0).then_inc(lvar_done, 1)
            dve.wait_ge(lroot_done, 1)
            settle(v.reciprocal(rstd_c[:, 0, :], rstd_c[:, 1, :]))
            v.tensor_tensor(conv_a[:, :, :], conv_a[:, :, :], row(rstd_c[:, 0, :], CC, T), ALU.mult).then_inc(lnorm_done, 1)
            residual(3, "out2")
            norm(3)
            dve.wait_ge(gain2_done, 16)
            for t in range(TT):
                ins = v.tensor_tensor(hn[:, t, :], xs[:, t, :], gain2[:, :], ALU.mult)
            ins.then_inc(u_free, 4)
            dve.wait_ge(u_free, 4)

            def best(values, top, left):
                settle(v.max(top[:, 0:8], values))
                settle(v.match_replace(left, top[:, 0:8], values, TAKEN))
                settle(v.max(top[:, 8:16], left))

            def find(values, left, top, index):
                settle(v.max_index(index[:, 0:8], top[:, 0:8], values))
                settle(v.max_index(index[:, 8:16], top[:, 8:16], left))

            def choose(g, b):
                dve.wait_ge(match_done, g + 1)
                both = match.rearrange("p g n -> p (g n)")[:, bass.ds(g * 2 * NKEY, 2 * NKEY)]
                settle(v.tensor_copy(s_work[:, 0, :, :].rearrange("p w n -> p (w n)"), both))
                for w in range(2):
                    best(s_work[:, 0, w, :], s_top[:, w, :], s_work[:, 1, w, :])
                    find(s_work[:, 0, w, :], s_work[:, 1, w, :], s_top[:, w, :], s_idx[:, w, :])
                square = lambda ap: ap.rearrange("p (a b) -> p a b", a=ETOP)
                settle(v.tensor_tensor(square(cand[:, 0, :]), each(s_top[:, 0, :], ETOP, ETOP), row(s_top[:, 1, :], ETOP, ETOP), ALU.add))
                best(cand[:, 0, :], c_top[:, b, :], cand[:, 1, :])
                find(cand[:, 0, :], cand[:, 1, :], c_top[:, b, :], c_pos[:, :])
                settle(v.tensor_scalar(c_digit[:, 0, :], c_pos[:, :], 4, None, ALU.logical_shift_right))
                settle(v.tensor_scalar(c_digit[:, 1, :], c_pos[:, :], 15, None, ALU.bitwise_and))
                for w in range(2):
                    hot = square(cand[:, 0, :])
                    settle(v.tensor_tensor(hot, each(c_digit[:, w, :], ETOP, ETOP), row(iota, ETOP, ETOP), ALU.is_equal))
                    settle(v.tensor_tensor(hot, hot, row(s_idx[:, w, :], ETOP, ETOP), ALU.mult))
                    settle(v.tensor_reduce(c_part[:, w, :], hot, AX_X, ALU.add))
                settle(v.tensor_scalar(c_neg[:, b, :], c_top[:, b, 0:1], -1.0, None, ALU.mult))
                v.scalar_tensor_tensor(expert[:, b, :], c_part[:, 0, :], float(NKEY), c_part[:, 1, :], ALU.mult,
                                       ALU.add).then_inc(experts_ready, 1)
                dve.wait_ge(experts_ready, g + 1)

            def group(g, b, t, more):
                for batch in range(4):
                    dve.wait_ge(u_in[batch], (g + 1) * 64)
                    for i in range(4 * batch, 4 * batch + 4):
                        ins = v.tensor_tensor_reduce(out=u_rows[i], in0=u_rows[i], in1=hn[:, t, :], scale=1.0, scalar=0.0,
                                                     op0=ALU.mult, op1=ALU.add, accum_out=dots[:, i:i + 1])
                    ins.then_inc(u_free, 1)
                dve.wait_ge(cexp_done, g + 1)
                settle(v.reciprocal(c_rs[:, b, :], c_sum[:, b, :]))
                dve.wait_ge(gelu_done, g + 1)
                if not (isinstance(g, int) and g == 0):
                    dve.wait_ge(diag_done, g * 4)
                v.scalar_tensor_tensor(mixw[:, :], c_exp[:, b, :], c_rs[:, b, :], gelu[:, :], ALU.mult,
                                       ALU.mult).then_inc(mixw_done, 1)
                if more:
                    if not (isinstance(g, int) and g == 0):
                        for batch in range(4):
                            dve.wait_ge(v_in[batch], g * 64)
                    choose(g + 1, 1 - b)

            choose(0, 0)
            group(0, 0, 0, True)
            group(1, 1, 0, True)
            for t in range(TT):
                dve.reg_mov(loop_step, steps[0] + 1)
                in_loop[0], before = True, steps[0]
                first, end = ((2, NH), (NH, TT * NH - 2))[t]
                with dve.Fori(first, end, 2) as g0:
                    for b in range(2):
                        group(g0 + b, b, t, True)
                in_loop[0] = False
                steps[0] = before + (steps[0] - before) * (end - first) // 2
            group(TT * NH - 2, 0, 1, True)
            group(TT * NH - 1, 1, 1, False)

            dve.wait_ge(final_done, 16)
            for t in range(TT):
                dve.wait_ge(v_free, 4 + 4 * NH * (t + 1))
                for half in range(2):
                    settle(v.tensor_copy(X[:, t, half * 512:(half + 1) * 512], ps.bank(("mix", t, half))[:, :]))
                v.memset(flag[:, :], 0.0).then_inc(residual_done, 1)
                norm_scale(5, t)
                v.scalar_tensor_tensor(X[:, t, :], X[:, t, :], column(rstd, TT * 5 + t), final_gain, ALU.mult,
                                       ALU.mult).then_inc(fout_done, 1)

        @block.gpsimd
        def _(pool):
            group_count = pool.alloc_register("group_count")
            u_count = pool.alloc_register("u_count")
            v_count = pool.alloc_register("v_count")
            for reg in (group_count, u_count, v_count):
                pool.reg_mov(reg, 1)
            with pool.Fori(0, TT * NH, 2) as g0:
                for b in range(2):
                    pool.wait_ge(experts_ready, group_count)
                    pool.reg_add(group_count, group_count, 1)
                    for table_in, rows, free, count, arrived in ((peer_u, u_rows, u_free, u_count, u_in),
                                                                 (peer_v, v_rows, v_free, v_count, v_in)):
                        for batch in range(4):
                            pool.wait_ge(free, count)
                            pool.reg_add(count, count, 1)
                            for i in range(4 * batch, 4 * batch + 4):
                                nc.gpsimd.indirect_dma_start(
                                    rows[i], None, table_in,
                                    bass.IndirectOffsetOnAxis(ap=expert[:, b, i:i + 1], axis=0)).then_inc(arrived[batch], 16)


def _blocks(w, n):
    k = w.shape[0] // P
    return [w[:, i:i + n].reshape(k, P, n).transpose(1, 0, 2).reshape(P, k * n) for i in range(0, w.shape[1], n)]


def kernel(**inputs):
    import concourse.bacc as _bacc
    from concourse.bass_utils import run_bass_kernel_spmd as _run

    a = {k: np.asarray(x) for k, x in inputs.items()}
    w_in, w_in2 = a["w_in"][0], a["w_in_2"]
    ofs = np.cumsum([0, 512, 512, 512, 512, HD, HD, 512, HD, NH, D, D])
    qa, ka, va, qb, kb, vb, qi, ki, wi, ga, gb = [w_in[:, ofs[i]:ofs[i + 1]] for i in range(11)]
    slots = {"qi": _blocks(qi, 512)[0], "qb": _blocks(qb, 512)[0], "qa": _blocks(qa, 512)[0],
             "ka": _blocks(ka, 512)[0], "va": _blocks(va, 512)[0],
             "upa": _blocks(a["w_up_a"][0], D)[0], "upb": _blocks(a["w_up_b"][0], D)[0]}
    for name, w in (("ga", ga), ("gb", gb), ("wo", a["w_out"][0]), ("wp", a["w_out_2"]), ("wq", a["peer_wq_2"])):
        for i, blk in enumerate(_blocks(w, 512)):
            slots[f"{name}{i}"] = blk
    gate, up = a["w_gate"][0], a["w_up"][0]
    for j in range(KF // 2):
        c = slice(2 * P * j, 2 * P * (j + 1))
        slots[f"ff{j}"] = _blocks(np.concatenate([gate[:, c], up[:, c]], 1), 512)[0]
    down = a["w_down"][0].reshape(KF, P, D)
    for j in range(5):
        slots[f"dn{j}"] = down[4 * j:4 * j + 4].transpose(1, 0, 2).reshape(P, SLOT)
    slots["dn5"] = np.concatenate([down[20:22].transpose(1, 0, 2).reshape(P, 2 * D), _blocks(w_in2[:, 512:768], T)[0]], 1)
    slots["q2"], slots["ca"], slots["cg"] = (_blocks(w_in2[:, c:c + 512], 512)[0] for c in (0, 768, 1280))
    stream = np.stack([slots[n] for n in WEIGHTS])
    small = _blocks(np.concatenate([kb, vb, ki, wi], 1), SMALL)[0]
    cols = lambda x: x.reshape(-1, P).T
    params = np.concatenate(
        [cols(a["norm_mix"]), cols(a["norm_ffn"]), cols(a["norm1_g_2"]), cols(a["norm2_g_2"]),
         np.broadcast_to(a["q_norm_g_2"], (P, HD)), np.broadcast_to(a["k_norm_g_2"], (P, HD)),
         a["conv_dw_2"][:, 0, :].T.reshape(CC, P, TAPS).transpose(1, 0, 2).reshape(P, CC * TAPS),
         cols(a["conv_b_2"]), cols(a["conv_ln_g_2"]), cols(a["conv_ln_b_2"]),
         a["peer_keys_2"].transpose(2, 0, 1).reshape(P, 2 * NKEY)], 1)
    arrays = {"x_in": a["x"].reshape(T, D), "stream": stream, "w_small": small, "consts_in": constants(), "params_in": params,
              "norm_final": np.broadcast_to(a["norm_final"], (P, D)),
              "norm2_g": np.broadcast_to(a["norm2_g_2"], (P, D)), "final_g": np.broadcast_to(a["final_g_2"], (P, D)),
              "peer_u": a["peer_u_2"], "peer_v": a["peer_v_2"]}
    nc = _bacc.Bacc("TRN2", target_bir_lowering=False, num_devices=1)
    args, sent = [], {}
    for name, x in arrays.items():
        sent[f"{name}_dram"] = np.ascontiguousarray(x)
        args.append(nc.dram_tensor(f"{name}_dram", x.shape, mybir.dt.from_np(x.dtype), kind="ExternalInput").ap())
    args.append(nc.dram_tensor("out_dram", (T, D), F32, kind="ExternalOutput").ap())
    bass_two_blocks_kernel(nc, *args)
    r = _run(nc, [sent], core_ids=[0])
    return r.results[0]["out_dram"].reshape(1, T, D)
```

```python
from contextlib import ExitStack

import numpy as np
import concourse.bass as bass
from concourse import mybir

F32 = mybir.dt.float32
F32R = mybir.dt.float32r
U32 = mybir.dt.uint32
ALU = mybir.AluOpType
ACT = mybir.ActivationFunctionType
AX_X = mybir.AxisListType.X

P = 128
T = 256
TT = T // P
D = 1024
KD = D // P
HD = 64
NH = 8
FF = 2816
KF = FF // P
TOPK = 64
TAPS = 31
PAD = (TAPS - 1) // 2
NKEY = 128
NEXP = NKEY * NKEY
UROWS, VROWS = 8, 4
BATCHES = 8
ROW_STEP = 16 * 2 * BATCHES // (VROWS // 2)
ETOP = 16
NGATE = 2 * KD
CC = 4
EPS = 1e-6
NNORM = 6
TURNED = (0, 1, 3, 4)
SCALE = HD ** -0.5
IDX_SCALE = (HD ** -0.5) * (NH ** -0.5)
MASKED = -1e30
TAKEN = -3e38

GRAIN = 2048
RING = 3
GRANULES = (["qi0", "qi1", "small", "qb0", "qb1", "qa0", "qa1", "ka0", "ka1", "va0", "va1"]
            + [f"gate{f}" for f in range(NGATE // 2)] + [f"up{u}" for u in range(KD // 2)]
            + [f"wo{q}" for q in range(4)]
            + [f"{n}{j}" for j in range(KF // 2) for n in ("ffg", "ffu")] + [f"dn{j}" for j in range(KF // 2)]
            + ["kv", "q20", "q21"] + [f"conv{c}" for c in range(CC)] + [f"wp{q}" for q in range(4)]
            + [f"wq{h}" for h in range(NH)])
NGRAN = len(GRANULES)
LATE = 2
PARTIAL = (["qi0", "qb0", "qa0", "ka0", "va0", "wo0", "wo2"] + [f"dn{j}" for j in range(KF // 2 - 1)]
           + ["q20", "wp0", "wp2"])
READ_BY = {"qi1": ("qi", 1), "small": ("small", 1), "qb1": ("qb", 1), "qa1": ("qa", 1), "ka1": ("ka", 1),
           "va1": ("va", 1), "wo1": ("out", 1, 0), "wo3": ("out", 1, 1), f"dn{KF // 2 - 1}": ("down", 1, 1),
           "kv": ("kv2", 1), "q21": ("q2", 1), "wp1": ("out2", 1, 0), "wp3": ("out2", 1, 1)}
READ_BY |= {f"gate{f}": ("gate", f) for f in range(NGATE // 2)}
READ_BY |= {f"up{u}": ("up", 2 * u + 1) for u in range(KD // 2)}
READ_BY |= {f"{n}{j}": (n, j) for j in range(KF // 2) for n in ("ffg", "ffu")}
READ_BY |= {f"conv{c}": ("conv", c) for c in range(CC)} | {f"wq{h}": ("query", h) for h in range(NH)}
SLAB = 47 * D + 512
SMALL = 3 * HD + NH

C_ID, C_COS, C_SIN, C_ACOS, C_ASIN = 0, 128, 256, 384, 512
C_MEAN, C_IOTA, C_LOGC, C_CAUSAL = 640, 768, 784, 784 + 512
NCONST = 784 + 1024
G_NORM, G_QK, G_TAP, G_CONV, G_KEYS = 0, 32, 160, 160 + CC * TAPS, 160 + CC * TAPS + 3 * CC
NPARAM = G_KEYS + 2 * NKEY


def constants():
    c = np.zeros((P, NCONST), np.float32)
    c[:, C_ID:C_ID + P] = np.eye(P)
    half = HD // 2
    freq = (np.float32(10000.0) ** (-np.arange(half, dtype=np.float32) / np.float32(half))).astype(np.float32)
    quarter = HD // 4
    afreq = (np.float32(10000.0) ** (-np.arange(quarter, dtype=np.float32) / np.float32(quarter))).astype(np.float32)
    for t in range(TT):
        pos = np.arange(t * P, (t + 1) * P)
        ang = pos.astype(np.float32)[:, None] * freq
        c[:, C_COS + t * HD:C_COS + (t + 1) * HD] = np.concatenate([np.cos(ang)] * 2, 1)
        c[:, C_SIN + t * HD:C_SIN + (t + 1) * HD] = np.concatenate([-np.sin(ang), np.sin(ang)], 1)
        row, col = (pos // 64).astype(np.float32)[:, None] * afreq, (pos % 64).astype(np.float32)[:, None] * afreq
        c[:, C_ACOS + t * HD:C_ACOS + (t + 1) * HD] = np.concatenate(
            [np.cos(row)] * 2 + [np.cos(col)] * 2, 1)
        c[:, C_ASIN + t * HD:C_ASIN + (t + 1) * HD] = np.concatenate(
            [-np.sin(row), np.sin(row), -np.sin(col), np.sin(col)], 1)
        q, k = pos[:, None], np.arange(T)[None, :]
        dist = q - k
        count = ((dist >= 0) & (dist <= P)).astype(np.int64)
        for dilation in (4, 16):
            count += (dist >= 0) & (dist % dilation == 0)
        c[:, C_LOGC + t * T:C_LOGC + (t + 1) * T] = np.where(count > 0, np.log(np.maximum(count, 1)), MASKED)
        c[:, C_CAUSAL + t * T:C_CAUSAL + (t + 1) * T] = np.where(dist >= 0, 0.0, MASKED)
    c[:, C_MEAN:C_MEAN + P] = 1.0 / (CC * P)
    c[:, C_IOTA:C_IOTA + 16] = np.arange(16)
    return c


def slab_base(nc, slab):
    return nc.sbuf_base - SLAB * 4


class Psum:

    POOLS = {"D": (0, 1, 2), "S": (3, 4), "T": (5, 6)}

    def __init__(self, banks, filled, emptied):
        self.banks, self.filled, self.emptied = banks, filled, emptied
        self.at, self.order, self.uses, self.turn = {}, [], [0] * 8, dict.fromkeys(self.POOLS, 0)
        self.started = 0

    def plan(self, pool, name, bank=None):
        if bank is None:
            bank = self.POOLS[pool][self.turn[pool] % len(self.POOLS[pool])]
            self.turn[pool] += 1
        self.at[name] = (bank, self.uses[bank])
        self.order.append(name)
        self.uses[bank] += 1

    def bank(self, name):
        return self.banks[self.at[name][0]]

    def start(self, pe, name, freed=None):
        assert self.order[self.started] == name, (self.order[self.started], name)
        self.started += 1
        b, n = self.at[name]
        if freed:
            pe.wait_ge(*freed)
        elif n:
            pe.wait_ge(self.emptied[b], n)
        return self.banks[b]

    def fill(self, ins, name):
        ins.then_inc(self.filled[self.at[name][0]], 1)

    def full(self, eng, name):
        b, n = self.at[name]
        eng.wait_ge(self.filled[b], n + 1)
        return self.banks[b]

    def empty(self, ins, name):
        ins.then_inc(self.emptied[self.at[name][0]], 1)

    def copied(self, eng, name):
        b, n = self.at[name]
        eng.wait_ge(self.emptied[b], n + 1)


def units(kind):
    return [(kind, t, j) for t in range(TT) for j in range(NH // 2)]


def pair_of(j):
    h = 4 * (j // 2) + j % 2
    return (h, h + 2)


IDX_UNITS = [(0, (0, 2, 4, 6)), (0, (1, 3, 5, 7))] + [(1, pair_of(j)) for j in range(NH // 2)]


def nkeys(kind, t):
    return TT if kind == "G" else t + 1


def plan_psum(ps):
    def norm(i):
        for t in range(TT):
            for half in range(2):
                ps.plan("ST"[half], ("norm", i, t, half))

    def attention(kind, extra):
        for s in range(len(units(kind)) + 2):
            if s < 8:
                ps.plan("S", ("scores",) + units(kind)[s])
            for name in extra.get(s, []):
                ps.plan("D", name)
            if 1 <= s < 9:
                ps.plan("T", ("probs",) + units(kind)[s - 1])
            if s == 7:
                ps.plan("T", ("y", kind, 0))
        ps.plan("T", ("y", kind, 1))

    norm(0)
    for block in ("qi", "small", "qb"):
        for t in range(TT):
            ps.plan("D", (block, t))
    for t in range(TT):
        ps.plan("T", ("turn", "qi", t))
    ps.plan("T", ("turn", "k"))
    for t in range(TT):
        ps.plan("D", ("qa", t))
    for t in range(TT):
        ps.plan("T", ("turn", "qb", t))
    for n in range(3):
        ps.plan("S", ("index", n))
    for t in range(TT):
        ps.plan("D", ("ka", t))
    for n in range(3, 6):
        ps.plan("S", ("index", n))
    for t in range(TT):
        ps.plan("T", ("turn", "qa", t))
    for t in range(TT):
        ps.plan("D", ("va", t))
    for t in range(TT):
        ps.plan("T", ("turn", "ka", t))
    attention("A", {s: [("gate", s // 2)] for s in (0, 2, 4, 6)})
    attention("B", {s: [("gate", 4 + s // 2)] for s in (0, 2, 4, 6)})
    for c in range(KD):
        ps.plan("D", ("up", c))
    for half in range(2):
        for t in range(TT):
            ps.plan("D", ("out", t, half))
    norm(1)
    for j in range(KF // 2):
        ps.plan("D", ("ffg", j))
        ps.plan("D", ("ffu", j))
    for t in range(TT):
        for half in range(2):
            n = t * 2 + half
            ps.plan(None, ("down", t, half), bank=(0, 1, 2, 3)[n])
    norm(2)
    for t in range(TT):
        ps.plan("D", ("kv2", t))
    for t in range(TT):
        ps.plan("D", ("q2", t))
    for c in range(CC):
        ps.plan("D", ("conv", c))
    ps.plan("T", ("turn", "k2"))
    for t in range(TT):
        ps.plan("T", ("turn", "q2", t))
    attention("G", {})
    ps.plan("D", ("mean",))
    ps.plan("D", ("var",))
    for half in range(2):
        for t in range(TT):
            ps.plan("D", ("out2", t, half))
    norm(3)
    for h in range(NH):
        ps.plan("D", ("query", h))
        if h:
            ps.plan("S", ("match", h - 1))
    ps.plan("S", ("match", NH - 1))
    for t in range(TT):
        for half in range(2):
            ps.plan(None, ("mix", t, half), bank=(0, 1, 2, 5)[t * 2 + half])


def bass_two_blocks_kernel(nc, x_in, stream, consts_in, params_in, norm_final, norm2_g, final_g,
                           peer_u, peer_v, out):
    with ExitStack() as ctx:
        def sb(name, shape, dt=F32):
            return ctx.enter_context(nc.sbuf_tensor(name, shape, dt))

        def sem(name):
            return ctx.enter_context(nc.semaphore(name))

        slab = sb("slab", [P, SLAB])
        base = slab_base(nc, slab)

        def at(name, col, shape, dt=F32):
            assert col + int(np.prod(shape[1:])) <= SLAB, name
            return nc.alloc_sbuf_tensor_at(name, shape, dt, offset=base + 4 * col)

        raw = [at(f"raw{r}", r * GRAIN, [P, GRAIN]) for r in range(RING)]
        w_hi = [at(f"w_hi{r}", (RING + r) * GRAIN, [P, GRAIN], F32R) for r in range(RING)]
        w_lo = [at(f"w_lo{r}", (2 * RING + r) * GRAIN, [P, GRAIN], F32R) for r in range(RING)]
        m0 = 3 * RING * GRAIN
        gates = at("gates", m0, [P, NGATE, T])
        q0 = m0 + NGATE * T
        qT = {n: at(f"qT_{n}", q0 + i * D, [P, 4, T]) for i, n in enumerate(("qi", "qb", "qa", "ka"))}
        qT["q2"] = qT["qi"]
        kT = at("kT", q0 + 4 * D, [P, 2, T])
        va = at("va", q0 + 4 * D + 512, [P, TT, 512])
        r0 = q0 + 4 * D + 512 + D
        rotated = at("rotated", r0, [P, 2, TT, 512])
        yT_lo = at("yT_lo", r0, [P, KD, T], F32R)
        vb = at("vb", r0 + 2048, [P, TT, HD])
        v2 = at("v2", r0 + 2048 + 128, [P, TT, 2 * HD])
        conv_in = at("conv_in", m0, [P, CC, T + 2 * PAD])
        conv_a = at("conv_a", m0 + 1144, [P, CC, T])
        conv_b = at("conv_b", m0 + 1144 + D, [P, CC, T])
        rstd_c = at("rstd_c", m0 + 1144 + 2 * D, [P, 2, T])
        ff_hi = at("ff_hi", m0, [P, KF, T], F32R)
        u_rows = [at(f"u_row{i}", m0 + i * D, [P, D]) for i in range(UROWS)]
        v_rows = [at(f"v_row{i}", m0 + (UROWS + i) * D, [P, D]) for i in range(VROWS)]
        x0 = m0 + (UROWS + VROWS) * D
        assert r0 + 2048 + 128 + 256 <= x0
        X = at("residual", x0, [P, TT, D])
        xs = at("normed_tokens", x0 + 2 * D, [P, TT, D])
        merged_hi = at("merged_hi", x0 + 2 * D, [P, KD, T], F32R)
        diag = at("diag", x0 + 2 * D, [P, ETOP, P])
        hT_hi = at("hT_hi", x0 + 4 * D, [P, KD, T], F32R)
        hT_lo = at("hT_lo", x0 + 6 * D, [P, KD, T], F32R)
        yT_hi = at("yT_hi", x0 + 8 * D, [P, KD, T], F32R)
        hn = at("hn", x0 + 8 * D, [P, TT, D])
        w0 = x0 + 10 * D
        S_sb = at("S_sb", w0, [P, 2, 512])
        E_sb = at("E_sb", w0 + D, [P, 2, 512])
        PT = at("PT", w0 + 2 * D, [P, 2, 512])
        merged_lo = at("merged_lo", w0, [P, KD, T], F32R)
        relu = at("relu", w0 + 3 * D, [P, 2, 512])
        score = at("score", w0 + 4 * D, [P, TT, T])
        selected = at("selected", w0 + 4 * D + 512, [P, TT, T])
        y_tok = at("y_tok", w0 + 5 * D, [P, 512])
        ff_lo = at("ff_lo", w0, [P, KF, T], F32R)
        match = at("match", w0, [P, TT * NH, 2 * NKEY])
        query = at("query", w0 + 4 * D, [P, 2, 2, T])
        assert w0 + 5 * D + 512 + 2 * D <= SLAB
        full = at("full", w0 + 5 * D + 512, [P, 4, 512])
        consts = sb("consts", [P, NCONST])
        params = sb("params", [P, NPARAM])
        gain2 = sb("gain2", [P, D])
        tmp = gain2[:, :].rearrange("p (b n) -> p b n", b=2)
        s_work = gain2[:, 0:4 * NKEY].rearrange("p (s w n) -> p s w n", s=2, w=2)
        cand = gain2[:, 4 * NKEY:4 * NKEY + 512].rearrange("p (s n) -> p s n", s=2)

        sumsq = sb("sumsq", [P, 2 * NNORM])
        var = sb("var", [P, 2 * NNORM])
        root = sb("root", [P, 2 * NNORM])
        rstd = sb("rstd", [P, 2 * NNORM])
        flag = sb("flag", [P, 1])
        wi = sb("wi", [P, TT, NH])
        top8 = sb("top8", [P, 8])
        negmax = sb("negmax", [P, 3, TT, NH])
        den = sb("den", [P, 3, TT, NH])
        rden = sb("rden", [P, 3, TT, NH])
        head_ss = sb("head_ss", [P, 2, NH])
        head_var = sb("head_var", [P, 2, NH])
        head_root = sb("head_root", [P, 2, NH])
        head_rstd = sb("head_rstd", [P, 2, NH])
        turn_tab = sb("turn_tab", [P, TT, 4, HD])
        s_top = sb("s_top", [P, 2, ETOP])
        s_idx = sb("s_idx", [P, 2, ETOP], U32)
        c_top = sb("c_top", [P, 3, ETOP])
        c_pos = sb("c_pos", [P, ETOP], U32)
        c_digit = sb("c_digit", [P, 2, ETOP], U32)
        c_part = sb("c_part", [P, 2, ETOP])
        expert = sb("expert", [P, 3, ETOP], U32)
        c_neg = sb("c_neg", [P, 3, 1])
        c_exp = sb("c_exp", [P, 3, ETOP])
        c_sum = sb("c_sum", [P, 3, 1])
        c_rs = sb("c_rs", [P, 3, 1])
        dots = sb("dots", [P, ETOP])
        gelu = sb("gelu", [P, ETOP])
        mixw = sb("mixw", [P, ETOP])

        ident = consts[:, C_ID:C_ID + P]
        mean_w = consts[:, C_MEAN:C_MEAN + P]
        iota = consts[:, C_IOTA:C_IOTA + 16]
        final_gain = consts[:, C_LOGC:C_LOGC + D]
        keysT = params[:, G_KEYS:G_KEYS + 2 * NKEY].rearrange("p (w n) -> p w n", w=2)

        def table(at, t, n=HD):
            return consts[:, at + t * n:at + (t + 1) * n]

        filled = [sem(f"filled_bank{b}") for b in range(7)]
        emptied = [sem(f"emptied_bank{b}") for b in range(7)]
        banks = [ctx.enter_context(nc.psum_tensor(f"bank{b}", [P, 512], F32)) for b in range(8)]
        y_bank = banks[7]
        ps = Psum(banks, filled, emptied)
        plan_psum(ps)
        weight_in = [sem(f"weight_in{r}") for r in range(RING)]
        x_in_done = [sem(f"x_in{t}") for t in range(TT)]
        consts_done = sem("consts_in")
        gain2_done = sem("gain2_in")
        norm_final_done = sem("norm_final_in")
        final_done = sem("final_gain_in")
        sumsq_done = sem("sumsq_done")
        var_done = sem("var_done")
        residual_done = sem("residual_done")
        merged_done = sem("merged_done")
        root_done = sem("root_done")
        normed = sem("normed")
        rotated_done = sem("rotated_done")
        relu_used = sem("relu_used")
        max_done = sem("max_done")
        exp_done = sem("exp_done")
        pv_done = sem("pv_done")
        y_emptied = sem("y_emptied")
        gate_done = sem("gate_done")
        part_read = sem("part_read")
        high_done = sem("high_done")
        split_done = sem("split_done")
        late_split_done = sem("late_split_done")
        ht_full = sem("ht_full")
        ht_high = sem("ht_high")
        ht_done = sem("ht_done")
        y_high = sem("y_high")
        ff_full = sem("ff_full")
        ff_high = sem("ff_high")
        ff_done = sem("ff_done")
        act_step = sem("act_step")
        dve_step = sem("dve_step")
        head_sq_done = sem("head_sq_done")
        head_var_done = sem("head_var_done")
        head_root_done = sem("head_root_done")
        conv_sig = sem("conv_sig")
        conv_done = sem("conv_done")
        center_done = sem("center_done")
        square_done = sem("square_done")
        lvar_done = sem("lvar_done")
        lroot_done = sem("lroot_done")
        lnorm_done = sem("lnorm_done")
        conv_high = sem("conv_high")
        conv_out = sem("conv_out")
        match_done = sem("match_done")
        u_free = sem("u_batches_free")
        v_free = sem("v_batches_free")
        u_in = [sem(f"u_in{b}") for b in range(UROWS // 2)]
        v_in = [sem(f"v_in{b}") for b in range(VROWS // 2)]
        experts_ready = sem("experts_ready")
        cexp_done = sem("cexp_done")
        gelu_done = sem("gelu_done")
        mixw_done = sem("mixw_done")
        diag_done = sem("diag_done")
        fout_done = sem("fout_done")
        out_done = sem("out_done")

        def was_read(eng, n):
            name = GRANULES[n]
            if name in READ_BY:
                ps.full(eng, READ_BY[name])
            else:
                eng.wait_ge(part_read, PARTIAL.index(name) + 1)

        block = ctx.enter_context(nc.Block())

        @block.sync
        def _(sp):
            for t in range(TT):
                sp.dma_start(X[:, t, :], x_in[t * P:(t + 1) * P, :]).then_inc(x_in_done[t], 16)
            sp.dma_start(consts[:, :], consts_in).then_inc(consts_done, 16)
            sp.dma_start(params[:, :], params_in).then_inc(consts_done, 16)
            for n in range(RING):
                sp.dma_start(raw[n][:, :], stream[n]).then_inc(weight_in[n], 16)
            rounds = NGRAN // RING
            with sp.Fori(1, rounds, 1) as q:
                for r in range(RING):
                    sp.wait_ge(split_done, q * RING + (r - RING + 1))
                    sp.dma_start(raw[r][:, :], stream[bass.ds(q * RING + r, 1), :, :].rearrange("g p n -> (g p) n")).then_inc(weight_in[r], 16)
            for n in range(rounds * RING, NGRAN):
                sp.wait_ge(split_done, n - RING + 1)
                sp.dma_start(raw[n % RING][:, :], stream[n]).then_inc(weight_in[n % RING], 16)
            for t in range(TT):
                sp.wait_ge(fout_done, t + 1)
                sp.dma_start(out[t * P:(t + 1) * P, :], X[:, t, :]).then_inc(out_done, 16)
            sp.wait_ge(out_done, 16 * TT)

        @block.tensor
        def _(pe):
            mm = nc.tensor.matmul
            parts_read = [0]

            def mm3(out_ap, left, right, first, last):
                mm(out_ap, left[0], right[0], start=first, stop=False)
                mm(out_ap, left[0], right[1], start=False, stop=False)
                return mm(out_ap, left[1], right[0], start=False, stop=last)

            def granule(name, k):
                n = GRANULES.index(name)
                if n < NGRAN - LATE:
                    pe.wait_ge(split_done, n + 1)
                else:
                    pe.wait_ge(late_split_done, n - (NGRAN - LATE) + 1)
                return [w[n % RING][:, :].rearrange("p (k n) -> p k n", k=k) for w in (w_hi, w_lo)]

            def cut(pair, *index):
                return [x[index] for x in pair]

            def partly_read(name, ins):
                assert PARTIAL[parts_read[0]] == name
                parts_read[0] += 1
                ins.then_inc(part_read, 1)

            hT = (hT_hi, hT_lo)
            yT = (yT_hi, yT_lo)
            everything = slice(None)

            def normed_turn(i):
                for t in range(TT):
                    pe.wait_ge(normed, TT * i + t + 1)
                    for half in range(2):
                        name = ("norm", i, t, half)
                        bank = ps.start(pe, name)
                        for c in range(4):
                            k = 4 * half + c
                            ins = nc.tensor.transpose(bank[:, c * P:(c + 1) * P], xs[:, t, k * P:(k + 1) * P], ident)
                        ps.fill(ins, name)
                pe.wait_ge(ht_done, 4 * (i + 1))

            def tokens(name, granules, source, width=512, tail=()):
                opened = [ps.start(pe, (name, t) + tail) for t in range(TT)]
                n = width // len(granules)
                for i, gname in enumerate(granules):
                    w = [x[:, :, 0:n] for x in granule(gname, KD)] if n == T else small_cols(gname)
                    for t in range(TT):
                        for k in range(KD):
                            ins = mm3(opened[t][:, i * n:(i + 1) * n], cut(source, everything, k, slice(t * P, (t + 1) * P)),
                                      cut(w, everything, k), k == 0, k == KD - 1)
                        if gname in READ_BY:
                            ps.fill(ins, (name, t) + tail)
                    if gname not in READ_BY:
                        partly_read(gname, ins)

            def small_cols(gname):
                n = GRANULES.index(gname)
                granule(gname, KD)
                return [w[n % RING][:, 0:KD * SMALL].rearrange("p (k n) -> p k n", k=KD) for w in (w_hi, w_lo)]

            def channels(bank, c, w, col, source, chunks):
                for i, k in enumerate(chunks):
                    ins = mm3(bank[:, c * T:(c + 1) * T], cut(w, everything, i, slice(col, col + P)),
                              cut(source, everything, k), i == 0, i == len(chunks) - 1)
                return ins

            def turn(source, name, n):
                bank = ps.start(pe, name)
                for c in range(n):
                    ins = nc.tensor.transpose(bank[:, c * P:(c + 1) * P], source(c), ident)
                ps.fill(ins, name)

            def turn_queries(name, b, count):
                for t in range(TT):
                    pe.wait_ge(rotated_done, count + t)
                    turn(lambda c: rotated[:, b, t, c * P:(c + 1) * P], ("turn", name, t), 4)

            pe.wait_ge(consts_done, 32)
            normed_turn(0)
            tokens("qi", ("qi0", "qi1"), hT)
            tokens("small", ("small",), hT, SMALL)
            tokens("qb", ("qb0", "qb1"), hT)
            turn_queries("qi", 0, 1)
            pe.wait_ge(rotated_done, 4)
            turn(lambda c: rotated[:, 1, c % 2, (c // 2) * P:(c // 2 + 1) * P], ("turn", "k"), 4)
            tokens("qa", ("qa0", "qa1"), hT)
            turn_queries("qb", 0, 5)

            def index_unit(n):
                t, heads = IDX_UNITS[n]
                nk = (t + 1) * P
                bank = ps.start(pe, ("index", n))
                for i, h in enumerate(heads):
                    rows = slice(HD * (h % 2), HD * (h % 2) + HD)
                    ins = mm(bank[:, i * nk:(i + 1) * nk], qT["qi"][rows, h // 2, t * P:(t + 1) * P],
                             kT[rows, 0, 0:nk], start=True, stop=True)
                ps.fill(ins, ("index", n))

            for t in range(TT):
                ps.copied(pe, ("turn", "qi", t))
            ps.copied(pe, ("turn", "k"))
            for n in range(3):
                index_unit(n)
            tokens("ka", ("ka0", "ka1"), hT)
            for n in range(3, 6):
                index_unit(n)
            turn_queries("qa", 1, 7)
            tokens("va", ("va0", "va1"), hT)
            turn_queries("ka", 0, 9)

            def gate_fill(f):
                w = granule(f"gate{f}", KD)
                bank = ps.start(pe, ("gate", f))
                for c in range(2):
                    ins = channels(bank, c, w, c * P, hT, range(KD))
                ps.fill(ins, ("gate", f))

            def attention(kind, index, queries, key_of, value_of, beside):
                todo = units(kind)
                for s in range(len(todo) + 2):
                    if s < len(todo):
                        _, t, j = todo[s]
                        nk = nkeys(kind, t) * P
                        bank = ps.start(pe, ("scores",) + todo[s])
                        for i, h in enumerate(pair_of(j)):
                            rows = slice(HD * (h % 2), HD * (h % 2) + HD)
                            ins = mm(bank[:, i * nk:(i + 1) * nk], queries[rows, h // 2, t * P:(t + 1) * P],
                                     key_of(h)[rows, 0:nk], start=True, stop=True)
                        ps.fill(ins, ("scores",) + todo[s])
                    if beside and s % 2 == 0 and s < 8:
                        gate_fill(beside - 1 + s // 2)
                    if 1 <= s < 9:
                        _, t, j = todo[s - 1]
                        nb = nkeys(kind, t)
                        pe.wait_ge(exp_done, 8 * index + s)
                        turn(lambda c: E_sb[:, (s - 1) % 2, c * P:(c + 1) * P], ("probs",) + todo[s - 1], 2 * nb)
                    if s == 7:
                        turn_y(kind, index, 0)
                    if s >= 2:
                        _, t, j = todo[s - 2]
                        nb = nkeys(kind, t)
                        ps.copied(pe, ("probs",) + todo[s - 2])
                        if j == 0 and 2 * index + t:
                            pe.wait_ge(y_emptied, 2 * index + t)
                        for i, h in enumerate(pair_of(j)):
                            for kb in range(nb):
                                ins = mm(y_bank[:, h * HD:(h + 1) * HD], PT[:, (s - 2) % 2, (i * nb + kb) * P:(i * nb + kb + 1) * P],
                                         value_of(kb, h), start=kb == 0, stop=kb == nb - 1)
                        ins.then_inc(pv_done, 1)
                turn_y(kind, index, 1)

            def turn_y(kind, index, t):
                pe.wait_ge(y_emptied, 2 * index + t + 1)
                turn(lambda c: y_tok[:, c * P:(c + 1) * P], ("y", kind, t), 4)

            for name in ("qa", "ka"):
                for t in range(TT):
                    ps.copied(pe, ("turn", name, t))
            for t in range(TT):
                ps.copied(pe, ("va", t))
            attention("A", 0, qT["qa"], lambda h: qT["ka"][:, h // 2, :], lambda kb, h: va[:, kb, h * HD:(h + 1) * HD], 1)
            for t in range(TT):
                ps.copied(pe, ("turn", "qb", t))
            attention("B", 1, qT["qb"], lambda h: kT[:, 1, :], lambda kb, h: vb[:, kb, :], 5)

            for kind in "AB":
                for t in range(TT):
                    ps.copied(pe, ("y", kind, t))
            for c in range(KD):
                w = granule(f"up{c // 2}", KD)
                bank = ps.start(pe, ("up", c))
                for i in range(2):
                    part = [x[:, 4 * i:4 * i + 4, :] for x in w]
                    ins = channels(bank, i, part, (c % 2) * P, yT, range(4 * i, 4 * i + 4))
                ps.fill(ins, ("up", c))

            pe.wait_ge(merged_done, KD)
            for half in range(2):
                tokens("out", (f"wo{2 * half}", f"wo{2 * half + 1}"), (merged_hi, merged_lo), tail=(half,))

            normed_turn(1)
            for j in range(KF // 2):
                for name in ("ffg", "ffu"):
                    w = granule(f"{name}{j}", KD)
                    bank = ps.start(pe, (name, j))
                    for c in range(2):
                        ins = channels(bank, c, w, c * P, hT, range(KD))
                    ps.fill(ins, (name, j))
            accs = [[ps.start(pe, ("down", t, half)) for half in range(2)] for t in range(TT)]
            for j in range(KF // 2):
                w = granule(f"dn{j}", 2)
                pe.wait_ge(ff_done, j + 1)
                for t in range(TT):
                    for half in range(2):
                        for i in range(2):
                            k = 2 * j + i
                            ins = mm3(accs[t][half][:, :], cut((ff_hi, ff_lo), everything, k, slice(t * P, (t + 1) * P)),
                                      cut(w, everything, i, slice(half * 512, (half + 1) * 512)), k == 0, k == KF - 1)
                        if j == KF // 2 - 1:
                            ps.fill(ins, ("down", t, half))
                if j < KF // 2 - 1:
                    partly_read(f"dn{j}", ins)

            normed_turn(2)
            tokens("kv2", ("kv",), hT, T)
            tokens("q2", ("q20", "q21"), hT)
            for c in range(CC):
                w = granule(f"conv{c}", KD)
                bank = ps.start(pe, ("conv", c))
                for i in range(2):
                    ins = channels(bank, i, w, i * P, hT, range(KD))
                ps.fill(ins, ("conv", c))
            pe.wait_ge(rotated_done, 12)
            turn(lambda c: rotated[:, 0, c % 2, (c // 2) * P:(c // 2 + 1) * P], ("turn", "k2"), 4)
            turn_queries("q2", 1, 13)
            ps.copied(pe, ("turn", "k2"))
            for t in range(TT):
                ps.copied(pe, ("turn", "q2", t))
            attention("G", 2, qT["q2"], lambda h: kT[:, h // 4, :], lambda kb, h: v2[:, kb, (h // 4) * HD:(h // 4 + 1) * HD], 0)
            pe.wait_ge(conv_done, 1)
            bank = ps.start(pe, ("mean",))
            for c in range(CC):
                ins = mm(bank[:, 0:T], mean_w, conv_a[:, c, :], start=c == 0, stop=c == CC - 1)
            ps.fill(ins, ("mean",))
            pe.wait_ge(square_done, 1)
            bank = ps.start(pe, ("var",))
            for c in range(CC):
                ins = mm(bank[:, 0:T], mean_w, conv_b[:, c, :], start=c == 0, stop=c == CC - 1)
            ps.fill(ins, ("var",))
            for t in range(TT):
                ps.copied(pe, ("y", "G", t))
            pe.wait_ge(conv_out, 1)
            for half in range(2):
                tokens("out2", (f"wp{2 * half}", f"wp{2 * half + 1}"), yT, tail=(half,))

            normed_turn(3)

            def key_scores(h):
                ps.copied(pe, ("query", h))
                bank = ps.start(pe, ("match", h), freed=(match_done, h - 1) if h >= 2 else None)
                for t in range(TT):
                    for i in range(2):
                        at = (2 * t + i) * NKEY
                        ins = mm(bank[:, at:at + NKEY], query[:, h % 2, i, t * P:(t + 1) * P], keysT[:, i, :],
                                 start=True, stop=True)
                ps.fill(ins, ("match", h))

            for h in range(NH):
                w = granule(f"wq{h}", KD)
                bank = ps.start(pe, ("query", h))
                for i in range(2):
                    ins = channels(bank, i, w, i * P, hT, range(KD))
                ps.fill(ins, ("query", h))
                if h:
                    key_scores(h - 1)
            key_scores(NH - 1)

            for t in range(TT):
                accs = [ps.start(pe, ("mix", t, half)) for half in range(2)]
                for half in range(2):
                    mm(accs[half][:, :], ident, X[:, t, half * 512:(half + 1) * 512], start=True, stop=True)
                with pe.Fori(t * NH, (t + 1) * NH, 1) as g:
                    for m in range(BATCHES):
                        slot = m % (VROWS // 2)
                        pe.wait_ge(v_in[slot], g * (BATCHES * 64 // VROWS) + 32 * (m // (VROWS // 2) + 1))
                        if m % 2 == 0:
                            pe.wait_ge(diag_done, g * 4 + (m // 2 + 1))
                        for i in range(2):
                            for half in range(2):
                                ins = mm(accs[half][:, :], diag[:, 2 * m + i, :],
                                         v_rows[2 * slot + i][:, half * 512:(half + 1) * 512],
                                         start=False, stop=True, skip_group_check=True)
                        ins.then_inc(v_free, 1)

        @block.scalar
        def _(act):
            activation = nc.scalar.activation
            steps = [0]

            def settle(ins):
                steps[0] += 1
                ins.then_inc(act_step, 1)
                act.wait_ge(act_step, steps[0])

            def norm_sums(i):
                for t in range(TT):
                    if i == 0:
                        act.wait_ge(x_in_done[t], 16)
                    else:
                        act.wait_ge(residual_done, TT * (i - 1) + t + 1)
                    activation(full[:, 2 * t:2 * t + 2, :].rearrange("p c t -> p (c t)"), X[:, t, :], ACT.Square,
                               accum_out=sumsq[:, TT * i + t:TT * i + t + 1]).then_inc(sumsq_done, 1)
                    act.wait_ge(var_done, TT * i + t + 1)
                    activation(root[:, TT * i + t:TT * i + t + 1], var[:, TT * i + t:TT * i + t + 1],
                               ACT.Sqrt).then_inc(root_done, 1)

            prepared = [0]

            def prepare(name, ahead=RING - 1):
                while prepared[0] <= min(GRANULES.index(name) + ahead, NGRAN - 1):
                    n = prepared[0]
                    act.wait_ge(weight_in[n % RING], 16 * (n // RING + 1))
                    if n >= RING:
                        was_read(act, n - RING)
                    activation(w_hi[n % RING][:, :], raw[n % RING][:, :], ACT.Copy).then_inc(high_done, 1)
                    prepared[0] += 1

            def high_of_norm(i):
                for t in range(TT):
                    for half in range(2):
                        piece = 2 * t + half
                        act.wait_ge(ht_full, 4 * i + piece + 1)
                        activation(hT_hi[:, 4 * half:4 * half + 4, t * P:(t + 1) * P],
                                   full[:, piece, :].rearrange("p (c t) -> p c t", c=4), ACT.Copy).then_inc(ht_high, 1)

            def high_of_y(kind, base, t):
                bank = ps.full(act, ("y", kind, t))
                activation(yT_hi[:, base:base + 4, t * P:(t + 1) * P], bank[:, :].rearrange("p (c t) -> p c t", c=4),
                           ACT.Copy).then_inc(y_high, 1)

            def copy_turned(name, out_ap):
                bank = ps.full(act, name)
                ps.empty(activation(out_ap, bank[:, :].rearrange("p (c t) -> p c t", c=4), ACT.Copy), name)

            def index_relu(n):
                bank = ps.full(act, ("index", n))
                if n >= 2:
                    act.wait_ge(relu_used, n - 1)
                ps.empty(activation(relu[:, n % 2, :], bank[:, :], ACT.Relu), ("index", n))

            def attention(kind, index, base, beside):
                todo = units(kind)
                for s in range(len(todo) + 1):
                    if s < len(todo):
                        _, t, j = todo[s]
                        nk = nkeys(kind, t) * P
                        act.wait_ge(max_done, 8 * index + s + 1)
                        if s >= 2:
                            ps.full(act, ("probs",) + todo[s - 2])
                        for i, h in enumerate(pair_of(j)):
                            source = ps.bank(("scores",) + todo[s]) if kind == "G" else S_sb[:, s % 2, :]
                            ins = activation(E_sb[:, s % 2, i * nk:(i + 1) * nk], source[:, i * nk:(i + 1) * nk], ACT.Exp,
                                             bias=negmax[:, index, t, h:h + 1], scale=SCALE if kind == "G" else 1.0,
                                             accum_out=den[:, index, t, h:h + 1])
                        ins.then_inc(exp_done, 1)
                    if beside and s % 2 == 0 and s < 8:
                        f = beside - 1 + s // 2
                        prepare(f"gate{f}")
                        bank = ps.full(act, ("gate", f))
                        ps.empty(activation(gates[:, 2 * f:2 * f + 2, :], bank[:, :].rearrange("p (c t) -> p c t", c=2),
                                            ACT.Copy), ("gate", f))
                    if s == 8:
                        high_of_y(kind, base, 0)
                    if s >= 1:
                        name = ("probs",) + todo[s - 1]
                        n = 2 * nkeys(kind, todo[s - 1][1]) * P
                        bank = ps.full(act, name)
                        if s >= 3:
                            act.wait_ge(pv_done, 8 * index + s - 2)
                        ps.empty(activation(PT[:, (s - 1) % 2, 0:n], bank[:, 0:n], ACT.Copy), name)
                high_of_y(kind, base, 1)

            act.wait_ge(consts_done, 32)
            norm_sums(0)
            prepare("qi0", 0)
            high_of_norm(0)
            prepare("qb1")
            for t in range(TT):
                copy_turned(("turn", "qi", t), qT["qi"][:, :, t * P:(t + 1) * P])
            name = ("turn", "k")
            ps.empty(activation(kT[:, :, :].rearrange("p w t -> p (w t)"), ps.full(act, name)[:, :], ACT.Copy), name)
            prepare("qa1")
            for t in range(TT):
                copy_turned(("turn", "qb", t), qT["qb"][:, :, t * P:(t + 1) * P])
            for n in range(3):
                index_relu(n)
            prepare("ka1")
            for n in range(3, 6):
                index_relu(n)
            for t in range(TT):
                copy_turned(("turn", "qa", t), qT["qa"][:, :, t * P:(t + 1) * P])
            prepare("va1")
            for t in range(TT):
                bank = ps.full(act, ("va", t))
                ps.empty(activation(va[:, t, :], bank[:, :], ACT.Copy), ("va", t))
            for t in range(TT):
                copy_turned(("turn", "ka", t), qT["ka"][:, :, t * P:(t + 1) * P])
            attention("A", 0, 0, 1)
            attention("B", 1, 4, 5)
            for f in (5, 6, 7):
                ps.copied(act, ("gate", f))
            for half in range(2):
                part = gates[:, :, :].rearrange("p (g c) t -> p g (c t)", g=2)[:, :, half * 4 * T:(half + 1) * 4 * T]
                activation(part, part, ACT.Sigmoid).then_inc(gate_done, 1)
                prepare("gate7", RING)
            prepare("wo3")
            norm_sums(1)
            act.dma_start(gain2[:, :], norm_final).then_inc(norm_final_done, 16)
            high_of_norm(1)

            def high_of_ff(j):
                act.wait_ge(ff_full, j + 1)
                activation(ff_hi[:, 2 * j:2 * j + 2, :], full[:, j % 4, :].rearrange("p (c t) -> p c t", c=2),
                           ACT.Copy).then_inc(ff_high, 1)

            for j in range(KF // 2):
                prepare(f"ffg{j}")
                bank = ps.full(act, ("ffg", j))
                if j >= 4:
                    act.wait_ge(ff_done, j - 3)
                ps.empty(activation(full[:, j % 4, :], bank[:, :], ACT.Silu), ("ffg", j))
                prepare(f"ffu{j}")
                if j:
                    high_of_ff(j - 1)
            high_of_ff(KF // 2 - 1)
            prepare(f"dn{KF // 2 - 1}")
            norm_sums(2)
            norm_sums(3)
            high_of_norm(2)

            for n in range(2 * TT):
                t = n % TT
                name, cols = (("kv2", t), 2 * HD) if n < TT else (("q2", t), NH * HD)
                prepare("kv" if n < TT else "q21")
                bank = ps.full(act, name)
                if n >= 2:
                    act.wait_ge(head_var_done, n - 1)
                activation(relu[:, n % 2, 0:cols], bank[:, 0:cols], ACT.Square).then_inc(head_sq_done, 1)
                act.wait_ge(head_var_done, n + 1)
                nh = cols // HD
                activation(head_root[:, n % 2, 0:nh], head_var[:, n % 2, 0:nh], ACT.Sqrt).then_inc(head_root_done, 1)
            for c in range(CC):
                prepare(f"conv{c}")
                bank = ps.full(act, ("conv", c))
                activation(conv_b[:, c, :], bank[:, T:2 * T], ACT.Sigmoid).then_inc(conv_sig, 1)
            name = ("turn", "k2")
            ps.empty(activation(kT[:, :, :].rearrange("p w t -> p (w t)"), ps.full(act, name)[:, :], ACT.Copy), name)
            for t in range(TT):
                copy_turned(("turn", "q2", t), qT["q2"][:, :, t * P:(t + 1) * P])
            attention("G", 2, 0, 0)
            act.wait_ge(center_done, 1)
            activation(conv_b[:, :, :], conv_a[:, :, :], ACT.Square).then_inc(square_done, 1)
            act.wait_ge(lvar_done, 1)
            activation(rstd_c[:, 1, :], rstd_c[:, 0, :], ACT.Sqrt).then_inc(lroot_done, 1)
            act.wait_ge(lnorm_done, 1)
            for c in range(CC):
                ins = activation(conv_b[:, c, :], conv_a[:, c, :], ACT.Silu,
                                 bias=params[:, G_CONV + 2 * CC + c:G_CONV + 2 * CC + c + 1],
                                 scale=params[:, G_CONV + CC + c:G_CONV + CC + c + 1])
            settle(ins)
            activation(yT_hi[:, 4:8, :], conv_b[:, :, :], ACT.Copy).then_inc(conv_high, 1)
            act.dma_start(gain2[:, :], norm2_g).then_inc(gain2_done, 16)
            act.dma_start(final_gain, final_g).then_inc(final_done, 16)
            prepare("wp3")
            norm_sums(4)
            high_of_norm(3)

            def copy_query(h):
                bank = ps.full(act, ("query", h))
                if h >= 2:
                    ps.full(act, ("match", h - 2))
                ps.empty(activation(query[:, h % 2, :, :], bank[:, :].rearrange("p (w t) -> p w t", w=2), ACT.Copy), ("query", h))

            def copy_match(h):
                bank = ps.full(act, ("match", h))
                out_ap = match[:, :, :].rearrange("p (t h) n -> p t h n", t=TT)[:, :, h, :]
                activation(out_ap, bank[:, :].rearrange("p (t n) -> p t n", t=TT), ACT.Copy)\
                    .then_inc(match_done, 1 if h < NH - 1 else 1 + NH)

            for h in range(NH):
                prepare(f"wq{h}")
                copy_query(h)
                if h:
                    copy_match(h - 1)
            copy_match(NH - 1)

            def expert_weights(g, b, first=False):
                act.wait_ge(experts_ready, g + 1)
                activation(c_exp[:, b, :], c_top[:, b, :], ACT.Exp, bias=c_neg[:, b, :],
                           accum_out=c_sum[:, b, :]).then_inc(cexp_done, 1)
                act.wait_ge(u_free, g * BATCHES + (UROWS // 2 + BATCHES))
                activation(gelu[:, :], dots[:, :], ACT.Gelu_apprx_tanh).then_inc(gelu_done, 1)
                act.wait_ge(mixw_done, g + 1)
                for q in range(4):
                    if not first:
                        act.wait_ge(v_free, g * BATCHES + (VROWS // 2 - BATCHES + 2 * q + 2))
                    for i in range(4 * q, 4 * q + 4):
                        ins = activation(diag[:, i, :], ident, ACT.Copy, scale=mixw[:, i:i + 1])
                    ins.then_inc(diag_done, 1)

            expert_weights(0, 0, first=True)
            with act.Fori(1, TT * NH, 3) as g0:
                for i in range(3):
                    expert_weights(g0 + i, (1 + i) % 3)
            norm_sums(5)

        @block.vector
        def _(dve):
            v = nc.vector
            steps = [0]
            loop_step = dve.alloc_register("dve_loop_step")
            in_loop = [False]

            def settle(ins):
                steps[0] += 1
                ins.then_inc(dve_step, 1)
                if in_loop[0]:
                    dve.wait_ge(dve_step, loop_step)
                    dve.reg_add(loop_step, loop_step, 1)
                else:
                    dve.wait_ge(dve_step, steps[0])

            def column(buf, n):
                return buf[:, n:n + 1]

            def row(ap, n, width):
                return ap.unsqueeze(1).broadcast_to([P, n, width])

            def each(ap, n, width):
                return ap.unsqueeze(2).broadcast_to([P, n, width])

            def norm_scale(i, t):
                n = TT * i + t
                dve.wait_ge(sumsq_done, n + 1)
                v.tensor_scalar(column(var, n), column(sumsq, n), 1.0 / D, EPS, ALU.mult, ALU.add).then_inc(var_done, 1)
                dve.wait_ge(root_done, n + 1)
                settle(v.reciprocal(column(rstd, n), column(root, n)))

            def norm(i):
                for t in range(TT):
                    norm_scale(TURNED[i], t)
                    v.tensor_scalar(xs[:, t, :], X[:, t, :], column(rstd, TT * TURNED[i] + t), None,
                                    ALU.mult).then_inc(normed, 1)
                for t in range(TT):
                    for half in range(2):
                        name = ("norm", i, t, half)
                        bank = ps.full(dve, name)
                        at = G_NORM + 8 * i + 4 * half
                        ps.empty(v.tensor_tensor(full[:, 2 * t + half, :].rearrange("p (c t) -> p c t", c=4),
                                                 bank[:, :].rearrange("p (c t) -> p c t", c=4),
                                                 each(params[:, at:at + 4], 4, P), ALU.mult), name)
                        ps.copied(dve, name)
                        v.memset(flag[:, :], 0.0).then_inc(ht_full, 1)
                        if t or half:
                            low_of_norm(i, 2 * t + half - 1)
                low_of_norm(i, 2 * TT - 1)

            def low_of_norm(i, piece):
                t, half = divmod(piece, 2)
                where = (slice(None), slice(4 * half, 4 * half + 4), slice(t * P, (t + 1) * P))
                dve.wait_ge(ht_high, 4 * i + piece + 1)
                v.tensor_tensor(hT_lo[where], full[:, piece, :].rearrange("p (c t) -> p c t", c=4),
                                hT_hi[where].bitcast(F32), ALU.subtract).then_inc(ht_done, 1)

            def residual(i, name):
                halves = [(t, half) for t in range(TT) for half in range(2)]
                if name != "down":
                    halves.sort(key=lambda x: x[1])
                for t, half in halves:
                    bank = ps.full(dve, (name, t, half))
                    part = X[:, t, half * 512:(half + 1) * 512]
                    ps.empty(v.tensor_tensor(part, part, bank[:, :], ALU.add), (name, t, half))
                    if half == 0:
                        continue
                    ps.copied(dve, (name, t, 0))
                    ps.copied(dve, (name, t, 1))
                    v.memset(flag[:, :], 0.0).then_inc(residual_done, 1)
                    dve.wait_ge(residual_done, TT * i + t + 1)

            def rope(source, heads, t, out_ap, last):
                n = heads * HD
                a, b = tmp[:, 0, 0:n], tmp[:, 1, 0:n]
                halves = lambda ap: ap.rearrange("p (h w) -> p h w", h=2)
                settle(v.tensor_tensor(a.rearrange("p (h w) -> p h w", w=HD), source.rearrange("p (h w) -> p h w", w=HD),
                                       row(table(C_COS, t), heads, HD), ALU.mult))
                swapped = source.rearrange("p (h s w) -> p h s w", s=2, w=HD // 2)[:, :, ::-1, :]
                sine = table(C_SIN, t).rearrange("p (s w) -> p s w", s=2).unsqueeze(1).broadcast_to([P, heads, 2, HD // 2])
                ins = v.tensor_tensor(b.rearrange("p (h s w) -> p h s w", s=2, w=HD // 2), swapped, sine, ALU.mult)
                if last is not None:
                    ps.empty(ins, last)
                    ps.copied(dve, last)
                else:
                    settle(ins)
                if out_ap.shape == (P, n):
                    return v.tensor_tensor(out_ap, a, b, ALU.add)
                return v.tensor_tensor(out_ap, row(a, 2, n), row(b, 2, n), ALU.add)

            def rope_queries(name, b, before):
                for t in range(TT):
                    bank = ps.full(dve, (name, t))
                    if before is not None:
                        ps.full(dve, before(t))
                    rope(bank[:, :], NH, t, rotated[:, b, t, :], (name, t)).then_inc(rotated_done, 1)
                    rotated_count[0] += 1
                    dve.wait_ge(rotated_done, rotated_count[0])

            rotated_count = [0]

            dve.wait_ge(consts_done, 32)
            for t in range(TT):
                for w in range(2):
                    gain = params[:, G_QK + w * HD:G_QK + (w + 1) * HD]
                    v.tensor_tensor(turn_tab[:, t, 2 * w, :], table(C_ACOS, t), gain, ALU.mult)
                    four = lambda ap: ap.rearrange("p (g s w) -> p g s w", g=2, s=2)
                    last = v.tensor_tensor(four(turn_tab[:, t, 2 * w + 1, :]), four(table(C_ASIN, t)),
                                           four(gain)[:, :, ::-1, :], ALU.mult)
            settle(last)
            norm(0)
            rope_queries("qi", 0, None)
            for t in range(TT):
                bank = ps.full(dve, ("small", t))
                v.tensor_copy(vb[:, t, :], bank[:, HD:2 * HD])
                v.tensor_copy(wi[:, t, :], bank[:, 3 * HD:SMALL])
                settle(rope(bank[:, 2 * HD:3 * HD], 1, t, rotated[:, 1, t, 0:P].rearrange("p (w n) -> p w n", w=2), None))
                rope(bank[:, 0:HD], 1, t, rotated[:, 1, t, P:2 * P].rearrange("p (w n) -> p w n", w=2),
                     ("small", t)).then_inc(rotated_done, 1)
                rotated_count[0] += 1
                dve.wait_ge(rotated_done, rotated_count[0])
            rope_queries("qb", 0, lambda t: ("turn", "qi", t))
            rope_queries("qa", 1, lambda t: ("turn", "k"))

            def index_sum(n):
                t, heads = IDX_UNITS[n]
                nk = (t + 1) * P
                ps.copied(dve, ("index", n))
                for i, h in enumerate(heads):
                    part = relu[:, n % 2, i * nk:(i + 1) * nk]
                    if h == 0:
                        ins = v.tensor_scalar(score[:, t, 0:nk], part, wi[:, t, 0:1], None, ALU.mult)
                    else:
                        ins = v.scalar_tensor_tensor(score[:, t, 0:nk], part, wi[:, t, h:h + 1], score[:, t, 0:nk],
                                                     ALU.mult, ALU.add)
                    if h != heads[-1]:
                        settle(ins)
                ins.then_inc(relu_used, 1)
                dve.wait_ge(relu_used, n + 1)

            for n in range(3):
                index_sum(n)
            rope_queries("ka", 0, lambda t: ("turn", "qb", t))
            for n in range(3, 6):
                index_sum(n)
            for t in range(TT):
                nk = (t + 1) * P
                settle(v.scalar_tensor_tensor(score[:, t, 0:nk], score[:, t, 0:nk], IDX_SCALE, table(C_CAUSAL, t, T)[:, 0:nk],
                                              ALU.mult, ALU.add))

            def select_round(t):
                nk = (t + 1) * P
                settle(v.max(top8[:, :], score[:, t, 0:nk]))
                settle(v.match_replace(score[:, t, 0:nk], top8[:, :], score[:, t, 0:nk], TAKEN))

            def select_mask(t):
                nk = (t + 1) * P
                settle(v.tensor_scalar(selected[:, t, 0:nk], score[:, t, 0:nk], TAKEN / 2, MASKED, ALU.is_gt, ALU.mult))
                settle(v.tensor_tensor(selected[:, t, 0:nk], selected[:, t, 0:nk], table(C_CAUSAL, t, T)[:, 0:nk], ALU.add))

            conv_turn = [0]

            def conv_taps(n):
                for _ in range(n):
                    tap, c = divmod(conv_turn[0], CC)
                    if tap == TAPS:
                        return
                    conv_turn[0] += 1
                    w = params[:, G_TAP + c * TAPS + tap:G_TAP + c * TAPS + tap + 1]
                    shifted = conv_in[:, c, tap:tap + T]
                    if tap == 0:
                        ins = v.tensor_scalar(conv_a[:, c, :], shifted, w, params[:, G_CONV + c:G_CONV + c + 1], ALU.mult, ALU.add)
                    else:
                        dve.wait_ge(dve_step, steps[0] - CC + 1)
                        ins = v.scalar_tensor_tensor(conv_a[:, c, :], shifted, w, conv_a[:, c, :], ALU.mult, ALU.add)
                    steps[0] += 1
                    ins.then_inc(dve_step, 1)

            def attention(kind, index, bias):
                todo = units(kind)
                for s in range(len(todo)):
                    _, t, j = todo[s]
                    nk = nkeys(kind, t) * P
                    name = ("scores",) + todo[s]
                    bank = ps.full(dve, name)
                    pair = negmax[:, index, t, pair_of(j)[0]:pair_of(j)[1] + 1:2]
                    if kind == "G":
                        settle(v.tensor_reduce(pair, bank[:, 0:2 * nk].rearrange("p (h n) -> p h n", h=2), AX_X, ALU.max))
                        v.tensor_scalar(pair, pair, -SCALE, None, ALU.mult).then_inc(max_done, 1)
                    else:
                        scaled = S_sb[:, s % 2, 0:2 * nk].rearrange("p (h n) -> p h n", h=2)
                        if s >= 2:
                            dve.wait_ge(exp_done, 8 * index + s - 1)
                        elif index:
                            dve.wait_ge(exp_done, 8 * index)
                        ps.empty(v.scalar_tensor_tensor(scaled, bank[:, 0:2 * nk].rearrange("p (h n) -> p h n", h=2), SCALE,
                                                        row(bias(t)[:, 0:nk], 2, nk), ALU.mult, ALU.add), name)
                        ps.copied(dve, name)
                        v.tensor_reduce(pair, scaled, AX_X, ALU.max, negate=True).then_inc(max_done, 1)
                    if kind == "A":
                        for _ in range(2):
                            select_round(s // 4)
                        if s % 4 == 3:
                            select_mask(s // 4)
                    if kind == "G":
                        dve.wait_ge(exp_done, 8 * index + s + 1)
                        ps.empty(v.memset(flag[:, :], 0.0), name)
                        ps.copied(dve, name)
                        conv_taps(18)
                    if s == 6:
                        normalise(kind, index, 0)
                    if s == 7:
                        low_of_y(kind, index, 0)
                normalise(kind, index, 1)
                low_of_y(kind, index, 1)

            def low_of_y(kind, index, t):
                base = 4 if kind == "B" else 0
                where = (slice(None), slice(base, base + 4), slice(t * P, (t + 1) * P))
                dve.wait_ge(y_high, 2 * index + t + 1)
                ps.empty(v.tensor_tensor(yT_lo[where], ps.bank(("y", kind, t))[:, :].rearrange("p (c t) -> p c t", c=4),
                                         yT_hi[where].bitcast(F32), ALU.subtract), ("y", kind, t))

            def normalise(kind, index, t):
                dve.wait_ge(exp_done, 8 * index + 4 * t + 4)
                settle(v.reciprocal(rden[:, index, t, :], den[:, index, t, :]))
                dve.wait_ge(pv_done, 8 * index + 4 * t + 4)
                if index or t:
                    before = ("y", kind, 0) if t else ("y", "ABG"[index - 1], 1)
                    ps.full(dve, before)
                v.tensor_tensor(y_tok[:, :].rearrange("p (h n) -> p h n", h=NH), y_bank[:, :].rearrange("p (h n) -> p h n", h=NH),
                                each(rden[:, index, t, :], NH, HD), ALU.mult).then_inc(y_emptied, 1)

            attention("A", 0, lambda t: table(C_LOGC, t, T))
            attention("B", 1, lambda t: selected[:, t, :])

            for c in range(KD):
                bank = ps.full(dve, ("up", c))
                dve.wait_ge(gate_done, c // 4 + 1)
                t2 = tmp[:, c % 2, :].rearrange("p (g t) -> p g t", g=2)
                ps.empty(v.tensor_tensor(t2, bank[:, :].rearrange("p (g t) -> p g t", g=2),
                                         gates[:, :, :].rearrange("p (g c) t -> p g c t", g=2)[:, :, c, :], ALU.mult), ("up", c))
                ps.copied(dve, ("up", c))
                part = full[:, c % 4, 0:T]
                settle(v.tensor_tensor(part, t2[:, 0, :], t2[:, 1, :], ALU.add))
                settle(v.tensor_copy(merged_hi[:, c, :], part))
                v.tensor_tensor(merged_lo[:, c, :], part, merged_hi[:, c, :].bitcast(F32), ALU.subtract).then_inc(merged_done, 1)
                dve.wait_ge(merged_done, c + 1)
            residual(0, "out")
            norm(1)

            def low_of_ff(j):
                dve.wait_ge(ff_high, j + 1)
                part = (slice(None), slice(2 * j, 2 * j + 2))
                v.tensor_tensor(ff_lo[part], full[:, j % 4, :].rearrange("p (c t) -> p c t", c=2),
                                ff_hi[part].bitcast(F32), ALU.subtract).then_inc(ff_done, 1)

            for j in range(KF // 2):
                bank = ps.full(dve, ("ffu", j))
                ps.copied(dve, ("ffg", j))
                part = full[:, j % 4, :]
                ps.empty(v.tensor_tensor(part, part, bank[:, :], ALU.mult), ("ffu", j))
                ps.copied(dve, ("ffu", j))
                v.memset(flag[:, :], 0.0).then_inc(ff_full, 1)
                if j:
                    low_of_ff(j - 1)
            low_of_ff(KF // 2 - 1)
            residual(1, "down")
            dve.wait_ge(norm_final_done, 16)
            for t in range(TT):
                norm_scale(2, t)
                v.scalar_tensor_tensor(X[:, t, :], X[:, t, :], column(rstd, TT * 2 + t), gain2[:, :], ALU.mult,
                                       ALU.mult).then_inc(residual_done, 1)
                dve.wait_ge(residual_done, TT * 2 + t + 1)
            norm(2)

            def head_norm(n, bank, heads):
                b = n % 2
                dve.wait_ge(head_sq_done, n + 1)
                settle(v.tensor_reduce(head_ss[:, b, 0:heads], relu[:, b, 0:heads * HD].rearrange("p (h w) -> p h w", w=HD), AX_X, ALU.add))
                v.tensor_scalar(head_var[:, b, 0:heads], head_ss[:, b, 0:heads], 1.0 / HD, EPS, ALU.mult, ALU.add).then_inc(head_var_done, 1)
                dve.wait_ge(head_root_done, n + 1)
                settle(v.reciprocal(head_rstd[:, b, 0:heads], head_root[:, b, 0:heads]))
                ins = v.tensor_tensor(tmp[:, 0, 0:heads * HD].rearrange("p (h w) -> p h w", w=HD),
                                      bank[:, 0:heads * HD].rearrange("p (h w) -> p h w", w=HD),
                                      each(head_rstd[:, b, 0:heads], heads, HD), ALU.mult)
                return ins

            def axial(t, heads, w, a, b):
                z = tmp[:, 0, 0:heads * HD]
                v.tensor_tensor(a.rearrange("p (h w) -> p h w", w=HD), z.rearrange("p (h w) -> p h w", w=HD),
                                row(turn_tab[:, t, 2 * w, :], heads, HD), ALU.mult)
                for g in range(2):
                    five = lambda ap: ap.rearrange("p (h g s w) -> p h g s w", g=2, s=2, w=HD // 4)[:, :, g]
                    sine = turn_tab[:, t, 2 * w + 1, :].rearrange("p (g s w) -> p g s w", g=2, s=2)[:, g]
                    ins = v.tensor_tensor(five(b), five(z)[:, :, ::-1, :], sine.unsqueeze(1).broadcast_to([P, heads, 2, HD // 4]), ALU.mult)
                settle(ins)

            settle(v.memset(conv_in[:, :, 0:PAD], 0.0))
            settle(v.memset(conv_in[:, :, PAD + T:], 0.0))
            for t in range(TT):
                bank = ps.full(dve, ("kv2", t))
                dve.wait_ge(head_sq_done, t + 1)
                v.tensor_copy(v2[:, t, :], bank[:, 2 * HD:4 * HD])
                ins = head_norm(t, bank, 2)
                ps.empty(ins, ("kv2", t))
                ps.copied(dve, ("kv2", t))
                a, b = tmp[:, 1, 0:P], tmp[:, 1, P:2 * P]
                axial(t, 2, 1, a, b)
                pair = lambda ap: ap.rearrange("p (h w) -> p h w", h=2).unsqueeze(2).broadcast_to([P, 2, 2, HD])
                v.tensor_tensor(rotated[:, 0, t, 0:2 * P].rearrange("p (h s w) -> p h s w", h=2, s=2), pair(a), pair(b),
                                ALU.add).then_inc(rotated_done, 1)
                rotated_count[0] += 1
                dve.wait_ge(rotated_done, rotated_count[0])
            for t in range(TT):
                bank = ps.full(dve, ("q2", t))
                ins = head_norm(TT + t, bank, NH)
                ps.empty(ins, ("q2", t))
                ps.copied(dve, ("q2", t))
                axial(t, NH, 0, rotated[:, 1, t, :], tmp[:, 1, :])
                v.tensor_tensor(rotated[:, 1, t, :], rotated[:, 1, t, :], tmp[:, 1, :], ALU.add).then_inc(rotated_done, 1)
                rotated_count[0] += 1
                dve.wait_ge(rotated_done, rotated_count[0])
            for c in range(CC):
                bank = ps.full(dve, ("conv", c))
                dve.wait_ge(conv_sig, c + 1)
                ps.empty(v.tensor_tensor(conv_in[:, c, PAD:PAD + T], bank[:, 0:T], conv_b[:, c, :], ALU.mult), ("conv", c))
            for c in range(CC):
                ps.copied(dve, ("conv", c))
            attention("G", 2, None)
            conv_taps(CC * TAPS)
            dve.wait_ge(dve_step, steps[0])
            settle(v.memset(flag[:, :], 0.0))
            v.memset(flag[:, :], 0.0).then_inc(conv_done, 1)
            bank = ps.full(dve, ("mean",))
            ps.empty(v.tensor_tensor(conv_a[:, :, :], conv_a[:, :, :], row(bank[:, 0:T], CC, T), ALU.subtract), ("mean",))
            ps.copied(dve, ("mean",))
            v.memset(flag[:, :], 0.0).then_inc(center_done, 1)
            bank = ps.full(dve, ("var",))
            ps.empty(v.tensor_scalar(rstd_c[:, 0, :], bank[:, 0:T], EPS, None, ALU.add), ("var",))
            ps.copied(dve, ("var",))
            v.memset(flag[:, :], 0.0).then_inc(lvar_done, 1)
            dve.wait_ge(lroot_done, 1)
            settle(v.reciprocal(rstd_c[:, 0, :], rstd_c[:, 1, :]))
            v.tensor_tensor(conv_a[:, :, :], conv_a[:, :, :], row(rstd_c[:, 0, :], CC, T), ALU.mult).then_inc(lnorm_done, 1)
            dve.wait_ge(conv_high, 1)
            v.tensor_tensor(yT_lo[:, 4:8, :], conv_b[:, :, :], yT_hi[:, 4:8, :].bitcast(F32), ALU.subtract).then_inc(conv_out, 1)
            residual(3, "out2")
            norm(3)
            dve.wait_ge(gain2_done, 16)
            for t in range(TT):
                ins = v.tensor_tensor(hn[:, t, :], xs[:, t, :], gain2[:, :], ALU.mult)
            settle(ins)
            v.memset(flag[:, :], 0.0).then_inc(u_free, UROWS // 2)
            dve.wait_ge(u_free, UROWS // 2)
            v.memset(flag[:, :], 0.0).then_inc(v_free, VROWS // 2)
            dve.wait_ge(v_free, VROWS // 2)

            def best(values, top, left):
                settle(v.max(top[:, 0:8], values))
                settle(v.match_replace(left, top[:, 0:8], values, TAKEN))
                settle(v.max(top[:, 8:16], left))

            def find(values, left, top, index):
                settle(v.max_index(index[:, 0:8], top[:, 0:8], values))
                settle(v.max_index(index[:, 8:16], top[:, 8:16], left))

            def choose(g, b):
                dve.wait_ge(match_done, g + 1)
                both = match[:, :, :].rearrange("p g n -> p (g n)")[:, bass.ds(g * 2 * NKEY, 2 * NKEY)]
                settle(v.tensor_copy(s_work[:, 0, :, :].rearrange("p w n -> p (w n)"), both))
                for w in range(2):
                    best(s_work[:, 0, w, :], s_top[:, w, :], s_work[:, 1, w, :])
                    find(s_work[:, 0, w, :], s_work[:, 1, w, :], s_top[:, w, :], s_idx[:, w, :])
                square = lambda ap: ap.rearrange("p (a b) -> p a b", a=ETOP)
                settle(v.tensor_tensor(square(cand[:, 0, :]), each(s_top[:, 0, :], ETOP, ETOP), row(s_top[:, 1, :], ETOP, ETOP), ALU.add))
                best(cand[:, 0, :], c_top[:, b, :], cand[:, 1, :])
                find(cand[:, 0, :], cand[:, 1, :], c_top[:, b, :], c_pos[:, :])
                settle(v.tensor_scalar(c_digit[:, 0, :], c_pos[:, :], 4, None, ALU.logical_shift_right))
                settle(v.tensor_scalar(c_digit[:, 1, :], c_pos[:, :], 15, None, ALU.bitwise_and))
                for w in range(2):
                    hot = square(cand[:, 0, :])
                    settle(v.tensor_tensor(hot, each(c_digit[:, w, :], ETOP, ETOP), row(iota, ETOP, ETOP), ALU.is_equal))
                    settle(v.tensor_tensor(hot, hot, row(s_idx[:, w, :], ETOP, ETOP), ALU.mult))
                    settle(v.tensor_reduce(c_part[:, w, :], hot, AX_X, ALU.add))
                settle(v.tensor_scalar(c_neg[:, b, :], c_top[:, b, 0:1], -1.0, None, ALU.mult))
                v.scalar_tensor_tensor(expert[:, b, :], c_part[:, 0, :], float(NKEY), c_part[:, 1, :], ALU.mult,
                                       ALU.add).then_inc(experts_ready, 1)
                dve.wait_ge(experts_ready, g + 1)

            def group(g, b, t, more=True, early=False):
                if more:
                    if not early:
                        for slot in range(VROWS // 2):
                            dve.wait_ge(v_in[slot], g * ROW_STEP - ROW_STEP)
                    choose(g + 1, (b + 1) % 3)
                for m in range(BATCHES):
                    slot = m % (UROWS // 2)
                    dve.wait_ge(u_in[slot], g * 64 + 32 * (m // (UROWS // 2) + 1))
                    for i in range(2):
                        row_of_u = u_rows[2 * slot + i][:, :]
                        ins = v.tensor_tensor_reduce(out=row_of_u, in0=row_of_u, in1=hn[:, t, :], scale=1.0, scalar=0.0,
                                                     op0=ALU.mult, op1=ALU.add, accum_out=dots[:, 2 * m + i:2 * m + i + 1])
                    ins.then_inc(u_free, 1)
                dve.wait_ge(cexp_done, g + 1)
                settle(v.reciprocal(c_rs[:, b, :], c_sum[:, b, :]))
                dve.wait_ge(gelu_done, g + 1)
                if not (isinstance(g, int) and g == 0):
                    dve.wait_ge(diag_done, g * 4)
                v.scalar_tensor_tensor(mixw[:, :], c_exp[:, b, :], c_rs[:, b, :], gelu[:, :], ALU.mult,
                                       ALU.mult).then_inc(mixw_done, 1)

            choose(0, 0)
            for n in range(NGRAN - LATE, NGRAN):
                dve.wait_ge(high_done, n + 1)
                v.tensor_tensor(w_lo[n % RING][:, :], raw[n % RING][:, :], w_hi[n % RING][:, :].bitcast(F32),
                                ALU.subtract).then_inc(late_split_done, 1)
            choose(1, 1)
            group(0, 0, 0, more=False)
            group(1, 1, 0, early=True)
            for t, (first, end) in enumerate(((2, NH), (NH, TT * NH - 2))):
                dve.reg_mov(loop_step, steps[0] + 1)
                in_loop[0], before = True, steps[0]
                with dve.Fori(0, (end - first) // 3, 1) as q:
                    for i in range(3):
                        group(q * 3 + (first + i), (first + i) % 3, t)
                in_loop[0] = False
                steps[0] = before + (steps[0] - before) * (end - first) // 3
            for g in (TT * NH - 2, TT * NH - 1):
                group(g, g % 3, 1, more=g < TT * NH - 1)

            dve.wait_ge(final_done, 16)
            for t in range(TT):
                dve.wait_ge(v_free, VROWS // 2 + BATCHES * NH * (t + 1))
                for half in range(2):
                    settle(v.tensor_copy(X[:, t, half * 512:(half + 1) * 512], ps.bank(("mix", t, half))[:, :]))
                v.memset(flag[:, :], 0.0).then_inc(residual_done, 1)
                norm_scale(5, t)
                v.scalar_tensor_tensor(X[:, t, :], X[:, t, :], column(rstd, TT * 5 + t), final_gain, ALU.mult,
                                       ALU.mult).then_inc(fout_done, 1)

        @block.gpsimd
        def _(pool):
            def low_part(n, r):
                pool.wait_ge(high_done, n + 1)
                nc.gpsimd.tensor_tensor(w_lo[r][:, :], raw[r][:, :], w_hi[r][:, :].bitcast(F32), ALU.subtract).then_inc(split_done, 1)

            whole = (NGRAN - LATE) // RING * RING
            with pool.Fori(0, whole, RING) as n0:
                for r in range(RING):
                    low_part(n0 + r, r)
            for n in range(whole, NGRAN - LATE):
                low_part(n, n % RING)

            u_count = pool.alloc_register("u_count")
            v_count = pool.alloc_register("v_count")
            pool.reg_mov(u_count, BATCHES + 1)
            pool.reg_mov(v_count, 1)

            def fetch(table_in, rows, free, count, arrived, slot, b, m):
                pool.wait_ge(free, count)
                if not isinstance(count, int):
                    pool.reg_add(count, count, 1)
                for i in range(2):
                    nc.gpsimd.indirect_dma_start(
                        rows[2 * slot + i][:, :], None, table_in,
                        bass.IndirectOffsetOnAxis(ap=expert[:, b, 2 * m + i:2 * m + i + 1], axis=0)).then_inc(arrived[slot], 16)

            def fetch_u(b, m, count=u_count):
                slot = m % (UROWS // 2)
                fetch(peer_u, u_rows, u_free, count, u_in, slot, b, m)

            def fetch_v(b, m, count=v_count):
                slot = m % (VROWS // 2)
                fetch(peer_v, v_rows, v_free, count, v_in, slot, b, m)

            pool.wait_ge(experts_ready, 1)
            for m in range(BATCHES):
                fetch_u(0, m, m + 1)
            group_count = pool.alloc_register("group_count")
            pool.reg_mov(group_count, 2)
            with pool.Fori(1, TT * NH, 3) as g0:
                for i in range(3):
                    pool.wait_ge(experts_ready, group_count)
                    pool.reg_add(group_count, group_count, 1)
                    for m in range(BATCHES):
                        fetch_u((1 + i) % 3, m)
                        fetch_v(i % 3, m)
            for m in range(BATCHES):
                fetch_v((TT * NH - 1) % 3, m, (TT * NH - 1) * BATCHES + m + 1)


def _blocks(w, n):
    k = w.shape[0] // P
    return [w[:, i:i + n].reshape(k, P, n).transpose(1, 0, 2).reshape(P, k * n) for i in range(0, w.shape[1], n)]


def kernel(**inputs):
    import concourse.bacc as _bacc
    from concourse.bass_utils import run_bass_kernel_spmd as _run

    a = {k: np.asarray(x) for k, x in inputs.items()}
    w_in, w_in2 = a["w_in"][0], a["w_in_2"]
    ofs = np.cumsum([0, 512, 512, 512, 512, HD, HD, 512, HD, NH, D, D])
    qa, ka, va, qb, kb, vb, qi, ki, wi, ga, gb = [w_in[:, ofs[i]:ofs[i + 1]] for i in range(11)]
    chunked = lambda w: w.reshape(-1, P, w.shape[1]).transpose(1, 0, 2)
    granules = {}
    for name, w in (("qi", qi), ("qb", qb), ("qa", qa), ("ka", ka), ("va", va), ("wo", a["w_out"][0]), ("wp", a["w_out_2"]),
                    ("wq", a["peer_wq_2"]), ("gate", np.concatenate([ga, gb], 1)), ("ffg", a["w_gate"][0]),
                    ("ffu", a["w_up"][0]), ("q2", w_in2[:, 0:512])):
        for i, blk in enumerate(_blocks(w, T)):
            granules[f"{name}{i}"] = blk
    granules["kv"] = _blocks(w_in2[:, 512:768], T)[0]
    small = _blocks(np.concatenate([kb, vb, ki, wi], 1), SMALL)[0]
    granules["small"] = np.concatenate([small, np.zeros((P, GRAIN - small.shape[1]), np.float32)], 1)
    up = np.concatenate([a["w_up_a"][0], a["w_up_b"][0]], 0)
    for u, blk in enumerate(_blocks(up, T)):
        granules[f"up{u}"] = blk
    down = chunked(a["w_down"][0])
    for j in range(KF // 2):
        granules[f"dn{j}"] = down[:, 2 * j:2 * j + 2].reshape(P, GRAIN)
    for c in range(CC):
        both = [w_in2[:, at + c * P:at + (c + 1) * P] for at in (768, 1280)]
        granules[f"conv{c}"] = _blocks(np.concatenate(both, 1), T)[0]
    stream = np.stack([granules[n] for n in GRANULES])
    cols = lambda x: x.reshape(-1, P).T
    params = np.concatenate(
        [cols(a["norm_mix"]), cols(a["norm_ffn"]), cols(a["norm1_g_2"]), cols(a["norm2_g_2"]),
         np.broadcast_to(a["q_norm_g_2"], (P, HD)), np.broadcast_to(a["k_norm_g_2"], (P, HD)),
         a["conv_dw_2"][:, 0, :].T.reshape(CC, P, TAPS).transpose(1, 0, 2).reshape(P, CC * TAPS),
         cols(a["conv_b_2"]), cols(a["conv_ln_g_2"]), cols(a["conv_ln_b_2"]),
         a["peer_keys_2"].transpose(2, 0, 1).reshape(P, 2 * NKEY)], 1)
    arrays = {"x_in": a["x"].reshape(T, D), "stream": stream, "consts_in": constants(), "params_in": params,
              "norm_final": np.broadcast_to(a["norm_final"], (P, D)),
              "norm2_g": np.broadcast_to(a["norm2_g_2"], (P, D)), "final_g": np.broadcast_to(a["final_g_2"], (P, D)),
              "peer_u": a["peer_u_2"], "peer_v": a["peer_v_2"]}
    nc = _bacc.Bacc("TRN2", target_bir_lowering=False, num_devices=1)
    args, sent = [], {}
    for name, x in arrays.items():
        sent[f"{name}_dram"] = np.ascontiguousarray(x)
        args.append(nc.dram_tensor(f"{name}_dram", x.shape, mybir.dt.from_np(x.dtype), kind="ExternalInput").ap())
    args.append(nc.dram_tensor("out_dram", (T, D), F32, kind="ExternalOutput").ap())
    bass_two_blocks_kernel(nc, *args)
    r = _run(nc, [sent], core_ids=[0])
    return r.results[0]["out_dram"].reshape(1, T, D)
```

```python
from contextlib import ExitStack

import numpy as np
import concourse.bass as bass
from concourse import mybir

F32 = mybir.dt.float32
F32R = mybir.dt.float32r
U32 = mybir.dt.uint32
ALU = mybir.AluOpType
ACT = mybir.ActivationFunctionType
AX_X = mybir.AxisListType.X

P = 128
T = 256
TT = T // P
D = 1024
KD = D // P
HD = 64
NH = 8
FF = 2816
KF = FF // P
TOPK = 64
TAPS = 31
PAD = (TAPS - 1) // 2
POOL_TAPS = 17
PE_TAPS = 28
NKEY = 128
UROWS, VROWS = 8, 4
SHARE = (2, 4, 6)
BATCHES = 8
ROW_STEP = 16 * 2 * BATCHES // (VROWS // 2)
ETOP = 16
NGATE = 2 * KD
CC = 4
EPS = 1e-6
NNORM = 6
TURNED = (0, 1, 3, 4)
SCALE = HD ** -0.5
IDX_SCALE = (HD ** -0.5) * (NH ** -0.5)
MASKED = -1e30
TAKEN = -3e38

GRAIN = 2048
RING = 3
GRANULES = (["qi0", "qi1", "small", "qb0", "qb1", "qa0", "qa1", "ka0", "ka1", "va0", "va1"]
            + [f"gate{f}" for f in range(NGATE // 2)] + [f"up{u}" for u in range(KD // 2)]
            + [f"wo{q}" for q in range(4)]
            + [f"{n}{j}" for j in range(KF // 2) for n in ("ffg", "ffu")] + [f"dn{j}" for j in range(KF // 2)]
            + [f"conv{c}" for c in range(CC)] + ["kv", "q20", "q21"] + [f"wp{q}" for q in range(4)]
            + [f"wq{h}" for h in range(NH)])
NGRAN = len(GRANULES)
LATE = 4
PARTIAL = (["qi0", "qb0", "qa0", "ka0", "va0", "wo0", "wo2"] + [f"dn{j}" for j in range(KF // 2 - 1)]
           + ["q20", "wp0", "wp2"])
READ_BY = {"qi1": ("qi", 1), "small": ("small", 1), "qb1": ("qb", 1), "qa1": ("qa", 1), "ka1": ("ka", 1),
           "va1": ("va", 1), "wo1": ("out", 1, 0), "wo3": ("out", 1, 1), f"dn{KF // 2 - 1}": ("down", 1, 1),
           "kv": ("kv2", 1), "q21": ("q2", 1), "wp1": ("out2", 1, 0), "wp3": ("out2", 1, 1)}
READ_BY |= {f"gate{f}": ("gate", f) for f in range(NGATE // 2)}
READ_BY |= {f"up{u}": ("up", 2 * u + 1) for u in range(KD // 2)}
READ_BY |= {f"{n}{j}": (n, j) for j in range(KF // 2) for n in ("ffg", "ffu")}
READ_BY |= {f"conv{c}": ("conv", c) for c in range(CC)} | {f"wq{h}": ("query", h) for h in range(NH)}
SLAB = 47 * D + 512
BRIDGE = {0: 0, 1: 8, 2: 20, 3: 8, "mean": 22, "branch": 8}
SMALL = 3 * HD + NH

C_ID, C_COS, C_SIN, C_ACOS, C_ASIN = 0, 128, 256, 384, 512
C_MEAN, C_IOTA, C_LOGC, C_CAUSAL = 640, 768, 784, 784 + 512
NCONST = 784 + 1024
G_NORM, G_QK, G_TAP, G_CONV, G_KEYS = 0, 32, 160, 160 + CC * TAPS, 160 + CC * TAPS + 3 * CC
NPARAM = G_KEYS + 2 * NKEY


def constants():
    c = np.zeros((P, NCONST), np.float32)
    c[:, C_ID:C_ID + P] = np.eye(P)
    half = HD // 2
    freq = (np.float32(10000.0) ** (-np.arange(half, dtype=np.float32) / np.float32(half))).astype(np.float32)
    quarter = HD // 4
    afreq = (np.float32(10000.0) ** (-np.arange(quarter, dtype=np.float32) / np.float32(quarter))).astype(np.float32)
    for t in range(TT):
        pos = np.arange(t * P, (t + 1) * P)
        ang = pos.astype(np.float32)[:, None] * freq
        c[:, C_COS + t * HD:C_COS + (t + 1) * HD] = np.concatenate([np.cos(ang)] * 2, 1)
        c[:, C_SIN + t * HD:C_SIN + (t + 1) * HD] = np.concatenate([-np.sin(ang), np.sin(ang)], 1)
        row, col = (pos // 64).astype(np.float32)[:, None] * afreq, (pos % 64).astype(np.float32)[:, None] * afreq
        c[:, C_ACOS + t * HD:C_ACOS + (t + 1) * HD] = np.concatenate(
            [np.cos(row)] * 2 + [np.cos(col)] * 2, 1)
        c[:, C_ASIN + t * HD:C_ASIN + (t + 1) * HD] = np.concatenate(
            [-np.sin(row), np.sin(row), -np.sin(col), np.sin(col)], 1)
        q, k = pos[:, None], np.arange(T)[None, :]
        dist = q - k
        count = ((dist >= 0) & (dist <= P)).astype(np.int64)
        for dilation in (4, 16):
            count += (dist >= 0) & (dist % dilation == 0)
        c[:, C_LOGC + t * T:C_LOGC + (t + 1) * T] = np.where(count > 0, np.log(np.maximum(count, 1)), MASKED)
        c[:, C_CAUSAL + t * T:C_CAUSAL + (t + 1) * T] = np.where(dist >= 0, 0.0, MASKED)
    c[:, C_MEAN:C_MEAN + P] = 1.0 / (CC * P)
    c[:, C_IOTA:C_IOTA + 16] = np.arange(16)
    return c


def slab_base(nc, slab):
    return nc.sbuf_base - SLAB * 4


class Psum:

    POOLS = {"D": (0, 1, 2), "S": (3, 4), "T": (5, 6)}

    def __init__(self, banks, filled, emptied):
        self.banks, self.filled, self.emptied = banks, filled, emptied
        self.at, self.order, self.uses, self.turn = {}, [], [0] * 8, dict.fromkeys(self.POOLS, 0)
        self.started = 0

    def plan(self, pool, name, bank=None):
        if bank is None:
            bank = self.POOLS[pool][self.turn[pool] % len(self.POOLS[pool])]
            self.turn[pool] += 1
        self.at[name] = (bank, self.uses[bank])
        self.order.append(name)
        self.uses[bank] += 1

    def bank(self, name):
        return self.banks[self.at[name][0]]

    def start(self, pe, name, freed=None):
        assert self.order[self.started] == name, (self.order[self.started], name)
        self.started += 1
        b, n = self.at[name]
        if freed:
            pe.wait_ge(*freed)
        elif n:
            pe.wait_ge(self.emptied[b], n)
        return self.banks[b]

    def fill(self, ins, name):
        ins.then_inc(self.filled[self.at[name][0]], 1)

    def full(self, eng, name):
        b, n = self.at[name]
        eng.wait_ge(self.filled[b], n + 1)
        return self.banks[b]

    def empty(self, ins, name):
        ins.then_inc(self.emptied[self.at[name][0]], 1)

    def copied(self, eng, name):
        b, n = self.at[name]
        eng.wait_ge(self.emptied[b], n + 1)


def units(kind):
    return [(kind, t, j) for t in range(TT) for j in range(NH // 2)]


def pair_of(j):
    h = 4 * (j // 2) + j % 2
    return (h, h + 2)


IDX_UNITS = [(0, (0, 2, 4, 6)), (0, (1, 3, 5, 7))] + [(1, pair_of(j)) for j in range(NH // 2)]


GATE_STEPS = {"A": (0, 2, 4, 6), "B": (0, 2, 4, 8), "G": ()}


def gate_beside(kind, s):
    if s in GATE_STEPS[kind]:
        return GATE_STEPS[kind].index(s) + (4 if kind == "B" else 0)
    return None


def nkeys(kind, t):
    return TT if kind == "G" else t + 1


def scored_after(h):
    return {0: [0], 1: []}.get(h, [h - 1]) + ([h] if h == NH - 1 else [])


def plan_psum(ps):
    def norm(i):
        for half in range(2):
            for t in range(TT):
                ps.plan("ST"[half], ("norm", i, t, half))

    def attention(kind):
        for s in range(len(units(kind)) + 2):
            if kind == "G" and s == 2:
                ps.plan("T", ("turn", "q2", 1))
            if s < 8:
                ps.plan("S", ("scores",) + units(kind)[s])
            if gate_beside(kind, s) is not None:
                ps.plan("D", ("gate", gate_beside(kind, s)))
            if 1 <= s < 9:
                ps.plan("T", ("probs",) + units(kind)[s - 1])
            if s == 7:
                ps.plan("T", ("y", kind, 0))
        ps.plan("T", ("y", kind, 1))

    norm(0)
    for block in ("qi", "small", "qb"):
        for t in range(TT):
            ps.plan("D", (block, t))
    for t in range(TT):
        ps.plan("T", ("turn", "qi", t))
    ps.plan("T", ("turn", "k"))
    for t in range(TT):
        ps.plan("D", ("qa", t))
    for t in range(TT):
        ps.plan("T", ("turn", "qb", t))
    for n in range(3):
        ps.plan("S", ("index", n))
    for t in range(TT):
        ps.plan("D", ("ka", t))
    for n in range(3, 6):
        ps.plan("S", ("index", n))
    for t in range(TT):
        ps.plan("T", ("turn", "qa", t))
    for t in range(TT):
        ps.plan("D", ("va", t))
    for t in range(TT):
        ps.plan("T", ("turn", "ka", t))
    attention("A")
    attention("B")
    for c in range(KD):
        ps.plan("D", ("up", c))
    for half in range(2):
        for t in range(TT):
            ps.plan("D", ("out", t, half))
    norm(1)
    for j in range(KF // 2):
        ps.plan("D", ("ffg", j))
        ps.plan("D", ("ffu", j))
    for t in range(TT):
        for half in range(2):
            n = t * 2 + half
            ps.plan(None, ("down", t, half), bank=(0, 1, 2, 3)[n])
    norm(2)
    for c in range(CC):
        ps.plan("D", ("conv", c))
    for t in range(TT):
        ps.plan("D", ("kv2", t))
    for t in range(TT):
        ps.plan("D", ("q2", t))
    ps.plan("T", ("turn", "k2"))
    ps.plan("T", ("turn", "q2", 0))
    ps.plan(None, ("taps",), bank=2)
    attention("G")
    ps.plan(None, ("mean",), bank=3)
    for t in range(TT):
        ps.plan(None, ("out2", t, 0), bank=t)
    ps.plan(None, ("var",), bank=3)
    for t in range(TT):
        ps.plan(None, ("out2", t, 1), bank=(2, 4)[t])
    norm(3)
    for h in range(NH):
        ps.plan("D", ("query", h))
        for m in scored_after(h):
            ps.plan("S", ("match", m))
    for t in range(TT):
        for half in range(2):
            ps.plan(None, ("mix", t, half), bank=(0, 1, 2, 5)[t * 2 + half])


def bass_two_blocks_kernel(nc, x_in, stream, consts_in, params_in, norm_final, norm2_g, final_g,
                           peer_u, peer_v, out):
    with ExitStack() as ctx:
        def sb(name, shape, dt=F32):
            return ctx.enter_context(nc.sbuf_tensor(name, shape, dt))

        def sem(name):
            return ctx.enter_context(nc.semaphore(name))

        slab = sb("slab", [P, SLAB])
        base = slab_base(nc, slab)

        def at(name, col, shape, dt=F32):
            assert col + int(np.prod(shape[1:])) <= SLAB, name
            return nc.alloc_sbuf_tensor_at(name, shape, dt, offset=base + 4 * col)

        raw = [at(f"raw{r}", r * GRAIN, [P, GRAIN]) for r in range(RING)]
        w_hi = [at(f"w_hi{r}", (RING + r) * GRAIN, [P, GRAIN], F32R) for r in range(RING)]
        w_lo = [at(f"w_lo{r}", (2 * RING + r) * GRAIN, [P, GRAIN], F32R) for r in range(RING)]
        m0 = 3 * RING * GRAIN
        gates = at("gates", m0, [P, NGATE, T])
        q0 = m0 + NGATE * T
        qT = {n: at(f"qT_{n}", q0 + i * D, [P, 4, T]) for i, n in enumerate(("qi", "qb", "qa", "ka"))}
        qT["q2"] = qT["qi"]
        kT = at("kT", q0 + 4 * D, [P, 2, T])
        va = at("va", q0 + 4 * D + 512, [P, TT, 512])
        r0 = q0 + 4 * D + 512 + D
        rotated = at("rotated", r0, [P, 2, TT, 512])
        yT_lo = at("yT_lo", r0, [P, KD, T], F32R)
        vb = at("vb", r0 + 2048, [P, TT, HD])
        v2 = at("v2", r0 + 2048 + 128, [P, TT, 2 * HD])
        conv_in = at("conv_in", m0, [P, CC, T + 2 * PAD])
        conv_a = at("conv_a", m0 + 1144, [P, CC, T])
        conv_b = at("conv_b", m0 + 1144 + D, [P, CC, T])
        rstd_c = at("rstd_c", m0 + 1144 + 2 * D, [P, 2, T])
        n1 = (q0 + 4 * D - (m0 + KF * T)) // P
        tap_diag1 = at("tap_diag1", m0 + KF * T, [P, n1, P])
        tap_diag2 = at("tap_diag2", q0 + 4 * D + 512, [P, PE_TAPS - n1, P])
        tap_diag = [tap_diag1[:, i, :] for i in range(n1)] + [tap_diag2[:, i, :] for i in range(PE_TAPS - n1)]
        assert PE_TAPS - n1 <= 8
        ff_hi = at("ff_hi", m0, [P, KF, T], F32R)
        u_rows = [at(f"u_row{i}", m0 + i * D, [P, D]) for i in range(UROWS)]
        v_rows = [at(f"v_row{i}", m0 + (UROWS + i) * D, [P, D]) for i in range(VROWS)]
        x0 = m0 + (UROWS + VROWS) * D
        assert r0 + 2048 + 128 + 256 <= x0
        X = at("residual", x0, [P, TT, D])
        xs = at("normed_tokens", x0 + 2 * D, [P, TT, D])
        merged_hi = at("merged_hi", x0 + 2 * D, [P, KD, T], F32R)
        diag = at("diag", x0 + 2 * D, [P, ETOP, P])
        hT_hi = at("hT_hi", x0 + 4 * D, [P, KD, T], F32R)
        hT_lo = at("hT_lo", x0 + 6 * D, [P, KD, T], F32R)
        yT_hi = at("yT_hi", x0 + 8 * D, [P, KD, T], F32R)
        hn = at("hn", x0 + 8 * D, [P, TT, D])
        w0 = x0 + 10 * D
        S_sb = at("S_sb", w0, [P, 2, 512])
        E_sb = at("E_sb", w0 + D, [P, 2, 512])
        PT = at("PT", w0 + 2 * D, [P, 2, 512])
        merged_lo = at("merged_lo", w0, [P, KD, T], F32R)
        relu = at("relu", w0 + 3 * D, [P, 2, 512])
        score = at("score", w0 + 4 * D, [P, TT, T])
        selected = at("selected", w0 + 4 * D + 512, [P, TT, T])
        conv_p = at("conv_p", w0 + 4 * D, [P, T])
        conv_m = at("conv_m", w0 + 4 * D + T, [P, T])
        y_tok = at("y_tok", w0 + 5 * D, [P, 512])
        ff_lo = at("ff_lo", w0, [P, KF, T], F32R)
        match = at("match", w0, [P, TT * NH, 2 * NKEY])
        query = at("query", w0 + 4 * D, [P, 2, 2, T])
        assert w0 + 5 * D + 512 + 2 * D <= SLAB
        full = at("full", w0 + 5 * D + 512, [P, 4, 512])
        consts = sb("consts", [P, NCONST])
        params = sb("params", [P, NPARAM])
        gain2 = sb("gain2", [P, D])
        tmp = gain2[:, :].rearrange("p (b n) -> p b n", b=2)
        s_work = gain2[:, 0:4 * NKEY].rearrange("p (s w n) -> p s w n", s=2, w=2)
        cand = gain2[:, 4 * NKEY:4 * NKEY + 512].rearrange("p (s n) -> p s n", s=2)

        sumsq = sb("sumsq", [P, 2 * NNORM])
        var = sb("var", [P, 2 * NNORM])
        root = sb("root", [P, 2 * NNORM])
        rstd = sb("rstd", [P, 2 * NNORM])
        little = sb("little", [P, 24])
        flag, spare = little[:, 0:1], little[:, 1:9]
        final_ss = little[:, 9:13].rearrange("p (t h) -> p t h", t=TT)
        top8 = little[:, 13:21]
        wi = sb("wi", [P, TT, NH])
        negmax = sb("negmax", [P, 3, TT, NH])
        den = sb("den", [P, 3, TT, NH])
        rden = sb("rden", [P, 3, TT, NH])
        head_ss = sb("head_ss", [P, 2, NH])
        head_var = sb("head_var", [P, 2, NH])
        head_root = sb("head_root", [P, 2, NH])
        head_rstd = sb("head_rstd", [P, 2, NH])
        turn_tab = sb("turn_tab", [P, TT, 4, HD])
        s_top = sb("s_top", [P, 2, ETOP])
        s_idx = sb("s_idx", [P, 2, ETOP], U32)
        c_top = sb("c_top", [P, 3, ETOP])
        c_pos = sb("c_pos", [P, ETOP], U32)
        c_digit = sb("c_digit", [P, 2, ETOP], U32)
        c_part = sb("c_part", [P, 2, ETOP])
        expert = sb("expert", [P, 3, ETOP], U32)
        c_scalars = sb("c_scalars", [P, 3, 3, 1])
        c_neg, c_sum, c_rs = (c_scalars[:, i] for i in range(3))
        c_exp = sb("c_exp", [P, 3, ETOP])
        dots = sb("dots", [P, ETOP])
        gelu = sb("gelu", [P, ETOP])
        mixw = sb("mixw", [P, ETOP])

        ident = consts[:, C_ID:C_ID + P]
        mean_w = consts[:, C_MEAN:C_MEAN + P]
        iota = consts[:, C_IOTA:C_IOTA + 16]
        final_gain = consts[:, C_LOGC:C_LOGC + D]
        keysT = params[:, G_KEYS:G_KEYS + 2 * NKEY].rearrange("p (w n) -> p w n", w=2)

        def table(at, t, n=HD):
            return consts[:, at + t * n:at + (t + 1) * n]

        filled = [sem(f"filled_bank{b}") for b in range(7)]
        emptied = [sem(f"emptied_bank{b}") for b in range(7)]
        banks = [ctx.enter_context(nc.psum_tensor(f"bank{b}", [P, 512], F32)) for b in range(8)]
        y_bank = banks[7]
        ps = Psum(banks, filled, emptied)
        plan_psum(ps)
        weight_in = [sem(f"weight_in{r}") for r in range(RING)]
        x_in_done = [sem(f"x_in{t}") for t in range(TT)]
        consts_done = sem("consts_in")
        tables_done = sem("tables_in")
        gain2_done = sem("gain2_in")
        norm_final_done = sem("norm_final_in")
        final_done = sem("final_gain_in")
        sumsq_done = sem("sumsq_done")
        var_done = sem("var_done")
        residual_done = sem("residual_done")
        merged_done = sem("merged_done")
        root_done = sem("root_done")
        normed = sem("normed")
        rotated_done = sem("rotated_done")
        relu_used = sem("relu_used")
        max_done = sem("max_done")
        exp_done = sem("exp_done")
        pv_done = sem("pv_done")
        y_emptied = sem("y_emptied")
        gate_done = sem("gate_done")
        part_read = sem("part_read")
        high_done = sem("high_done")
        split_done = sem("split_done")
        late_split_done = sem("late_split_done")
        ht_full = sem("ht_full")
        ht_high = sem("ht_high")
        ht_done = sem("ht_done")
        y_high = sem("y_high")
        ff_full = sem("ff_full")
        ff_high = sem("ff_high")
        ff_done = sem("ff_done")
        act_step = sem("act_step")
        dve_step = sem("dve_step")
        head_sq_done = sem("head_sq_done")
        head_var_done = sem("head_var_done")
        head_root_done = sem("head_root_done")
        conv_sig = sem("conv_sig")
        conv_done = sem("conv_done")
        center_done = sem("center_done")
        square_done = sem("square_done")
        lvar_done = sem("lvar_done")
        lroot_done = sem("lroot_done")
        lnorm_done = sem("lnorm_done")
        pool_step = sem("pool_step")
        tap_diag_done = sem("tap_diag_done")
        gained = sem("gained")
        conv_high = sem("conv_high")
        conv_out = sem("conv_out")
        match_done = sem("match_done")
        u_free = sem("u_batches_free")
        v_free = sem("v_batches_free")
        u_in = [sem(f"u_in{b}") for b in range(UROWS // 2)]
        v_in = [sem(f"v_in{b}") for b in range(VROWS // 2)]
        experts_ready = sem("experts_ready")
        cexp_done = sem("cexp_done")
        gelu_done = sem("gelu_done")
        mixw_done = sem("mixw_done")
        diag_done = sem("diag_done")
        share_done = sem("share_done")
        fout_done = sem("fout_done")
        out_done = sem("out_done")

        def tap_weight(tap, c):
            return params[:, G_TAP + c * TAPS + tap:G_TAP + c * TAPS + tap + 1]

        def first_tap(eng, c):
            return eng.tensor_scalar(conv_a[:, c, :], conv_in[:, c, 0:T], tap_weight(0, c),
                                     params[:, G_CONV + c:G_CONV + c + 1], ALU.mult, ALU.add)

        def next_tap(eng, acc, tap, c):
            return eng.scalar_tensor_tensor(acc, conv_in[:, c, tap:tap + T], tap_weight(tap, c), acc, ALU.mult, ALU.add)

        def last_place(m):
            g = TT * NH - 1
            if 2 <= m < 2 + UROWS // 2:
                return u_rows[2 * (m - 2):2 * (m - 2) + 2], u_in[m - 2], 64 * (g + 1) + 32
            slot = m % 2
            return v_rows[2 * slot:2 * slot + 2], v_in[slot], g * ROW_STEP + (32 if m < 2 else 64)

        def was_read(eng, n):
            name = GRANULES[n]
            if name in READ_BY:
                ps.full(eng, READ_BY[name])
            else:
                eng.wait_ge(part_read, PARTIAL.index(name) + 1)

        block = ctx.enter_context(nc.Block())

        @block.sync
        def _(sp):
            sp.dma_start(X[:, 0, :], x_in[0:P, :]).then_inc(x_in_done[0], 16)
            sp.dma_start(raw[0][:, :], stream[0]).then_inc(weight_in[0], 16)
            sp.dma_start(X[:, 1, :], x_in[P:2 * P, :]).then_inc(x_in_done[1], 16)
            sp.dma_start(consts[:, 0:P], consts_in[:, 0:P]).then_inc(consts_done, 16)
            sp.dma_start(params[:, :], params_in).then_inc(consts_done, 16)
            sp.dma_start(raw[1][:, :], stream[1]).then_inc(weight_in[1], 16)
            sp.dma_start(consts[:, P:], consts_in[:, P:]).then_inc(tables_done, 16)
            sp.dma_start(raw[2][:, :], stream[2]).then_inc(weight_in[2], 16)
            rounds = NGRAN // RING
            with sp.Fori(1, rounds, 1) as q:
                for r in range(RING):
                    sp.wait_ge(split_done, q * RING + (r - RING + 1))
                    sp.dma_start(raw[r][:, :], stream[bass.ds(q * RING + r, 1), :, :].rearrange("g p n -> (g p) n")).then_inc(weight_in[r], 16)
            for n in range(rounds * RING, NGRAN):
                late = n - RING - (NGRAN - LATE)
                if late < 0:
                    sp.wait_ge(split_done, n - RING + 1)
                else:
                    sp.wait_ge(late_split_done, late + 1)
                sp.dma_start(raw[n % RING][:, :], stream[n]).then_inc(weight_in[n % RING], 16)
            for t in range(TT):
                for half in range(2):
                    cols = slice(half * 512, (half + 1) * 512)
                    sp.wait_ge(fout_done, 2 * t + half + 1)
                    sp.dma_start(out[t * P:(t + 1) * P, cols], X[:, t, cols]).then_inc(out_done, 16)
            sp.wait_ge(out_done, 2 * 16 * TT)

        @block.tensor
        def _(pe):
            mm = nc.tensor.matmul
            parts_read = [0]

            def mm3(out_ap, left, right, first, last, resumed=False):
                mm(out_ap, left[0], right[0], start=first, stop=False, skip_group_check=resumed)
                mm(out_ap, left[0], right[1], start=False, stop=False, skip_group_check=resumed)
                return mm(out_ap, left[1], right[0], start=False, stop=last, skip_group_check=resumed)

            def granule(name, k):
                n = GRANULES.index(name)
                if n < NGRAN - LATE:
                    pe.wait_ge(split_done, n + 1)
                else:
                    pe.wait_ge(late_split_done, n - (NGRAN - LATE) + 1)
                return [w[n % RING][:, :].rearrange("p (k n) -> p k n", k=k) for w in (w_hi, w_lo)]

            def cut(pair, *index):
                return [x[index] for x in pair]

            def partly_read(name, ins):
                assert PARTIAL[parts_read[0]] == name
                parts_read[0] += 1
                ins.then_inc(part_read, 1)

            hT = (hT_hi, hT_lo)
            yT = (yT_hi, yT_lo)
            everything = slice(None)

            def keep_warm(n):
                for _ in range(n):
                    mm(y_bank[:, 0:P], ident, ident, start=True, stop=True)

            def normed_turn(i):
                keep_warm(BRIDGE[i])
                for half in range(2):
                    for t in range(TT):
                        if half == 0:
                            pe.wait_ge(normed, TT * i + t + 1)
                        name = ("norm", i, t, half)
                        bank = ps.start(pe, name)
                        for c in range(4):
                            k = 4 * half + c
                            ins = nc.tensor.transpose(bank[:, c * P:(c + 1) * P], xs[:, t, k * P:(k + 1) * P], ident)
                        ps.fill(ins, name)

            def halves_of(fresh):
                if fresh is None:
                    return [range(KD)]

                def wait(half):
                    pe.wait_ge(ht_done, 4 * fresh + 2 * (half + 1))
                    return range(4 * half, 4 * half + 4)

                return (wait(half) for half in range(2))

            def tokens(name, granules, source, width=512, tail=(), fresh=None):
                opened = [ps.start(pe, (name, t) + tail) for t in range(TT)]
                n = width // len(granules)
                for i, gname in enumerate(granules):
                    w = [x[:, :, 0:n] for x in granule(gname, KD)] if n == T else small_cols(gname)
                    for chunks in halves_of(None if i else fresh):
                        for t in range(TT):
                            ins = token_part(opened[t][:, i * n:(i + 1) * n], source, t, w, chunks)
                            if gname in READ_BY and chunks[-1] == KD - 1:
                                ps.fill(ins, (name, t) + tail)
                    if gname not in READ_BY:
                        partly_read(gname, ins)

            def token_part(out_ap, source, t, w, chunks, beside=False):
                for k in chunks:
                    ins = mm3(out_ap, cut(source, everything, k, slice(t * P, (t + 1) * P)), cut(w, everything, k),
                              k == 0 and not beside, k == chunks[-1], beside or chunks[0] > 0)
                return ins

            def small_cols(gname):
                n = GRANULES.index(gname)
                granule(gname, KD)
                return [w[n % RING][:, 0:KD * SMALL].rearrange("p (k n) -> p k n", k=KD) for w in (w_hi, w_lo)]

            def channels(bank, c, w, col, source, chunks, first=0, beside=False):
                for k in chunks:
                    ins = mm3(bank[:, c * T:(c + 1) * T], cut(w, everything, k - first, slice(col, col + P)),
                              cut(source, everything, k), k == first and not beside, k == chunks[-1],
                              beside or chunks[0] > first)
                return ins

            def pair(gname, name, fresh=None):
                w = granule(gname, KD)
                bank = ps.start(pe, name)
                for chunks in halves_of(fresh):
                    for c in range(2):
                        ins = channels(bank, c, w, c * P, hT, chunks, beside=c == 1)
                ps.fill(ins, name)

            def turn(source, name, n):
                bank = ps.start(pe, name)
                for c in range(n):
                    ins = nc.tensor.transpose(bank[:, c * P:(c + 1) * P], source(c), ident)
                ps.fill(ins, name)

            def turn_queries(name, b, count, tiles=range(TT)):
                for t in tiles:
                    pe.wait_ge(rotated_done, count + t)
                    turn(lambda c: rotated[:, b, t, c * P:(c + 1) * P], ("turn", name, t), 4)

            pe.wait_ge(consts_done, 32)
            normed_turn(0)
            tokens("qi", ("qi0", "qi1"), hT, fresh=0)
            tokens("small", ("small",), hT, SMALL)
            tokens("qb", ("qb0", "qb1"), hT)
            turn_queries("qi", 0, 1)
            pe.wait_ge(rotated_done, 4)
            turn(lambda c: rotated[:, 1, c % 2, (c // 2) * P:(c // 2 + 1) * P], ("turn", "k"), 4)
            tokens("qa", ("qa0", "qa1"), hT)
            turn_queries("qb", 0, 5)

            def index_unit(n):
                t, heads = IDX_UNITS[n]
                nk = (t + 1) * P
                bank = ps.start(pe, ("index", n))
                for i, h in enumerate(heads):
                    rows = slice(HD * (h % 2), HD * (h % 2) + HD)
                    ins = mm(bank[:, i * nk:(i + 1) * nk], qT["qi"][rows, h // 2, t * P:(t + 1) * P],
                             kT[rows, 0, 0:nk], start=True, stop=True)
                ps.fill(ins, ("index", n))

            for t in range(TT):
                ps.copied(pe, ("turn", "qi", t))
            ps.copied(pe, ("turn", "k"))
            for n in range(3):
                index_unit(n)
            tokens("ka", ("ka0", "ka1"), hT)
            for n in range(3, 6):
                index_unit(n)
            turn_queries("qa", 1, 7)
            tokens("va", ("va0", "va1"), hT)
            turn_queries("ka", 0, 9)

            def attention(kind, index, queries, key_of, value_of):
                todo = units(kind)
                for s in range(len(todo) + 2):
                    if kind == "G" and s == 2:
                        turn_queries("q2", 1, 13, tiles=[1])
                    if kind == "G" and s == 4:
                        ps.copied(pe, ("turn", "q2", 1))
                    if s < len(todo):
                        _, t, j = todo[s]
                        nk = nkeys(kind, t) * P
                        bank = ps.start(pe, ("scores",) + todo[s])
                        for i, h in enumerate(pair_of(j)):
                            rows = slice(HD * (h % 2), HD * (h % 2) + HD)
                            ins = mm(bank[:, i * nk:(i + 1) * nk], queries[rows, h // 2, t * P:(t + 1) * P],
                                     key_of(h)[rows, 0:nk], start=True, stop=True)
                        ps.fill(ins, ("scores",) + todo[s])
                    f = gate_beside(kind, s)
                    if f is not None:
                        pair(f"gate{f}", ("gate", f))
                    if 1 <= s < 9:
                        _, t, j = todo[s - 1]
                        nb = nkeys(kind, t)
                        pe.wait_ge(exp_done, 8 * index + s)
                        turn(lambda c: E_sb[:, (s - 1) % 2, c * P:(c + 1) * P], ("probs",) + todo[s - 1], 2 * nb)
                    if s == 7:
                        turn_y(kind, index, 0)
                    if s >= 2:
                        _, t, j = todo[s - 2]
                        nb = nkeys(kind, t)
                        ps.copied(pe, ("probs",) + todo[s - 2])
                        if j == 0 and 2 * index + t:
                            pe.wait_ge(y_emptied, 2 * index + t)
                        for i, h in enumerate(pair_of(j)):
                            for kb in range(nb):
                                ins = mm(y_bank[:, h * HD:(h + 1) * HD], PT[:, (s - 2) % 2, (i * nb + kb) * P:(i * nb + kb + 1) * P],
                                         value_of(kb, h), start=kb == 0, stop=kb == nb - 1)
                        ins.then_inc(pv_done, 1)
                    if kind == "G":
                        taps(range(FIRST_TAPS + s * 2, min(FIRST_TAPS + s * 2 + 2, PE_TAPS)))
                turn_y(kind, index, 1)

            FIRST_TAPS = PE_TAPS - 2 * (len(units("G")) + 2)

            def taps(steps):
                for i in steps:
                    if i == 0:
                        pe.wait_ge(tap_diag_done, 1)
                        ps.copied(pe, ("conv", 3))
                        ps.start(pe, ("taps",))
                    ins = mm(ps.bank(("taps",))[:, 0:T], tap_diag[i], conv_in[:, 3, TAPS - PE_TAPS + i:TAPS - PE_TAPS + i + T],
                             start=i == 0, stop=i == PE_TAPS - 1)
                    if i == PE_TAPS - 1:
                        ps.fill(ins, ("taps",))

            def turn_y(kind, index, t):
                pe.wait_ge(y_emptied, 2 * index + t + 1)
                turn(lambda c: y_tok[:, c * P:(c + 1) * P], ("y", kind, t), 4)

            for name in ("qa", "ka"):
                for t in range(TT):
                    ps.copied(pe, ("turn", name, t))
            for t in range(TT):
                ps.copied(pe, ("va", t))
            attention("A", 0, qT["qa"], lambda h: qT["ka"][:, h // 2, :], lambda kb, h: va[:, kb, h * HD:(h + 1) * HD])
            for t in range(TT):
                ps.copied(pe, ("turn", "qb", t))
            attention("B", 1, qT["qb"], lambda h: kT[:, 1, :], lambda kb, h: vb[:, kb, :])

            for kind in "AB":
                for t in range(TT):
                    ps.copied(pe, ("y", kind, t))
            for c in range(KD):
                w = granule(f"up{c // 2}", KD)
                bank = ps.start(pe, ("up", c))
                for i in range(2):
                    part = [x[:, 4 * i:4 * i + 4, :] for x in w]
                    ins = channels(bank, i, part, (c % 2) * P, yT, range(4 * i, 4 * i + 4), 4 * i)
                ps.fill(ins, ("up", c))

            pe.wait_ge(merged_done, KD)
            for half in range(2):
                tokens("out", (f"wo{2 * half}", f"wo{2 * half + 1}"), (merged_hi, merged_lo), tail=(half,))

            normed_turn(1)
            for j in range(KF // 2):
                pair(f"ffg{j}", ("ffg", j), fresh=None if j else 1)
                pair(f"ffu{j}", ("ffu", j))
            accs = [[ps.start(pe, ("down", t, half)) for half in range(2)] for t in range(TT)]
            for j in range(KF // 2):
                w = granule(f"dn{j}", 2)
                pe.wait_ge(ff_done, j + 1)
                for t in range(TT):
                    for half in range(2):
                        for i in range(2):
                            k = 2 * j + i
                            ins = mm3(accs[t][half][:, :], cut((ff_hi, ff_lo), everything, k, slice(t * P, (t + 1) * P)),
                                      cut(w, everything, i, slice(half * 512, (half + 1) * 512)), k == 0, k == KF - 1)
                        if j == KF // 2 - 1:
                            ps.fill(ins, ("down", t, half))
                if j < KF // 2 - 1:
                    partly_read(f"dn{j}", ins)

            normed_turn(2)
            for c in range(CC):
                pair(f"conv{c}", ("conv", c), fresh=None if c else 2)
            tokens("kv2", ("kv",), hT, T)
            tokens("q2", ("q20", "q21"), hT)
            pe.wait_ge(rotated_done, 12)
            turn(lambda c: rotated[:, 0, c % 2, (c // 2) * P:(c // 2 + 1) * P], ("turn", "k2"), 4)
            turn_queries("q2", 1, 13, tiles=[0])
            taps(range(0, FIRST_TAPS))
            ps.copied(pe, ("turn", "k2"))
            ps.copied(pe, ("turn", "q2", 0))
            attention("G", 2, qT["q2"], lambda h: kT[:, h // 4, :], lambda kb, h: v2[:, kb, (h // 4) * HD:(h // 4 + 1) * HD])
            keep_warm(BRIDGE["mean"])
            bank = ps.start(pe, ("mean",))
            for c in range(CC):
                if c % 2 == 0:
                    pe.wait_ge(conv_done, c // 2 + 1)
                ins = mm(bank[:, 0:T], mean_w, conv_a[:, c, :], start=c == 0, stop=c == CC - 1)
            ps.fill(ins, ("mean",))
            def half_sum(q, chunks):
                w = granule(f"wp{q}", KD)
                for t in range(TT):
                    ins = token_part(ps.bank(("out2", t, q // 2))[:, (q % 2) * T:(q % 2 + 1) * T], yT, t, w, chunks,
                                     beside=q % 2 == 1)
                    if chunks[-1] == KD - 1 and q % 2:
                        ps.fill(ins, ("out2", t, q // 2))
                if chunks[-1] == KD - 1 and q % 2 == 0:
                    partly_read(f"wp{q}", ins)

            for t in range(TT):
                ps.copied(pe, ("y", "G", t))
                ps.start(pe, ("out2", t, 0))
            half_sum(0, range(4))
            bank = ps.start(pe, ("var",))
            for c in range(CC):
                if c % 2 == 0:
                    pe.wait_ge(square_done, c // 2 + 1)
                ins = mm(bank[:, 0:T], mean_w, conv_b[:, c, :], start=c == 0, stop=c == CC - 1)
            ps.fill(ins, ("var",))
            for t in range(TT):
                ps.start(pe, ("out2", t, 1))
            half_sum(1, range(4))
            half_sum(2, range(4))
            keep_warm(BRIDGE["branch"])
            pe.wait_ge(conv_out, 2)
            for q in range(3):
                half_sum(q, range(4, KD))
            half_sum(3, range(KD))

            normed_turn(3)

            def key_scores(h):
                ps.copied(pe, ("query", h))
                bank = ps.start(pe, ("match", h), freed=(match_done, h - 1) if h >= 2 else None)
                for t in range(TT):
                    for i in range(2):
                        at = (2 * t + i) * NKEY
                        ins = mm(bank[:, at:at + NKEY], query[:, h % 2, i, t * P:(t + 1) * P], keysT[:, i, :],
                                 start=True, stop=True)
                ps.fill(ins, ("match", h))

            for h in range(NH):
                pair(f"wq{h}", ("query", h), fresh=None if h else 3)
                for m in scored_after(h):
                    key_scores(m)

            def add_rows(accs, m, rows):
                for i, row in enumerate(rows):
                    for half in range(2):
                        ins = mm(accs[half][:, :], diag[:, 2 * m + i, :], row[:, half * 512:(half + 1) * 512],
                                 start=False, stop=True, skip_group_check=True)
                return ins

            for t in range(TT):
                accs = [ps.start(pe, ("mix", t, half)) for half in range(2)]
                for half in range(2):
                    mm(accs[half][:, :], ident, X[:, t, half * 512:(half + 1) * 512], start=True, stop=True)
                with pe.Fori(t * NH, (t + 1) * NH - t, 1) as g:
                    for m in range(BATCHES):
                        slot = m % (VROWS // 2)
                        pe.wait_ge(v_in[slot], g * ROW_STEP + 32 * (m // (VROWS // 2) + 1))
                        if m % 2 == 0:
                            pe.wait_ge(diag_done, g * 4 + (m // 2 + 1))
                        add_rows(accs, m, v_rows[2 * slot:2 * slot + 2]).then_inc(v_free, 1)
            g = TT * NH - 1
            pe.wait_ge(diag_done, 4 * (g + 1))
            for m in range(BATCHES):
                if m == BATCHES - 1:
                    pe.wait_ge(share_done, 1)
                    for half in range(2):
                        mm(accs[half][:, :], ident, hn[:, 0, half * 512:(half + 1) * 512], start=False, stop=True,
                           skip_group_check=True)
                if m not in SHARE:
                    rows, arrived, value = last_place(m)
                    pe.wait_ge(arrived, value)
                    ins = add_rows(accs, m, rows)
                    if m < 2:
                        ins.then_inc(v_free, 1)
            ins.then_inc(v_free, BATCHES - 2)

        @block.scalar
        def _(act):
            activation = nc.scalar.activation
            steps = [0]

            def settle(ins):
                steps[0] += 1
                ins.then_inc(act_step, 1)
                act.wait_ge(act_step, steps[0])

            warmed = [0]

            def warm(function):
                activation(spare[:, warmed[0]:warmed[0] + 1], consts[:, C_IOTA + 1:C_IOTA + 2], function)
                warmed[0] += 1

            def norm_sums(i):
                if i:
                    warm(ACT.Sqrt)
                for t in range(TT):
                    if i == 0:
                        act.wait_ge(x_in_done[t], 16)
                    else:
                        act.wait_ge(residual_done, TT * (i - 1) + t + 1)
                    activation(full[:, 2 * t:2 * t + 2, :].rearrange("p c t -> p (c t)"), X[:, t, :], ACT.Square,
                               accum_out=sumsq[:, TT * i + t:TT * i + t + 1]).then_inc(sumsq_done, 1)
                    act.wait_ge(var_done, TT * i + t + 1)
                    activation(root[:, TT * i + t:TT * i + t + 1], var[:, TT * i + t:TT * i + t + 1],
                               ACT.Sqrt).then_inc(root_done, 1)
                    if i == t == 0:
                        prepare("qi0", 0)

            def both_sums():
                warm(ACT.Sqrt)
                for t in range(TT):
                    for i, source in ((2, X), (3, hn)):
                        if i == 2:
                            act.wait_ge(residual_done, TT + t + 1)
                        else:
                            act.wait_ge(gained, t + 1)
                        place = full[:, 2 * (i - 2):2 * (i - 2) + 2, :].rearrange("p c t -> p (c t)")
                        if t:
                            act.wait_ge(sumsq_done, TT * 2 + i - 1)
                        activation(place, source[:, t, :], ACT.Square,
                                   accum_out=sumsq[:, TT * i + t:TT * i + t + 1]).then_inc(sumsq_done, 1)
                act.wait_ge(var_done, TT * 4)
                activation(root[:, TT * 2:TT * 4], var[:, TT * 2:TT * 4], ACT.Sqrt).then_inc(root_done, 2 * TT)

            prepared = [0]

            def prepare(name, ahead=RING - 1):
                while prepared[0] <= min(GRANULES.index(name) + ahead, NGRAN - 1):
                    n = prepared[0]
                    act.wait_ge(weight_in[n % RING], 16 * (n // RING + 1))
                    if n >= RING:
                        was_read(act, n - RING)
                    activation(w_hi[n % RING][:, :], raw[n % RING][:, :], ACT.Copy).then_inc(high_done, 1)
                    prepared[0] += 1

            def high_of_norm(i):
                for half in range(2):
                    for t in range(TT):
                        piece = 2 * half + t
                        act.wait_ge(ht_full, 4 * i + piece + 1)
                        activation(hT_hi[:, 4 * half:4 * half + 4, t * P:(t + 1) * P],
                                   full[:, piece, :].rearrange("p (c t) -> p c t", c=4), ACT.Copy).then_inc(ht_high, 1)

            def high_of_y(kind, base, t):
                bank = ps.full(act, ("y", kind, t))
                activation(yT_hi[:, base:base + 4, t * P:(t + 1) * P], bank[:, :].rearrange("p (c t) -> p c t", c=4),
                           ACT.Copy).then_inc(y_high, 1)

            def copy_turned(name, out_ap):
                bank = ps.full(act, name)
                ps.empty(activation(out_ap, bank[:, :].rearrange("p (c t) -> p c t", c=4), ACT.Copy), name)

            def index_relu(n):
                bank = ps.full(act, ("index", n))
                if n >= 2:
                    act.wait_ge(relu_used, n - 1)
                ps.empty(activation(relu[:, n % 2, :], bank[:, :], ACT.Relu), ("index", n))

            def attention(kind, index, base):
                todo = units(kind)
                for s in range(len(todo) + 1):
                    if kind == "G" and s == 2:
                        copy_turned(("turn", "q2", 1), qT["q2"][:, :, P:T])
                    if s < len(todo):
                        _, t, j = todo[s]
                        nk = nkeys(kind, t) * P
                        act.wait_ge(max_done, 8 * index + s + 1)
                        if s >= 2:
                            ps.full(act, ("probs",) + todo[s - 2])
                        for i, h in enumerate(pair_of(j)):
                            source = ps.bank(("scores",) + todo[s]) if kind == "G" else S_sb[:, s % 2, :]
                            ins = activation(E_sb[:, s % 2, i * nk:(i + 1) * nk], source[:, i * nk:(i + 1) * nk], ACT.Exp,
                                             bias=negmax[:, index, t, h:h + 1], scale=SCALE if kind == "G" else 1.0,
                                             accum_out=den[:, index, t, h:h + 1])
                        ins.then_inc(exp_done, 1)
                    if s == 8:
                        high_of_y(kind, base, 0)
                    f = gate_beside(kind, s)
                    if f is not None:
                        prepare(f"gate{f}")
                        bank = ps.full(act, ("gate", f))
                        ps.empty(activation(gates[:, 2 * f:2 * f + 2, :], bank[:, :].rearrange("p (c t) -> p c t", c=2),
                                            ACT.Copy), ("gate", f))
                    if s >= 1:
                        name = ("probs",) + todo[s - 1]
                        n = 2 * nkeys(kind, todo[s - 1][1]) * P
                        bank = ps.full(act, name)
                        if s >= 3:
                            act.wait_ge(pv_done, 8 * index + s - 2)
                        ps.empty(activation(PT[:, (s - 1) % 2, 0:n], bank[:, 0:n], ACT.Copy), name)
                if kind == "B":
                    prepare("gate7", RING)
                high_of_y(kind, base, 1)

            def sigmoid_of_gates(half):
                for f in (4, 5) if half == 0 else (6, 7):
                    ps.copied(act, ("gate", f))
                part = gates[:, :, :].rearrange("p (g c) t -> p g (c t)", g=2)[:, :, half * 4 * T:(half + 1) * 4 * T]
                activation(part, part, ACT.Sigmoid).then_inc(gate_done, 1)

            norm_sums(0)
            high_of_norm(0)
            prepare("qb1")
            for t in range(TT):
                copy_turned(("turn", "qi", t), qT["qi"][:, :, t * P:(t + 1) * P])
            name = ("turn", "k")
            ps.empty(activation(kT[:, :, :].rearrange("p w t -> p (w t)"), ps.full(act, name)[:, :], ACT.Copy), name)
            prepare("qa1")
            for t in range(TT):
                copy_turned(("turn", "qb", t), qT["qb"][:, :, t * P:(t + 1) * P])
            for n in range(3):
                index_relu(n)
            prepare("ka1")
            for n in range(3, 6):
                index_relu(n)
            for t in range(TT):
                copy_turned(("turn", "qa", t), qT["qa"][:, :, t * P:(t + 1) * P])
            prepare("va1")
            for t in range(TT):
                bank = ps.full(act, ("va", t))
                ps.empty(activation(va[:, t, :], bank[:, :], ACT.Copy), ("va", t))
            for t in range(TT):
                copy_turned(("turn", "ka", t), qT["ka"][:, :, t * P:(t + 1) * P])
            attention("A", 0, 0)
            attention("B", 1, 4)
            sigmoid_of_gates(0)
            sigmoid_of_gates(1)
            prepare("wo3")
            norm_sums(1)
            act.dma_start(gain2[:, :], norm_final).then_inc(norm_final_done, 16)
            high_of_norm(1)

            def high_of_ff(j):
                act.wait_ge(ff_full, j + 1)
                activation(ff_hi[:, 2 * j:2 * j + 2, :], full[:, j % 4, :].rearrange("p (c t) -> p c t", c=2),
                           ACT.Copy).then_inc(ff_high, 1)

            for j in range(KF // 2):
                prepare(f"ffg{j}")
                bank = ps.full(act, ("ffg", j))
                if j >= 4:
                    act.wait_ge(ff_done, j - 3)
                ps.empty(activation(full[:, j % 4, :], bank[:, :], ACT.Silu), ("ffg", j))
                prepare(f"ffu{j}")
                if j:
                    high_of_ff(j - 1)
            high_of_ff(KF // 2 - 1)
            prepare(f"dn{KF // 2 - 1}")
            both_sums()
            high_of_norm(2)

            for c in range(CC):
                prepare(f"conv{c}")
                bank = ps.full(act, ("conv", c))
                activation(conv_b[:, c, :], bank[:, T:2 * T], ACT.Sigmoid).then_inc(conv_sig, 1)
            for n in range(2 * TT):
                t = n % TT
                name, cols = (("kv2", t), 2 * HD) if n < TT else (("q2", t), NH * HD)
                prepare("kv" if n < TT else "q21")
                bank = ps.full(act, name)
                if n >= 2:
                    act.wait_ge(head_var_done, n - 1)
                activation(relu[:, n % 2, 0:cols], bank[:, 0:cols], ACT.Square).then_inc(head_sq_done, 1)
                act.wait_ge(head_var_done, n + 1)
                nh = cols // HD
                activation(head_root[:, n % 2, 0:nh], head_var[:, n % 2, 0:nh], ACT.Sqrt).then_inc(head_root_done, 1)
            prepare("q21", RING)
            name = ("turn", "k2")
            ps.empty(activation(kT[:, :, :].rearrange("p w t -> p (w t)"), ps.full(act, name)[:, :], ACT.Copy), name)
            copy_turned(("turn", "q2", 0), qT["q2"][:, :, 0:P])
            attention("G", 2, 0)
            for half in range(2):
                act.wait_ge(center_done, half + 1)
                pair = slice(2 * half, 2 * half + 2)
                activation(conv_b[:, pair, :], conv_a[:, pair, :], ACT.Square).then_inc(square_done, 1)
            warm(ACT.Sqrt)
            act.wait_ge(lvar_done, 1)
            activation(rstd_c[:, 1, :], rstd_c[:, 0, :], ACT.Sqrt).then_inc(lroot_done, 1)
            warm(ACT.Silu)
            for half in range(2):
                act.wait_ge(lnorm_done, half + 1)
                for c in range(2 * half, 2 * half + 2):
                    ins = activation(conv_b[:, c, :], conv_a[:, c, :], ACT.Silu,
                                     bias=params[:, G_CONV + 2 * CC + c:G_CONV + 2 * CC + c + 1],
                                     scale=params[:, G_CONV + CC + c:G_CONV + CC + c + 1])
                settle(ins)
                activation(yT_hi[:, 4 + 2 * half:6 + 2 * half, :], conv_b[:, 2 * half:2 * half + 2, :], ACT.Copy).then_inc(conv_high, 1)
            act.dma_start(gain2[:, :], norm2_g).then_inc(gain2_done, 16)
            act.dma_start(final_gain, final_g).then_inc(final_done, 16)
            prepare("wp3")
            norm_sums(4)
            high_of_norm(3)

            def copy_query(h):
                bank = ps.full(act, ("query", h))
                if h >= 2:
                    ps.full(act, ("match", h - 2))
                ps.empty(activation(query[:, h % 2, :, :], bank[:, :].rearrange("p (w t) -> p w t", w=2), ACT.Copy), ("query", h))

            def copy_match(h):
                bank = ps.full(act, ("match", h))
                out_ap = match[:, :, :].rearrange("p (t h) n -> p t h n", t=TT)[:, :, h, :]
                activation(out_ap, bank[:, :].rearrange("p (t n) -> p t n", t=TT), ACT.Copy)\
                    .then_inc(match_done, 1 if h < NH - 1 else 1 + NH)

            for h in range(NH):
                prepare(f"wq{h}")
                copy_query(h)
                for m in scored_after(h):
                    copy_match(m)

            def expert_weights(g, b, first=False):
                act.wait_ge(experts_ready, g + 1)
                activation(c_exp[:, b, :], c_top[:, b, :], ACT.Exp, bias=c_neg[:, b, :],
                           accum_out=c_sum[:, b, :]).then_inc(cexp_done, 1)
                act.wait_ge(u_free, g * BATCHES + (UROWS // 2 + BATCHES))
                activation(gelu[:, :], dots[:, :], ACT.Gelu_apprx_tanh).then_inc(gelu_done, 1)
                act.wait_ge(mixw_done, g + 1)
                for q in range(4):
                    if not first:
                        act.wait_ge(v_free, g * BATCHES + (VROWS // 2 - BATCHES + 2 * q + 2))
                    for i in range(4 * q, 4 * q + 4):
                        ins = activation(diag[:, i, :], ident, ACT.Copy, scale=mixw[:, i:i + 1])
                    ins.then_inc(diag_done, 1)

            expert_weights(0, 0, first=True)
            with act.Fori(1, TT * NH, 3) as g0:
                for i in range(3):
                    expert_weights(g0 + i, (1 + i) % 3)
            warm(ACT.Sqrt)
            for t in range(TT):
                act.wait_ge(v_free, VROWS // 2 + BATCHES * NH * (t + 1))
                for half in range(2):
                    activation(full[:, 2 * t + half, :], ps.bank(("mix", t, half))[:, :], ACT.Square,
                               accum_out=final_ss[:, t, half:half + 1]).then_inc(sumsq_done, 1)
                n = TT * 5 + t
                act.wait_ge(var_done, n + 1)
                activation(root[:, n:n + 1], var[:, n:n + 1], ACT.Sqrt).then_inc(root_done, 1)

        @block.vector
        def _(dve):
            v = nc.vector
            steps = [0]
            loop_step = dve.alloc_register("dve_loop_step")
            in_loop = [False]

            def settle(ins):
                steps[0] += 1
                ins.then_inc(dve_step, 1)
                if in_loop[0]:
                    dve.wait_ge(dve_step, loop_step)
                    dve.reg_add(loop_step, loop_step, 1)
                else:
                    dve.wait_ge(dve_step, steps[0])

            def column(buf, n):
                return buf[:, n:n + 1]

            def row(ap, n, width):
                return ap.unsqueeze(1).broadcast_to([P, n, width])

            def each(ap, n, width):
                return ap.unsqueeze(2).broadcast_to([P, n, width])

            def norm_scale(i, t):
                n = TT * i + t
                dve.wait_ge(sumsq_done, n + 1)
                v.tensor_scalar(column(var, n), column(sumsq, n), 1.0 / D, EPS, ALU.mult, ALU.add).then_inc(var_done, 1)
                dve.wait_ge(root_done, n + 1)
                settle(v.reciprocal(column(rstd, n), column(root, n)))

            def norm(i):
                for t in range(TT):
                    norm_scale(TURNED[i], t)
                    v.tensor_scalar(xs[:, t, :], X[:, t, :], column(rstd, TT * TURNED[i] + t), None,
                                    ALU.mult).then_inc(normed, 1)
                turned_norm(i)

            def turned_norm(i):
                for half in range(2):
                    for t in range(TT):
                        name = ("norm", i, t, half)
                        bank = ps.full(dve, name)
                        at = G_NORM + 8 * i + 4 * half
                        ps.empty(v.tensor_tensor(full[:, 2 * half + t, :].rearrange("p (c t) -> p c t", c=4),
                                                 bank[:, :].rearrange("p (c t) -> p c t", c=4),
                                                 each(params[:, at:at + 4], 4, P), ALU.mult), name)
                        ps.copied(dve, name)
                        v.memset(flag[:, :], 0.0).then_inc(ht_full, 1)
                    for t in range(TT):
                        low_of_norm(i, 2 * half + t)

            def low_of_norm(i, piece):
                half, t = divmod(piece, 2)
                where = (slice(None), slice(4 * half, 4 * half + 4), slice(t * P, (t + 1) * P))
                dve.wait_ge(ht_high, 4 * i + piece + 1)
                v.tensor_tensor(hT_lo[where], full[:, piece, :].rearrange("p (c t) -> p c t", c=4),
                                hT_hi[where].bitcast(F32), ALU.subtract).then_inc(ht_done, 1)

            def residual(i, name, then=None):
                halves = [(t, half) for t in range(TT) for half in range(2)]
                if name != "down":
                    halves.sort(key=lambda x: x[1])
                for t, half in halves:
                    bank = ps.full(dve, (name, t, half))
                    part = X[:, t, half * 512:(half + 1) * 512]
                    ps.empty(v.tensor_tensor(part, part, bank[:, :], ALU.add), (name, t, half))
                    if half == 0:
                        continue
                    ps.copied(dve, (name, t, 0))
                    ps.copied(dve, (name, t, 1))
                    v.memset(flag[:, :], 0.0).then_inc(residual_done, 1)
                    dve.wait_ge(residual_done, TT * i + t + 1)
                    if then:
                        then(t)

            def rope(source, heads, t, out_ap, last):
                n = heads * HD
                a, b = tmp[:, 0, 0:n], tmp[:, 1, 0:n]
                halves = lambda ap: ap.rearrange("p (h w) -> p h w", h=2)
                settle(v.tensor_tensor(a.rearrange("p (h w) -> p h w", w=HD), source.rearrange("p (h w) -> p h w", w=HD),
                                       row(table(C_COS, t), heads, HD), ALU.mult))
                swapped = source.rearrange("p (h s w) -> p h s w", s=2, w=HD // 2)[:, :, ::-1, :]
                sine = table(C_SIN, t).rearrange("p (s w) -> p s w", s=2).unsqueeze(1).broadcast_to([P, heads, 2, HD // 2])
                ins = v.tensor_tensor(b.rearrange("p (h s w) -> p h s w", s=2, w=HD // 2), swapped, sine, ALU.mult)
                if last is not None:
                    ps.empty(ins, last)
                    ps.copied(dve, last)
                else:
                    settle(ins)
                if out_ap.shape == (P, n):
                    return v.tensor_tensor(out_ap, a, b, ALU.add)
                return v.tensor_tensor(out_ap, row(a, 2, n), row(b, 2, n), ALU.add)

            def rope_queries(name, b, before):
                for t in range(TT):
                    bank = ps.full(dve, (name, t))
                    if before is not None:
                        ps.full(dve, before(t))
                    rope(bank[:, :], NH, t, rotated[:, b, t, :], (name, t)).then_inc(rotated_done, 1)
                    rotated_count[0] += 1
                    dve.wait_ge(rotated_done, rotated_count[0])

            rotated_count = [0]

            dve.wait_ge(consts_done, 32)
            norm(0)
            dve.wait_ge(tables_done, 16)
            for t in range(TT):
                for w in range(2):
                    gain = params[:, G_QK + w * HD:G_QK + (w + 1) * HD]
                    v.tensor_tensor(turn_tab[:, t, 2 * w, :], table(C_ACOS, t), gain, ALU.mult)
                    four = lambda ap: ap.rearrange("p (g s w) -> p g s w", g=2, s=2)
                    last = v.tensor_tensor(four(turn_tab[:, t, 2 * w + 1, :]), four(table(C_ASIN, t)),
                                           four(gain)[:, :, ::-1, :], ALU.mult)
            settle(last)
            rope_queries("qi", 0, None)
            for t in range(TT):
                bank = ps.full(dve, ("small", t))
                v.tensor_copy(vb[:, t, :], bank[:, HD:2 * HD])
                v.tensor_copy(wi[:, t, :], bank[:, 3 * HD:SMALL])
                settle(rope(bank[:, 2 * HD:3 * HD], 1, t, rotated[:, 1, t, 0:P].rearrange("p (w n) -> p w n", w=2), None))
                rope(bank[:, 0:HD], 1, t, rotated[:, 1, t, P:2 * P].rearrange("p (w n) -> p w n", w=2),
                     ("small", t)).then_inc(rotated_done, 1)
                rotated_count[0] += 1
                dve.wait_ge(rotated_done, rotated_count[0])
            rope_queries("qb", 0, lambda t: ("turn", "qi", t))
            rope_queries("qa", 1, lambda t: ("turn", "k"))

            def index_sum(n):
                t, heads = IDX_UNITS[n]
                nk = (t + 1) * P
                ps.copied(dve, ("index", n))
                for i, h in enumerate(heads):
                    part = relu[:, n % 2, i * nk:(i + 1) * nk]
                    if h == 0:
                        ins = v.tensor_scalar(score[:, t, 0:nk], part, wi[:, t, 0:1], None, ALU.mult)
                    else:
                        ins = v.scalar_tensor_tensor(score[:, t, 0:nk], part, wi[:, t, h:h + 1], score[:, t, 0:nk],
                                                     ALU.mult, ALU.add)
                    if h != heads[-1]:
                        settle(ins)
                ins.then_inc(relu_used, 1)
                dve.wait_ge(relu_used, n + 1)

            for n in range(3):
                index_sum(n)
            rope_queries("ka", 0, lambda t: ("turn", "qb", t))
            for n in range(3, 6):
                index_sum(n)
            for t in range(TT):
                nk = (t + 1) * P
                settle(v.scalar_tensor_tensor(score[:, t, 0:nk], score[:, t, 0:nk], IDX_SCALE, table(C_CAUSAL, t, T)[:, 0:nk],
                                              ALU.mult, ALU.add))

            def select_round(t):
                nk = (t + 1) * P
                settle(v.max(top8[:, :], score[:, t, 0:nk]))
                settle(v.match_replace(score[:, t, 0:nk], top8[:, :], score[:, t, 0:nk], TAKEN))

            def select_mask(t):
                nk = (t + 1) * P
                settle(v.tensor_scalar(selected[:, t, 0:nk], score[:, t, 0:nk], TAKEN / 2, MASKED, ALU.is_gt, ALU.mult))
                settle(v.tensor_tensor(selected[:, t, 0:nk], selected[:, t, 0:nk], table(C_CAUSAL, t, T)[:, 0:nk], ALU.add))

            my_taps = [(tap, c) for tap in range(TAPS) for c in range(2)]
            my_taps += [(tap, c) for tap in range(TAPS) for c in (2, 3) if tap < TAPS - (POOL_TAPS if c == 2 else PE_TAPS)]
            at_step = {}

            def conv_taps(n):
                for tap, c in my_taps[:n]:
                    if tap == 0:
                        ins = first_tap(v, c)
                    else:
                        dve.wait_ge(dve_step, at_step[c])
                        ins = next_tap(v, conv_a[:, c, :], tap, c)
                    steps[0] += 1
                    at_step[c] = steps[0]
                    ins.then_inc(dve_step, 1)
                    if (tap, c) == (TAPS - 1, 1):
                        dve.wait_ge(dve_step, steps[0])
                        v.memset(flag[:, :], 0.0).then_inc(conv_done, 1)
                        dve.wait_ge(conv_done, 1)
                del my_taps[:n]

            def attention(kind, index, bias):
                todo = units(kind)
                for s in range(len(todo)):
                    _, t, j = todo[s]
                    nk = nkeys(kind, t) * P
                    name = ("scores",) + todo[s]
                    bank = ps.full(dve, name)
                    pair = negmax[:, index, t, pair_of(j)[0]:pair_of(j)[1] + 1:2]
                    if kind == "G":
                        settle(v.tensor_reduce(pair, bank[:, 0:2 * nk].rearrange("p (h n) -> p h n", h=2), AX_X, ALU.max))
                        v.tensor_scalar(pair, pair, -SCALE, None, ALU.mult).then_inc(max_done, 1)
                    else:
                        scaled = S_sb[:, s % 2, 0:2 * nk].rearrange("p (h n) -> p h n", h=2)
                        if s >= 2:
                            dve.wait_ge(exp_done, 8 * index + s - 1)
                        elif index:
                            dve.wait_ge(exp_done, 8 * index)
                        ps.empty(v.scalar_tensor_tensor(scaled, bank[:, 0:2 * nk].rearrange("p (h n) -> p h n", h=2), SCALE,
                                                        row(bias(t)[:, 0:nk], 2, nk), ALU.mult, ALU.add), name)
                        ps.copied(dve, name)
                        v.tensor_reduce(pair, scaled, AX_X, ALU.max, negate=True).then_inc(max_done, 1)
                    if s == 6 and kind == "G":
                        normalise(kind, index, 0)
                    if kind == "A":
                        for _ in range(TOPK // 8 // (NH // 2)):
                            select_round(s // 4)
                        if s % 4 == 3:
                            select_mask(s // 4)
                    if kind == "G":
                        conv_taps(4)
                        dve.wait_ge(exp_done, 8 * index + s + 1)
                        ps.empty(v.memset(flag[:, :], 0.0), name)
                        ps.copied(dve, name)
                    if s == 6 and kind != "G":
                        normalise(kind, index, 0)
                    if s == 7:
                        low_of_y(kind, index, 0)
                normalise(kind, index, 1)
                if kind == "G":
                    conv_end()
                low_of_y(kind, index, 1)

            def conv_end():
                conv_taps(len(my_taps))
                dve.wait_ge(dve_step, steps[0])
                dve.wait_ge(pool_step, 2 * POOL_TAPS - 1)
                v.tensor_tensor(conv_a[:, 2, :], conv_a[:, 2, :], conv_p[:, :], ALU.add)
                bank = ps.full(dve, ("taps",))
                ps.empty(v.tensor_tensor(conv_a[:, 3, :], conv_a[:, 3, :], bank[:, 0:T], ALU.add), ("taps",))
                ps.copied(dve, ("taps",))
                v.memset(flag[:, :], 0.0).then_inc(conv_done, 1)

            def low_of_y(kind, index, t):
                base = 4 if kind == "B" else 0
                where = (slice(None), slice(base, base + 4), slice(t * P, (t + 1) * P))
                dve.wait_ge(y_high, 2 * index + t + 1)
                ps.empty(v.tensor_tensor(yT_lo[where], ps.bank(("y", kind, t))[:, :].rearrange("p (c t) -> p c t", c=4),
                                         yT_hi[where].bitcast(F32), ALU.subtract), ("y", kind, t))

            def normalise(kind, index, t):
                dve.wait_ge(exp_done, 8 * index + 4 * t + 4)
                settle(v.reciprocal(rden[:, index, t, :], den[:, index, t, :]))
                dve.wait_ge(pv_done, 8 * index + 4 * t + 4)
                if index or t:
                    before = ("y", kind, 0) if t else ("y", "ABG"[index - 1], 1)
                    ps.full(dve, before)
                v.tensor_tensor(y_tok[:, :].rearrange("p (h n) -> p h n", h=NH), y_bank[:, :].rearrange("p (h n) -> p h n", h=NH),
                                each(rden[:, index, t, :], NH, HD), ALU.mult).then_inc(y_emptied, 1)

            attention("A", 0, lambda t: table(C_LOGC, t, T))
            attention("B", 1, lambda t: selected[:, t, :])

            for c in range(KD):
                bank = ps.full(dve, ("up", c))
                dve.wait_ge(gate_done, c // 4 + 1)
                t2 = tmp[:, c % 2, :].rearrange("p (g t) -> p g t", g=2)
                ps.empty(v.tensor_tensor(t2, bank[:, :].rearrange("p (g t) -> p g t", g=2),
                                         gates[:, :, :].rearrange("p (g c) t -> p g c t", g=2)[:, :, c, :], ALU.mult), ("up", c))
                ps.copied(dve, ("up", c))
                part = full[:, c % 4, 0:T]
                settle(v.tensor_tensor(part, t2[:, 0, :], t2[:, 1, :], ALU.add))
                settle(v.tensor_copy(merged_hi[:, c, :], part))
                v.tensor_tensor(merged_lo[:, c, :], part, merged_hi[:, c, :].bitcast(F32), ALU.subtract).then_inc(merged_done, 1)
                dve.wait_ge(merged_done, c + 1)
            residual(0, "out")
            norm(1)

            def low_of_ff(j):
                dve.wait_ge(ff_high, j + 1)
                part = (slice(None), slice(2 * j, 2 * j + 2))
                v.tensor_tensor(ff_lo[part], full[:, j % 4, :].rearrange("p (c t) -> p c t", c=2),
                                ff_hi[part].bitcast(F32), ALU.subtract).then_inc(ff_done, 1)

            for j in range(KF // 2):
                bank = ps.full(dve, ("ffu", j))
                ps.copied(dve, ("ffg", j))
                part = full[:, j % 4, :]
                ps.empty(v.tensor_tensor(part, part, bank[:, :], ALU.mult), ("ffu", j))
                ps.copied(dve, ("ffu", j))
                v.memset(flag[:, :], 0.0).then_inc(ff_full, 1)
                if j:
                    low_of_ff(j - 1)
            low_of_ff(KF // 2 - 1)
            for i in range(PE_TAPS):
                ins = v.tensor_scalar(tap_diag[i], ident, tap_weight(TAPS - PE_TAPS + i, 3), None, ALU.mult)
            ins.then_inc(tap_diag_done, 1)
            dve.wait_ge(norm_final_done, 16)
            residual(1, "down", then=lambda t: v.tensor_tensor(hn[:, t, :], X[:, t, :], gain2[:, :], ALU.mult).then_inc(gained, 1))
            first, second = slice(TT * 2, TT * 3), slice(TT * 3, TT * 4)
            dve.wait_ge(sumsq_done, TT * 4)
            v.tensor_scalar(root[:, second], sumsq[:, second], 1.0 / D, None, ALU.mult)
            settle(v.tensor_scalar(var[:, first], sumsq[:, first], 1.0 / D, EPS, ALU.mult, ALU.add))
            v.scalar_tensor_tensor(var[:, second], var[:, first], EPS, root[:, second], ALU.mult, ALU.add).then_inc(var_done, 2 * TT)
            dve.wait_ge(root_done, TT * 4)
            settle(v.reciprocal(rstd[:, TT * 2:TT * 4], root[:, TT * 2:TT * 4]))
            for t in range(TT):
                v.tensor_scalar(xs[:, t, :], hn[:, t, :], column(rstd, TT * 3 + t), None, ALU.mult).then_inc(normed, 1)
            turned_norm(2)
            for t in range(TT):
                v.tensor_scalar(X[:, t, :], hn[:, t, :], column(rstd, TT * 2 + t), None, ALU.mult).then_inc(residual_done, 1)

            def head_norm(n, bank, heads):
                b = n % 2
                dve.wait_ge(head_sq_done, n + 1)
                settle(v.tensor_reduce(head_ss[:, b, 0:heads], relu[:, b, 0:heads * HD].rearrange("p (h w) -> p h w", w=HD), AX_X, ALU.add))
                v.tensor_scalar(head_var[:, b, 0:heads], head_ss[:, b, 0:heads], 1.0 / HD, EPS, ALU.mult, ALU.add).then_inc(head_var_done, 1)
                dve.wait_ge(head_root_done, n + 1)
                settle(v.reciprocal(head_rstd[:, b, 0:heads], head_root[:, b, 0:heads]))
                ins = v.tensor_tensor(tmp[:, 0, 0:heads * HD].rearrange("p (h w) -> p h w", w=HD),
                                      bank[:, 0:heads * HD].rearrange("p (h w) -> p h w", w=HD),
                                      each(head_rstd[:, b, 0:heads], heads, HD), ALU.mult)
                return ins

            def axial(t, heads, w, a, b):
                z = tmp[:, 0, 0:heads * HD]
                v.tensor_tensor(a.rearrange("p (h w) -> p h w", w=HD), z.rearrange("p (h w) -> p h w", w=HD),
                                row(turn_tab[:, t, 2 * w, :], heads, HD), ALU.mult)
                for g in range(2):
                    five = lambda ap: ap.rearrange("p (h g s w) -> p h g s w", g=2, s=2, w=HD // 4)[:, :, g]
                    sine = turn_tab[:, t, 2 * w + 1, :].rearrange("p (g s w) -> p g s w", g=2, s=2)[:, g]
                    ins = v.tensor_tensor(five(b), five(z)[:, :, ::-1, :], sine.unsqueeze(1).broadcast_to([P, heads, 2, HD // 4]), ALU.mult)
                settle(ins)

            settle(v.memset(conv_in[:, :, 0:PAD], 0.0))
            settle(v.memset(conv_in[:, :, PAD + T:], 0.0))
            for c in range(CC):
                bank = ps.full(dve, ("conv", c))
                dve.wait_ge(conv_sig, c + 1)
                ps.empty(v.tensor_tensor(conv_in[:, c, PAD:PAD + T], bank[:, 0:T], conv_b[:, c, :], ALU.mult), ("conv", c))
                ps.copied(dve, ("conv", c))
                if c:
                    conv_taps(11)
            for t in range(TT):
                bank = ps.full(dve, ("kv2", t))
                dve.wait_ge(head_sq_done, t + 1)
                v.tensor_copy(v2[:, t, :], bank[:, 2 * HD:4 * HD])
                ins = head_norm(t, bank, 2)
                ps.empty(ins, ("kv2", t))
                ps.copied(dve, ("kv2", t))
                a, b = tmp[:, 1, 0:P], tmp[:, 1, P:2 * P]
                axial(t, 2, 1, a, b)
                pair = lambda ap: ap.rearrange("p (h w) -> p h w", h=2).unsqueeze(2).broadcast_to([P, 2, 2, HD])
                v.tensor_tensor(rotated[:, 0, t, 0:2 * P].rearrange("p (h s w) -> p h s w", h=2, s=2), pair(a), pair(b),
                                ALU.add).then_inc(rotated_done, 1)
                rotated_count[0] += 1
                dve.wait_ge(rotated_done, rotated_count[0])
                conv_taps(3)
            for t in range(TT):
                bank = ps.full(dve, ("q2", t))
                ins = head_norm(TT + t, bank, NH)
                ps.empty(ins, ("q2", t))
                ps.copied(dve, ("q2", t))
                axial(t, NH, 0, rotated[:, 1, t, :], tmp[:, 1, :])
                v.tensor_tensor(rotated[:, 1, t, :], rotated[:, 1, t, :], tmp[:, 1, :], ALU.add).then_inc(rotated_done, 1)
                rotated_count[0] += 1
                dve.wait_ge(rotated_done, rotated_count[0])
            attention("G", 2, None)
            bank = ps.full(dve, ("mean",))
            for half in range(2):
                pair = conv_a[:, 2 * half:2 * half + 2, :]
                ins = v.tensor_tensor(pair, pair, row(bank[:, 0:T], 2, T), ALU.subtract)
                if half == 0:
                    ins.then_inc(center_done, 1)
                else:
                    ps.empty(ins, ("mean",))
            ps.copied(dve, ("mean",))
            v.memset(flag[:, :], 0.0).then_inc(center_done, 1)
            bank = ps.full(dve, ("var",))
            ps.empty(v.tensor_scalar(rstd_c[:, 0, :], bank[:, 0:T], EPS, None, ALU.add), ("var",))
            ps.copied(dve, ("var",))
            v.memset(flag[:, :], 0.0).then_inc(lvar_done, 1)
            dve.wait_ge(lroot_done, 1)
            settle(v.reciprocal(rstd_c[:, 0, :], rstd_c[:, 1, :]))
            for half in range(2):
                pair = conv_a[:, 2 * half:2 * half + 2, :]
                v.tensor_tensor(pair, pair, row(rstd_c[:, 0, :], 2, T), ALU.mult).then_inc(lnorm_done, 1)
            for half in range(2):
                dve.wait_ge(conv_high, half + 1)
                rows = slice(4 + 2 * half, 6 + 2 * half)
                v.tensor_tensor(yT_lo[:, rows, :], conv_b[:, 2 * half:2 * half + 2, :], yT_hi[:, rows, :].bitcast(F32),
                                ALU.subtract).then_inc(conv_out, 1)
            residual(3, "out2")
            norm(3)
            dve.wait_ge(gain2_done, 16)
            for t in range(TT):
                ins = v.tensor_tensor(hn[:, t, :], xs[:, t, :], gain2[:, :], ALU.mult)
            settle(ins)
            v.memset(flag[:, :], 0.0).then_inc(u_free, UROWS // 2)
            dve.wait_ge(u_free, UROWS // 2)
            v.memset(flag[:, :], 0.0).then_inc(v_free, VROWS // 2)
            dve.wait_ge(v_free, VROWS // 2)

            def sorted_top(lists):
                for values, top, left, index in lists:
                    ins = v.max(top[:, 0:8], values)
                settle(ins)
                for values, top, left, index in lists:
                    ins = v.match_replace(left, top[:, 0:8], values, TAKEN)
                settle(ins)
                for values, top, left, index in lists:
                    v.max_index(index[:, 0:8], top[:, 0:8], values)
                    ins = v.max(top[:, 8:16], left)
                settle(ins)
                for values, top, left, index in lists:
                    ins = v.max_index(index[:, 8:16], top[:, 8:16], left)
                settle(ins)

            def choose(g, b):
                dve.wait_ge(match_done, g + 1)
                both = match[:, :, :].rearrange("p g n -> p (g n)")[:, bass.ds(g * 2 * NKEY, 2 * NKEY)]
                settle(v.tensor_copy(s_work[:, 0, :, :].rearrange("p w n -> p (w n)"), both))
                sorted_top([(s_work[:, 0, w, :], s_top[:, w, :], s_work[:, 1, w, :], s_idx[:, w, :]) for w in range(2)])
                square = lambda ap: ap.rearrange("p (a b) -> p a b", a=ETOP)
                settle(v.tensor_tensor(square(cand[:, 0, :]), each(s_top[:, 0, :], ETOP, ETOP), row(s_top[:, 1, :], ETOP, ETOP), ALU.add))
                sorted_top([(cand[:, 0, :], c_top[:, b, :], cand[:, 1, :], c_pos[:, :])])
                v.tensor_scalar(c_neg[:, b, :], c_top[:, b, 0:1], -1.0, None, ALU.mult)
                v.tensor_scalar(c_digit[:, 0, :], c_pos[:, :], 4, None, ALU.logical_shift_right)
                settle(v.tensor_scalar(c_digit[:, 1, :], c_pos[:, :], 15, None, ALU.bitwise_and))
                for w in range(2):
                    ins = v.tensor_tensor(square(cand[:, w, :]), each(c_digit[:, w, :], ETOP, ETOP), row(iota, ETOP, ETOP), ALU.is_equal)
                settle(ins)
                for w in range(2):
                    ins = v.tensor_tensor(square(cand[:, w, :]), square(cand[:, w, :]), row(s_idx[:, w, :], ETOP, ETOP), ALU.mult)
                settle(ins)
                for w in range(2):
                    ins = v.tensor_reduce(c_part[:, w, :], square(cand[:, w, :]), AX_X, ALU.add)
                settle(ins)
                v.scalar_tensor_tensor(expert[:, b, :], c_part[:, 0, :], float(NKEY), c_part[:, 1, :], ALU.mult,
                                       ALU.add).then_inc(experts_ready, 1)
                dve.wait_ge(experts_ready, g + 1)

            def group(g, b, t, more=True):
                if more:
                    for slot in range(VROWS // 2):
                        dve.wait_ge(v_in[slot], g * ROW_STEP - ROW_STEP)
                    choose(g + 1, (b + 1) % 3)
                dot_products(g, t, range(BATCHES))
                weights(g, b)

            def dot_products(g, t, batches):
                for m in batches:
                    slot = m % (UROWS // 2)
                    dve.wait_ge(u_in[slot], g * 64 + 32 * (m // (UROWS // 2) + 1))
                    for i in range(2):
                        row_of_u = u_rows[2 * slot + i][:, :]
                        ins = v.tensor_tensor_reduce(out=row_of_u, in0=row_of_u, in1=hn[:, t, :], scale=1.0, scalar=0.0,
                                                     op0=ALU.mult, op1=ALU.add, accum_out=dots[:, 2 * m + i:2 * m + i + 1])
                    ins.then_inc(u_free, 1)

            def weights(g, b):
                dve.wait_ge(cexp_done, g + 1)
                settle(v.reciprocal(c_rs[:, b, :], c_sum[:, b, :]))
                dve.wait_ge(gelu_done, g + 1)
                if not (isinstance(g, int) and g == 0):
                    dve.wait_ge(diag_done, g * 4)
                v.scalar_tensor_tensor(mixw[:, :], c_exp[:, b, :], c_rs[:, b, :], gelu[:, :], ALU.mult,
                                       ALU.mult).then_inc(mixw_done, 1)

            def late_split(n):
                dve.wait_ge(high_done, n + 1)
                v.tensor_tensor(w_lo[n % RING][:, :], raw[n % RING][:, :], w_hi[n % RING][:, :].bitcast(F32),
                                ALU.subtract).then_inc(late_split_done, 1)

            choose(0, 0)
            late_split(NGRAN - 4)
            choose(1, 1)
            late_split(NGRAN - 3)
            dot_products(0, 0, range(0, 2))
            late_split(NGRAN - 2)
            dot_products(0, 0, range(2, 4))
            late_split(NGRAN - 1)
            dot_products(0, 0, range(4, BATCHES))
            weights(0, 0)
            dot_products(1, 0, range(0, 4))
            choose(2, 2)
            dot_products(1, 0, range(4, BATCHES))
            weights(1, 1)
            for t, (first, end) in enumerate(((2, NH), (NH, TT * NH - 2))):
                dve.reg_mov(loop_step, steps[0] + 1)
                in_loop[0], before = True, steps[0]
                with dve.Fori(0, (end - first) // 3, 1) as q:
                    for i in range(3):
                        group(q * 3 + (first + i), (first + i) % 3, t)
                in_loop[0] = False
                steps[0] = before + (steps[0] - before) * (end - first) // 3
            for g in (TT * NH - 2, TT * NH - 1):
                group(g, g % 3, 1, more=g < TT * NH - 1)
            dve.wait_ge(mixw_done, TT * NH)
            acc = hn[:, 0, :]
            for m in SHARE:
                rows, arrived, value = last_place(m)
                dve.wait_ge(arrived, value)
                for i in range(2):
                    w, row_of_v = mixw[:, 2 * m + i:2 * m + i + 1], rows[i][:, :]
                    if m == SHARE[0] and i == 0:
                        ins = v.tensor_scalar(acc, row_of_v, w, None, ALU.mult)
                    else:
                        ins = v.scalar_tensor_tensor(acc, row_of_v, w, acc, ALU.mult, ALU.add)
                    if m == SHARE[-1] and i:
                        ins.then_inc(share_done, 1)
                    else:
                        settle(ins)

            dve.wait_ge(final_done, 16)
            for t in range(TT):
                n = TT * 5 + t
                dve.wait_ge(sumsq_done, TT * 5 + 2 * (t + 1))
                settle(v.tensor_tensor(column(sumsq, n), final_ss[:, t, 0:1], final_ss[:, t, 1:2], ALU.add))
                v.tensor_scalar(column(var, n), column(sumsq, n), 1.0 / D, EPS, ALU.mult, ALU.add).then_inc(var_done, 1)
                dve.wait_ge(root_done, n + 1)
                settle(v.reciprocal(column(rstd, n), column(root, n)))
                for half in range(2):
                    cols = slice(half * 512, (half + 1) * 512)
                    v.scalar_tensor_tensor(X[:, t, cols], ps.bank(("mix", t, half))[:, :], column(rstd, n), final_gain[:, cols],
                                           ALU.mult, ALU.mult).then_inc(fout_done, 1)

        @block.gpsimd
        def _(pool):
            def low_part(n, r):
                pool.wait_ge(high_done, n + 1)
                nc.gpsimd.tensor_tensor(w_lo[r][:, :], raw[r][:, :], w_hi[r][:, :].bitcast(F32), ALU.subtract).then_inc(split_done, 1)

            def low_parts(begin, end):
                rounds = (end - begin) // RING
                with pool.Fori(0, rounds, 1) as q:
                    for i in range(RING):
                        low_part(q * RING + (begin + i), (begin + i) % RING)
                for n in range(begin + rounds * RING, end):
                    low_part(n, n % RING)

            before = GRANULES.index("wp2") + 1
            low_parts(0, before)

            ps.copied(pool, ("conv", 2))
            done = 0
            for tap in range(TAPS - POOL_TAPS, TAPS):
                first = tap == TAPS - POOL_TAPS
                if not first:
                    pool.wait_ge(pool_step, done)
                nc.gpsimd.tensor_scalar(conv_p[:, :] if first else conv_m[:, :], conv_in[:, 2, tap:tap + T], tap_weight(tap, 2),
                                        None, ALU.mult).then_inc(pool_step, 1)
                done += 1
                if not first:
                    pool.wait_ge(pool_step, done)
                    nc.gpsimd.tensor_tensor(conv_p[:, :], conv_p[:, :], conv_m[:, :], ALU.add).then_inc(pool_step, 1)
                    done += 1
            low_parts(before, NGRAN - LATE)

            u_count = pool.alloc_register("u_count")
            v_count = pool.alloc_register("v_count")
            def fetch(table_in, rows, free, count, arrived, slot, b, m):
                pool.wait_ge(free, count)
                if not isinstance(count, int):
                    pool.reg_add(count, count, 1)
                for i in range(2):
                    nc.gpsimd.indirect_dma_start(
                        rows[2 * slot + i][:, :], None, table_in,
                        bass.IndirectOffsetOnAxis(ap=expert[:, b, 2 * m + i:2 * m + i + 1], axis=0)).then_inc(arrived[slot], 16)

            def fetch_u(b, m, count=u_count):
                slot = m % (UROWS // 2)
                fetch(peer_u, u_rows, u_free, count, u_in, slot, b, m)

            def fetch_v(b, m, count=v_count):
                slot = m % (VROWS // 2)
                fetch(peer_v, v_rows, v_free, count, v_in, slot, b, m)

            pool.wait_ge(experts_ready, 1)
            for m in range(BATCHES):
                fetch_u(0, m, m + 1)
                if m % 4 == 3:
                    fetch_v(0, m // 4, m // 4 + 1)
            pool.wait_ge(experts_ready, 2)
            for m in range(BATCHES):
                fetch_u(1, m, BATCHES + m + 1)
                if m >= 2:
                    fetch_v(0, m, m + 1)
            group_count = pool.alloc_register("group_count")
            pool.reg_mov(group_count, 3)
            pool.reg_mov(u_count, 2 * BATCHES + 1)
            pool.reg_mov(v_count, BATCHES + 1)
            with pool.Fori(0, (TT * NH - 4) // 3, 1):
                for i in range(3):
                    pool.wait_ge(experts_ready, group_count)
                    pool.reg_add(group_count, group_count, 1)
                    for m in range(BATCHES):
                        fetch_u((2 + i) % 3, m)
                        fetch_v((1 + i) % 3, m)
            for g in (TT * NH - 2, TT * NH - 1):
                pool.wait_ge(experts_ready, g + 1)
                for m in range(BATCHES):
                    fetch_u(g % 3, m, g * BATCHES + m + 1)
                    fetch_v((g - 1) % 3, m, (g - 1) * BATCHES + m + 1)
            g, in_u = TT * NH - 1, UROWS // 2
            for m in range(BATCHES):
                if m < 2:
                    fetch_v(g % 3, m, g * BATCHES + m + 1)
                elif m < 2 + in_u:
                    fetch(peer_v, u_rows, u_free, (g + 1) * BATCHES + m - 1, u_in, m - 2, g % 3, m)
                else:
                    fetch(peer_v, v_rows, v_free, g * BATCHES + m - in_u + 1, v_in, m % 2, g % 3, m)


def _blocks(w, n):
    k = w.shape[0] // P
    return [w[:, i:i + n].reshape(k, P, n).transpose(1, 0, 2).reshape(P, k * n) for i in range(0, w.shape[1], n)]


def kernel(**inputs):
    import concourse.bacc as _bacc
    from concourse.bass_utils import run_bass_kernel_spmd as _run

    a = {k: np.asarray(x) for k, x in inputs.items()}
    w_in, w_in2 = a["w_in"][0], a["w_in_2"]
    ofs = np.cumsum([0, 512, 512, 512, 512, HD, HD, 512, HD, NH, D, D])
    qa, ka, va, qb, kb, vb, qi, ki, wi, ga, gb = [w_in[:, ofs[i]:ofs[i + 1]] for i in range(11)]
    chunked = lambda w: w.reshape(-1, P, w.shape[1]).transpose(1, 0, 2)
    granules = {}
    for name, w in (("qi", qi), ("qb", qb), ("qa", qa), ("ka", ka), ("va", va), ("wo", a["w_out"][0]), ("wp", a["w_out_2"]),
                    ("wq", a["peer_wq_2"]), ("gate", np.concatenate([ga, gb], 1)), ("ffg", a["w_gate"][0]),
                    ("ffu", a["w_up"][0]), ("q2", w_in2[:, 0:512])):
        for i, blk in enumerate(_blocks(w, T)):
            granules[f"{name}{i}"] = blk
    granules["kv"] = _blocks(w_in2[:, 512:768], T)[0]
    small = _blocks(np.concatenate([kb, vb, ki, wi], 1), SMALL)[0]
    granules["small"] = np.concatenate([small, np.zeros((P, GRAIN - small.shape[1]), np.float32)], 1)
    up = np.concatenate([a["w_up_a"][0], a["w_up_b"][0]], 0)
    for u, blk in enumerate(_blocks(up, T)):
        granules[f"up{u}"] = blk
    down = chunked(a["w_down"][0])
    for j in range(KF // 2):
        granules[f"dn{j}"] = down[:, 2 * j:2 * j + 2].reshape(P, GRAIN)
    for c in range(CC):
        both = [w_in2[:, at + c * P:at + (c + 1) * P] for at in (768, 1280)]
        granules[f"conv{c}"] = _blocks(np.concatenate(both, 1), T)[0]
    stream = np.stack([granules[n] for n in GRANULES])
    cols = lambda x: x.reshape(-1, P).T
    params = np.concatenate(
        [cols(a["norm_mix"]), cols(a["norm_ffn"]), cols(a["norm1_g_2"]), cols(a["norm2_g_2"]),
         np.broadcast_to(a["q_norm_g_2"], (P, HD)), np.broadcast_to(a["k_norm_g_2"], (P, HD)),
         a["conv_dw_2"][:, 0, :].T.reshape(CC, P, TAPS).transpose(1, 0, 2).reshape(P, CC * TAPS),
         cols(a["conv_b_2"]), cols(a["conv_ln_g_2"]), cols(a["conv_ln_b_2"]),
         a["peer_keys_2"].transpose(2, 0, 1).reshape(P, 2 * NKEY)], 1)
    arrays = {"x_in": a["x"].reshape(T, D), "stream": stream, "consts_in": constants(), "params_in": params,
              "norm_final": np.broadcast_to(a["norm_final"], (P, D)),
              "norm2_g": np.broadcast_to(a["norm2_g_2"], (P, D)), "final_g": np.broadcast_to(a["final_g_2"], (P, D)),
              "peer_u": a["peer_u_2"], "peer_v": a["peer_v_2"]}
    nc = _bacc.Bacc("TRN2", target_bir_lowering=False, num_devices=1)
    args, sent = [], {}
    for name, x in arrays.items():
        sent[f"{name}_dram"] = np.ascontiguousarray(x)
        args.append(nc.dram_tensor(f"{name}_dram", x.shape, mybir.dt.from_np(x.dtype), kind="ExternalInput").ap())
    args.append(nc.dram_tensor("out_dram", (T, D), F32, kind="ExternalOutput").ap())
    bass_two_blocks_kernel(nc, *args)
    r = _run(nc, [sent], core_ids=[0])
    return r.results[0]["out_dram"].reshape(1, T, D)
```
